# Optimizing a Trainium2 kernel written in Bass

```python
import math
import jax, jax.numpy as jnp
from jax import lax
import numpy as np

D_MODEL = 1024
BATCH = 1
SEQ = 256
DEPTH = 2

HEAD_DIM = 64
DSA_HEADS = 4
DSA_TOPK = 256
IDX_HEADS = 8
IDX_DIM = 32
FOX_HEADS = 6
NSA_HEADS = 6
NSA_KV_GROUPS = 2
NSA_HPG = NSA_HEADS // NSA_KV_GROUPS
NSA_CMP_LEN = 32
NSA_CMP_STRIDE = 16
NSA_SEL_BLOCK = 64
NSA_SEL_N = 16
NSA_WINDOW = 512
NSA_Q_BLOCK = 64

Q_BLOCK = 128
ROPE_THETA = 10000.0
LN_EPS = 1e-5
ALPHA = (2.0 * DEPTH) ** 0.25
BETA = (8.0 * DEPTH) ** -0.25

DSA_W = DSA_HEADS * HEAD_DIM
FOX_W = FOX_HEADS * HEAD_DIM
NSA_W = NSA_HEADS * HEAD_DIM
NSA_KV_W = NSA_KV_GROUPS * HEAD_DIM
MIX_W = DSA_W + FOX_W + NSA_W

IN_SPLITS = (
    ("dsa_q", DSA_W), ("dsa_k", HEAD_DIM), ("dsa_v", HEAD_DIM),
    ("idx_q", IDX_HEADS * IDX_DIM), ("idx_k", IDX_DIM), ("idx_w", IDX_HEADS),
    ("fox_q", FOX_W), ("fox_k", FOX_W), ("fox_v", FOX_W), ("fox_f", FOX_HEADS),
    ("nsa_q", NSA_W),
    ("nsa_kc", NSA_KV_W), ("nsa_vc", NSA_KV_W),
    ("nsa_ks", NSA_KV_W), ("nsa_vs", NSA_KV_W),
    ("nsa_kw", NSA_KV_W), ("nsa_vw", NSA_KV_W),
    ("nsa_g", 3 * NSA_HEADS),
    ("gate", MIX_W),
)
IN_WIDTH = sum(w for _, w in IN_SPLITS)


def split_cols(h):
    out, off = {}, 0
    for name, w in IN_SPLITS:
        out[name] = h[..., off:off + w]
        off += w
    return out

def layer_norm(x, g, b):
    xf = x.astype(jnp.float32)
    mu = jnp.mean(xf, -1, keepdims=True)
    var = jnp.mean(jnp.square(xf - mu), -1, keepdims=True)
    return ((xf - mu) * lax.rsqrt(var + LN_EPS) * g + b).astype(x.dtype)

def rope(x, pos):
    half = x.shape[-1] // 2
    inv = ROPE_THETA ** (-jnp.arange(half, dtype=jnp.float32) / half)
    ang = pos.astype(jnp.float32)[:, None] * inv[None, :]
    cos = jnp.cos(ang)[:, None, :]
    sin = jnp.sin(ang)[:, None, :]
    x1, x2 = x[..., :half], x[..., half:]
    return jnp.concatenate([x1 * cos - x2 * sin, x1 * sin + x2 * cos], -1).astype(x.dtype)

def masked_softmax(s, mask):
    s = jnp.where(mask, s.astype(jnp.float32), -jnp.inf)
    m = jnp.max(s, -1, keepdims=True)
    m = jnp.where(jnp.isfinite(m), m, 0.0)
    e = jnp.where(mask, jnp.exp(s - m), 0.0)
    return e / jnp.maximum(jnp.sum(e, -1, keepdims=True), 1e-30)

def stack_blocks(out):
    nb, B, T, H, D = out.shape
    return out.transpose(1, 0, 2, 3, 4).reshape(B, nb * T, H, D)

def dsa_mixer(q, k, v, iq, ik, iw):
    B, S, H, D = q.shape
    topk = min(DSA_TOPK, S // 4)
    kpos = jnp.arange(S)
    scale = D ** -0.5
    gather = jax.vmap(lambda kb, ib: kb[ib])

    def block(i):
        t0 = i * Q_BLOCK
        tpos = t0 + jnp.arange(Q_BLOCK)
        qb = lax.dynamic_slice_in_dim(q, t0, Q_BLOCK, 1)
        iqb = lax.dynamic_slice_in_dim(iq, t0, Q_BLOCK, 1)
        iwb = lax.dynamic_slice_in_dim(iw, t0, Q_BLOCK, 1).astype(jnp.float32)
        isc = jnp.einsum("bthd,bsd->bths", iqb, ik).astype(jnp.float32)
        isc = jnp.einsum("bth,bths->bts", iwb, jax.nn.relu(isc))
        causal = kpos[None, :] <= tpos[:, None]
        isc = jnp.where(causal[None], isc, -jnp.inf)
        _, idx = lax.top_k(isc, topk)
        kg = gather(k, idx)
        vg = gather(v, idx)
        valid = idx <= tpos[None, :, None]
        s = jnp.einsum("bthd,btkd->bthk", qb, kg) * scale
        p = masked_softmax(s, valid[:, :, None, :])
        return jnp.einsum("bthk,btkd->bthd", p.astype(v.dtype), vg)

    return stack_blocks(lax.map(block, jnp.arange(S // Q_BLOCK)))

def fox_mixer(q, k, v, logf):
    B, S, H, D = q.shape
    cum = jnp.cumsum(logf.astype(jnp.float32), axis=1).transpose(0, 2, 1)
    kpos = jnp.arange(S)
    scale = D ** -0.5

    def block(i):
        t0 = i * Q_BLOCK
        tpos = t0 + jnp.arange(Q_BLOCK)
        qb = lax.dynamic_slice_in_dim(q, t0, Q_BLOCK, 1)
        cb = lax.dynamic_slice_in_dim(cum, t0, Q_BLOCK, 2)
        s = jnp.einsum("bthd,bshd->bhts", qb, k).astype(jnp.float32) * scale
        s = s + cb[:, :, :, None] - cum[:, :, None, :]
        causal = kpos[None, :] <= tpos[:, None]
        p = masked_softmax(s, causal)
        return jnp.einsum("bhts,bshd->bthd", p.astype(v.dtype), v)

    return stack_blocks(lax.map(block, jnp.arange(S // Q_BLOCK)))

def nsa_compress(kv, pe, w1, w2):
    B, S, G, D = kv.shape
    n_c = (S - NSA_CMP_LEN) // NSA_CMP_STRIDE + 1
    idx = jnp.arange(n_c)[:, None] * NSA_CMP_STRIDE + jnp.arange(NSA_CMP_LEN)[None, :]
    blocks = kv[:, idx] + pe[None, None, :, None, :]
    blocks = blocks.transpose(0, 1, 3, 2, 4).reshape(B, n_c, G, NSA_CMP_LEN * D)
    return jax.nn.silu(blocks @ w1) @ w2

def nsa_mixer(q, q_rot, kc, vc, ks, vs, kw, vw, gates):
    B, S, G, J, D = q.shape
    n_c = kc.shape[1]
    nsb = S // NSA_SEL_BLOCK
    n_sel = min(NSA_SEL_N, nsb)
    scale = D ** -0.5
    cstart = jnp.arange(n_c) * NSA_CMP_STRIDE
    cend = cstart + NSA_CMP_LEN - 1
    bstart = jnp.arange(nsb) * NSA_SEL_BLOCK
    overlap = ((cstart[:, None] < bstart[None, :] + NSA_SEL_BLOCK)
               & (cstart[:, None] + NSA_CMP_LEN > bstart[None, :])).astype(jnp.float32)
    ks_t = ks.transpose(0, 2, 1, 3)
    vs_t = vs.transpose(0, 2, 1, 3)
    pad = ((0, 0), (NSA_WINDOW, 0), (0, 0), (0, 0))
    kw_pad = jnp.pad(kw, pad)
    vw_pad = jnp.pad(vw, pad)
    gather = jax.vmap(jax.vmap(lambda kk, ii: kk[ii]))
    jb = jnp.arange(nsb)
    tok_off = jnp.arange(NSA_SEL_BLOCK)

    def block(i):
        T = NSA_Q_BLOCK
        t0 = i * T
        tpos = t0 + jnp.arange(T)
        qb = lax.dynamic_slice_in_dim(q, t0, T, 1)
        qrb = lax.dynamic_slice_in_dim(q_rot, t0, T, 1)
        gb = lax.dynamic_slice_in_dim(gates, t0, T, 1)
        s = jnp.einsum("btgjd,bcgd->bgjtc", qb, kc) * scale
        p_cmp = masked_softmax(s, cend[None, :] <= tpos[:, None])
        o_cmp = jnp.einsum("bgjtc,bcgd->btgjd", p_cmp.astype(vc.dtype), vc)
        score = jnp.einsum("bgjtc,cn->bgtn", p_cmp, overlap)
        cur = tpos // NSA_SEL_BLOCK
        forced = (jb[None, :] == 0) | (jb[None, :] == cur[:, None]) | (jb[None, :] == cur[:, None] - 1)
        future = bstart[None, :] > tpos[:, None]
        score = jnp.where(forced, jnp.inf, jnp.where(future, -jnp.inf, score))
        _, blk = lax.top_k(score, n_sel)
        tok = (blk[..., None] * NSA_SEL_BLOCK + tok_off).reshape(B, G, T, n_sel * NSA_SEL_BLOCK)
        kg = gather(ks_t, tok)
        vg = gather(vs_t, tok)
        s = jnp.einsum("btgjd,bgtnd->bgjtn", qrb, kg) * scale
        p = masked_softmax(s, (tok <= tpos[None, None, :, None])[:, :, None])
        o_slc = jnp.einsum("bgjtn,bgtnd->btgjd", p.astype(vs.dtype), vg)
        kwb = lax.dynamic_slice_in_dim(kw_pad, t0, NSA_WINDOW + T, 1)
        vwb = lax.dynamic_slice_in_dim(vw_pad, t0, NSA_WINDOW + T, 1)
        kpos = t0 - NSA_WINDOW + jnp.arange(NSA_WINDOW + T)
        wmask = ((kpos[None, :] <= tpos[:, None]) & (kpos[None, :] > tpos[:, None] - NSA_WINDOW)
                 & (kpos[None, :] >= 0))
        s = jnp.einsum("btgjd,bkgd->bgjtk", qrb, kwb) * scale
        p = masked_softmax(s, wmask)
        o_win = jnp.einsum("bgjtk,bkgd->btgjd", p.astype(vw.dtype), vwb)
        o = (gb[:, :, 0, :, :, None] * o_cmp + gb[:, :, 1, :, :, None] * o_slc
             + gb[:, :, 2, :, :, None] * o_win)
        return o.reshape(B, T, G * J, D)

    return stack_blocks(lax.map(block, jnp.arange(S // NSA_Q_BLOCK)))

def hybrid_layer(x, c, w_ada, b_ada, w_in, b_f, cmp_pe, cmp_w1, cmp_w2, w_out, ln_g, ln_b):
    B, S, _ = x.shape
    pos = jnp.arange(S)
    shift, scale, gate = jnp.split(c @ w_ada + b_ada, 3, axis=-1)
    u = x * (1.0 + scale[:, None, :]) + shift[:, None, :]
    h = split_cols(u @ w_in)

    dq = rope(h["dsa_q"].reshape(B, S, DSA_HEADS, HEAD_DIM), pos)
    dk = rope(h["dsa_k"][:, :, None, :], pos)[:, :, 0]
    iq = rope(h["idx_q"].reshape(B, S, IDX_HEADS, IDX_DIM), pos)
    ik = rope(h["idx_k"][:, :, None, :], pos)[:, :, 0]
    iw = h["idx_w"] * (IDX_HEADS ** -0.5)
    o_dsa = dsa_mixer(dq, dk, h["dsa_v"], iq, ik, iw)

    fq = h["fox_q"].reshape(B, S, FOX_HEADS, HEAD_DIM)
    fk = h["fox_k"].reshape(B, S, FOX_HEADS, HEAD_DIM)
    fv = h["fox_v"].reshape(B, S, FOX_HEADS, HEAD_DIM)
    logf = jax.nn.log_sigmoid(h["fox_f"].astype(jnp.float32) + b_f)
    o_fox = fox_mixer(fq, fk, fv, logf)

    kvs = lambda name: h[name].reshape(B, S, NSA_KV_GROUPS, HEAD_DIM)
    nq = h["nsa_q"].reshape(B, S, NSA_HEADS, HEAD_DIM)
    nq_rot = rope(nq, pos)
    kc = nsa_compress(kvs("nsa_kc"), cmp_pe[0], cmp_w1[0], cmp_w2[0])
    vc = nsa_compress(kvs("nsa_vc"), cmp_pe[1], cmp_w1[1], cmp_w2[1])
    ks = rope(kvs("nsa_ks"), pos)
    kw = rope(kvs("nsa_kw"), pos)
    gates = jax.nn.sigmoid(h["nsa_g"].reshape(B, S, 3, NSA_KV_GROUPS, NSA_HPG))
    grp = lambda t: t.reshape(B, S, NSA_KV_GROUPS, NSA_HPG, HEAD_DIM)
    o_nsa = nsa_mixer(grp(nq), grp(nq_rot), kc, vc, ks, kvs("nsa_vs"), kw, kvs("nsa_vw"), gates)

    mix = jnp.concatenate([o_dsa.reshape(B, S, DSA_W), o_fox.reshape(B, S, FOX_W),
                           o_nsa.reshape(B, S, NSA_W)], axis=-1)
    y = (mix * jax.nn.silu(h["gate"])) @ w_out
    return layer_norm(ALPHA * x + (1.0 + gate[:, None, :]) * y, ln_g, ln_b)

def first_inputs(seed: int = 0) -> dict:
    key = jax.random.key(seed)
    ks = jax.random.split(key, 12)
    D = D_MODEL
    L = NSA_CMP_LEN
    nrm = lambda k, shape, s: jax.random.normal(k, shape, jnp.float32) * s
    return {
        "x": nrm(ks[0], (BATCH, SEQ, D), 1.0),
        "c": nrm(ks[1], (BATCH, D), 1.0),
        "w_ada": nrm(ks[2], (DEPTH, D, 3 * D), 0.1 * D ** -0.5),
        "b_ada": nrm(ks[3], (DEPTH, 3 * D), 0.01),
        "w_in": nrm(ks[4], (DEPTH, D, IN_WIDTH), D ** -0.5),
        "b_f": jax.random.uniform(ks[5], (DEPTH, FOX_HEADS), jnp.float32, 1.0, 4.0),
        "cmp_pe": nrm(ks[6], (DEPTH, 2, L, HEAD_DIM), 0.1),
        "cmp_w1": nrm(ks[7], (DEPTH, 2, L * HEAD_DIM, HEAD_DIM), (L * HEAD_DIM) ** -0.5),
        "cmp_w2": nrm(ks[8], (DEPTH, 2, HEAD_DIM, HEAD_DIM), HEAD_DIM ** -0.5),
        "w_out": nrm(ks[9], (DEPTH, MIX_W, D), BETA * MIX_W ** -0.5),
        "ln_g": 1.0 + nrm(ks[10], (DEPTH, D), 0.01),
        "ln_b": nrm(ks[11], (DEPTH, D), 0.01),
    }

def first_block(x, c, w_ada, b_ada, w_in, b_f, cmp_pe, cmp_w1, cmp_w2, w_out, ln_g, ln_b):
    for l in range(DEPTH):
        x = hybrid_layer(x, c, w_ada[l], b_ada[l], w_in[l], b_f[l], cmp_pe[l], cmp_w1[l],
                         cmp_w2[l], w_out[l], ln_g[l], ln_b[l])
    return x


MIX_WIDTH = D_MODEL
CONV_WIDTH = MIX_WIDTH // 2
CONV_GROUPS = 4
CONV_WIN = 31
DN_WIDTH = MIX_WIDTH - CONV_WIDTH
DN_HEADS = 4
DN_HEAD_DIM = DN_WIDTH // DN_HEADS
SHORT_CONV = 4
CHUNK = 64
D_FF_DENSE = 2816
N_EXPERTS = 8
TOP_K = 2
D_FF_EXPERT = 3584
N_DENSE = (DEPTH + 1) // 2
N_MOE = DEPTH // 2
DEEPNORM_ALPHA = (2 * DEPTH) ** 0.25
DEEPNORM_BETA = (8 * DEPTH) ** -0.25
RMS_EPS = 1e-6
L2_EPS = 1e-6
IN_SIZES = (CONV_WIDTH, CONV_WIDTH, DN_WIDTH, DN_WIDTH, DN_WIDTH, DN_WIDTH, DN_HEADS, DN_HEADS)
IN_COLS = sum(IN_SIZES)
IN_SPLITS_2 = tuple(int(s) for s in np.cumsum(IN_SIZES)[:-1])


def layer_norm_2(x, g, b):
    xf = x.astype(jnp.float32)
    mu = xf.mean(-1, keepdims=True)
    var = jnp.square(xf - mu).mean(-1, keepdims=True)
    return ((xf - mu) * lax.rsqrt(var + LN_EPS) * g + b).astype(x.dtype)

def causal_depthwise_conv(x, w):
    width = w.shape[0]
    return lax.conv_general_dilated(
        x, w[:, None, :].astype(x.dtype), (1,), ((width - 1, 0),),
        dimension_numbers=("NWC", "WIO", "NWC"), feature_group_count=x.shape[-1])

def conformer_conv(h_val, h_gate, dw_w, dw_b, ln_g, ln_b):
    h = h_val * jax.nn.sigmoid(h_gate)
    h = causal_depthwise_conv(h, dw_w) + dw_b
    h = layer_norm_2(h, ln_g, ln_b)
    return jax.nn.silu(h)

def l2norm(t):
    return t * lax.rsqrt(jnp.sum(t * t, -1, keepdims=True) + L2_EPS)

def chunk_gated_delta_rule(q, k, v, g, beta):
    B, S, H, Dk = q.shape
    Dv = v.shape[-1]
    N = S // CHUNK
    q = q * (Dk ** -0.5)
    to_chunks = lambda t: t.reshape(B, N, CHUNK, H, t.shape[-1]).transpose(0, 3, 1, 2, 4)
    q, k, v = to_chunks(q), to_chunks(k), to_chunks(v)
    g = g.reshape(B, N, CHUNK, H).transpose(0, 3, 1, 2)
    beta = beta.reshape(B, N, CHUNK, H).transpose(0, 3, 1, 2)
    g = jnp.cumsum(g, axis=-1)
    kb = k * beta[..., None]
    vb = v * beta[..., None]
    causal = jnp.tril(jnp.ones((CHUNK, CHUNK), bool))
    strict = jnp.tril(jnp.ones((CHUNK, CHUNK), bool), -1)
    decay = jnp.exp(jnp.where(causal, g[..., :, None] - g[..., None, :], -jnp.inf))
    lower = jnp.where(strict, jnp.einsum('bhncd,bhnjd->bhncj', kb, k) * decay, 0.0)
    eye = jnp.eye(CHUNK, dtype=jnp.float32)
    rhs = jnp.concatenate([vb, kb * jnp.exp(g)[..., None]], axis=-1)
    sol = lax.linalg.triangular_solve(eye + lower, rhs, left_side=True, lower=True, unit_diagonal=True)
    u, w = sol[..., :Dv], sol[..., Dv:]
    attn = jnp.einsum('bhncd,bhnjd->bhncj', q, k) * decay

    def step(state, inp):
        qc, kc, uc, wc, gc, ac = inp
        v_new = uc - jnp.einsum('bhcd,bhde->bhce', wc, state)
        o = jnp.einsum('bhcd,bhde->bhce', qc * jnp.exp(gc)[..., None], state) \
            + jnp.einsum('bhcj,bhje->bhce', ac, v_new)
        g_last = gc[..., -1]
        k_dec = kc * jnp.exp(g_last[..., None] - gc)[..., None]
        state = state * jnp.exp(g_last)[..., None, None] + jnp.einsum('bhcd,bhce->bhde', k_dec, v_new)
        return state, o

    lead = lambda t: jnp.moveaxis(t, 2, 0)
    s0 = jnp.zeros((B, H, Dk, Dv), jnp.float32)
    _, o = lax.scan(step, s0, (lead(q), lead(k), lead(u), lead(w), lead(g), lead(attn)))
    o = jnp.moveaxis(o, 0, 2)
    return o.transpose(0, 2, 3, 1, 4).reshape(B, S, H, Dv)

def gated_deltanet(q, k, v, z, b_logit, a_logit, sc_w, a_log, dt_bias, on_g):
    B, S, _ = q.shape
    qkv = jax.nn.silu(causal_depthwise_conv(jnp.concatenate([q, k, v], -1), sc_w))
    q, k, v = jnp.split(qkv, 3, axis=-1)
    heads = lambda t: t.reshape(B, S, DN_HEADS, DN_HEAD_DIM).astype(jnp.float32)
    q, k, v = l2norm(heads(q)), l2norm(heads(k)), heads(v)
    beta = jax.nn.sigmoid(b_logit.astype(jnp.float32))
    g = -jnp.exp(a_log.astype(jnp.float32)) * jax.nn.softplus(
        a_logit.astype(jnp.float32) + dt_bias.astype(jnp.float32))
    o = chunk_gated_delta_rule(q, k, v, g, beta)
    o = o * lax.rsqrt(jnp.mean(o * o, -1, keepdims=True) + RMS_EPS) * on_g.astype(jnp.float32)
    o = o * jax.nn.silu(heads(z))
    return o.reshape(B, S, DN_WIDTH).astype(z.dtype)

def hybrid_mixer(x, w_in, dw_w, dw_b, cln_g, cln_b, sc_w, a_log, dt_bias, on_g, w_out):
    h = x @ w_in
    c_val, c_gate, q, k, v, z, b_logit, a_logit = jnp.split(h, IN_SPLITS_2, axis=-1)
    y_conv = conformer_conv(c_val, c_gate, dw_w, dw_b, cln_g, cln_b)
    y_dn = gated_deltanet(q, k, v, z, b_logit, a_logit, sc_w, a_log, dt_bias, on_g)
    return jnp.concatenate([y_conv, y_dn], axis=-1) @ w_out

def swiglu(x, w_gate, w_up, w_down):
    return (jax.nn.silu(x @ w_gate) * (x @ w_up)) @ w_down

def moe_swiglu(x, router_w, w_gate, w_up, w_down):
    logits = (x @ router_w).astype(jnp.float32)
    top_v, top_i = lax.top_k(logits, TOP_K)
    gates = jax.nn.softmax(top_v, axis=-1)
    combine = jnp.sum(jax.nn.one_hot(top_i, N_EXPERTS, dtype=jnp.float32) * gates[..., None], axis=-2)
    y = jnp.zeros_like(x)
    for e in range(N_EXPERTS):
        y = y + combine[..., e:e + 1].astype(x.dtype) * swiglu(x, w_gate[e], w_up[e], w_down[e])
    return y

def second_inputs(seed: int = 0) -> dict:
    key = jax.random.key(seed)
    ks = jax.random.split(key, 24)
    f32 = jnp.float32
    nrm = lambda k, shape, scale: jax.random.normal(k, shape, f32) * scale
    dt = jnp.exp(jax.random.uniform(ks[8], (DEPTH, DN_HEADS), f32, np.log(1e-3), np.log(1e-1)))
    return {
        "x": nrm(ks[0], (BATCH, SEQ, D_MODEL), 1.0),
        "w_in": nrm(ks[1], (DEPTH, D_MODEL, IN_COLS), D_MODEL ** -0.5),
        "conv_dw_w": nrm(ks[2], (DEPTH, CONV_WIN, CONV_WIDTH), CONV_WIN ** -0.5),
        "conv_dw_b": nrm(ks[3], (DEPTH, CONV_WIDTH), 0.02),
        "conv_ln_g": 1.0 + nrm(ks[4], (DEPTH, CONV_WIDTH), 0.02),
        "conv_ln_b": nrm(ks[5], (DEPTH, CONV_WIDTH), 0.02),
        "short_conv_w": nrm(ks[6], (DEPTH, SHORT_CONV, 3 * DN_WIDTH), SHORT_CONV ** -0.5),
        "a_log": jnp.log(jax.random.uniform(ks[7], (DEPTH, DN_HEADS), f32, 1.0, 16.0)),
        "dt_bias": dt + jnp.log(-jnp.expm1(-dt)),
        "out_norm_g": 1.0 + nrm(ks[9], (DEPTH, DN_HEAD_DIM), 0.02),
        "w_out": nrm(ks[10], (DEPTH, MIX_WIDTH, D_MODEL), MIX_WIDTH ** -0.5 * DEEPNORM_BETA),
        "ln_mix_g": 1.0 + nrm(ks[11], (DEPTH, D_MODEL), 0.02),
        "ln_mix_b": nrm(ks[12], (DEPTH, D_MODEL), 0.02),
        "ffn_w_gate": nrm(ks[13], (N_DENSE, D_MODEL, D_FF_DENSE), D_MODEL ** -0.5),
        "ffn_w_up": nrm(ks[14], (N_DENSE, D_MODEL, D_FF_DENSE), D_MODEL ** -0.5),
        "ffn_w_down": nrm(ks[15], (N_DENSE, D_FF_DENSE, D_MODEL), D_FF_DENSE ** -0.5 * DEEPNORM_BETA),
        "router_w": nrm(ks[16], (N_MOE, D_MODEL, N_EXPERTS), D_MODEL ** -0.5),
        "moe_w_gate": nrm(ks[17], (N_MOE, N_EXPERTS, D_MODEL, D_FF_EXPERT), D_MODEL ** -0.5),
        "moe_w_up": nrm(ks[18], (N_MOE, N_EXPERTS, D_MODEL, D_FF_EXPERT), D_MODEL ** -0.5),
        "moe_w_down": nrm(ks[19], (N_MOE, N_EXPERTS, D_FF_EXPERT, D_MODEL), D_FF_EXPERT ** -0.5 * DEEPNORM_BETA),
        "ln_ffn_g": 1.0 + nrm(ks[20], (DEPTH, D_MODEL), 0.02),
        "ln_ffn_b": nrm(ks[21], (DEPTH, D_MODEL), 0.02),
    }

def second_block(x, w_in, conv_dw_w, conv_dw_b, conv_ln_g, conv_ln_b, short_conv_w, a_log, dt_bias,
              out_norm_g, w_out, ln_mix_g, ln_mix_b, ffn_w_gate, ffn_w_up, ffn_w_down, router_w,
              moe_w_gate, moe_w_up, moe_w_down, ln_ffn_g, ln_ffn_b):
    for layer in range(DEPTH):
        m = hybrid_mixer(x, w_in[layer], conv_dw_w[layer], conv_dw_b[layer], conv_ln_g[layer],
                         conv_ln_b[layer], short_conv_w[layer], a_log[layer], dt_bias[layer],
                         out_norm_g[layer], w_out[layer])
        x = layer_norm_2(DEEPNORM_ALPHA * x + m, ln_mix_g[layer], ln_mix_b[layer])
        j = layer // 2
        if layer % 2 == 0:
            f = swiglu(x, ffn_w_gate[j], ffn_w_up[j], ffn_w_down[j])
        else:
            f = moe_swiglu(x, router_w[j], moe_w_gate[j], moe_w_up[j], moe_w_down[j])
        x = layer_norm_2(DEEPNORM_ALPHA * x + f, ln_ffn_g[layer], ln_ffn_b[layer])
    return x


def setup_inputs(seed=0):
    out = dict(first_inputs(seed))
    for name, value in second_inputs(seed + 1).items():
        if name != "x":
            out[name + "_2"] = value
    return out


def reference(
    x, c, w_ada, b_ada, w_in, b_f, cmp_pe, cmp_w1, cmp_w2, w_out, ln_g, ln_b, w_in_2,
    conv_dw_w_2, conv_dw_b_2, conv_ln_g_2, conv_ln_b_2, short_conv_w_2, a_log_2, dt_bias_2,
    out_norm_g_2, w_out_2, ln_mix_g_2, ln_mix_b_2, ffn_w_gate_2, ffn_w_up_2, ffn_w_down_2,
    router_w_2, moe_w_gate_2, moe_w_up_2, moe_w_down_2, ln_ffn_g_2, ln_ffn_b_2,
):
    x = first_block(
        x, c, w_ada, b_ada, w_in, b_f, cmp_pe, cmp_w1, cmp_w2, w_out, ln_g, ln_b,
    )
    return second_block(
        x, w_in_2, conv_dw_w_2, conv_dw_b_2, conv_ln_g_2, conv_ln_b_2, short_conv_w_2, a_log_2,
        dt_bias_2, out_norm_g_2, w_out_2, ln_mix_g_2, ln_mix_b_2, ffn_w_gate_2, ffn_w_up_2,
        ffn_w_down_2, router_w_2, moe_w_gate_2, moe_w_up_2, moe_w_down_2, ln_ffn_g_2,
        ln_ffn_b_2,
    )


_drawn_inputs = setup_inputs


def setup_inputs(seed=0):
    import zlib

    import numpy as np

    out = dict(_drawn_inputs(seed))
    spreads = {}
    factors = {'b_ada': 8.0,
     'cmp_pe': 8.0,
     'ln_g': 2.718,
     'ln_b': 2.946,
     'conv_dw_b_2': 5.875,
     'conv_ln_g_2': 5.596,
     'conv_ln_b_2': 7.428,
     'out_norm_g_2': 8.0}
    for name, (base, spread) in spreads.items():
        noise = np.random.default_rng([zlib.crc32(name.encode()), seed]).standard_normal(out[name].shape)
        drawn = base * np.exp(spread * noise) if base else spread * noise
        out[name] = __import__('jax').numpy.asarray(drawn.astype(out[name].dtype))
    for name, factor in factors.items():
        out[name] = (out[name] * factor).astype(out[name].dtype)
    return out
```

```python
import math
from contextlib import ExitStack

import numpy as np
import concourse.bass as bass
from concourse import mybir

P = 128
D = 1024
T = 256
NT = T // P
KD = D // P
DEPTH = 2
HD = 64
DSA_HEADS, FOX_HEADS, NSA_HEADS, NSA_GROUPS = 4, 6, 6, 2
NSA_HPG = NSA_HEADS // NSA_GROUPS
IDX_HEADS, IDX_DIM = 8, 32
TOPK = min(256, T // 4)
CMP_LEN, CMP_STRIDE = 32, 16
NCMP = (T - CMP_LEN) // CMP_STRIDE + 1
NHC = NSA_HEADS * NCMP
ALPHA = (2.0 * DEPTH) ** 0.25
LN_EPS = 1e-5
RMS_EPS = 1e-6
L2_EPS = 1e-6
NEG = -1e30
TAKEN = -3e38
ROPE_THETA = 10000.0

_names = [("dsa_q", 256), ("dsa_k", 64), ("dsa_v", 64), ("idx_q", 256), ("idx_k", 32), ("idx_w", 8),
          ("fox_q", 384), ("fox_k", 384), ("fox_v", 384), ("fox_f", 6), ("nsa_q", 384),
          ("nsa_kc", 128), ("nsa_vc", 128), ("nsa_ks", 128), ("nsa_vs", 128), ("nsa_kw", 128),
          ("nsa_vw", 128), ("nsa_g", 18), ("gate", 1024)]
COL = {}
_at = 0
for _n, _w in _names:
    COL[_n] = (_at, _at + _w)
    _at += _w

W_IN_PARTS = [("idx_q", "idx_w"), ("dsa_q", "dsa_v"), ("fox_v", "fox_f"), ("fox_q", "fox_q"), ("fox_k", "fox_k"),
              ("nsa_q", "nsa_q"), ("nsa_kc", "nsa_ks"), ("nsa_vs", "nsa_g")]
PART_OF = {}
for _a, _b in W_IN_PARTS:
    for _n, _ in _names:
        if COL[_a][0] <= COL[_n][0] < COL[_b][1]:
            PART_OF[_n] = _a

CW = 512
CONV_WIN = 31
SHORT = 4
DH = 4
DK = 128
D_FF = 2816
KF = D_FF // P
NE = 8
D_FE = 3584
KE = D_FE // P

RING = 5
SLOT = KD * 512
FE_PART = 512
NQ = D_FE // FE_PART
MOE_RING = 7
FAR = 1e4


def constants():
    r = np.arange(P)
    row, col = r[:, None], r[None, :]
    parts, later = {}, {}
    parts["ident"] = (row == col).astype(np.float32)
    parts["causal"] = np.where(col <= row, 0.0, NEG).astype(np.float32)
    later["tri_le"] = (row <= col).astype(np.float32)
    later["tri_lt"] = (row < col).astype(np.float32)
    parts["ones"] = np.ones((P, P), np.float32)
    for dim in (HD, IDX_DIM):
        half = dim // 2
        inv = np.float32(ROPE_THETA) ** (-np.arange(half, dtype=np.float32) / np.float32(half))
        ang = np.arange(T, dtype=np.float32)[None, :] * inv.astype(np.float32)[r % half][:, None]
        parts[f"cos{dim}"] = np.cos(ang).astype(np.float32)
        parts[f"sin{dim}"] = np.sin(ang).astype(np.float32)
        rot = np.zeros((P, P), np.float32)
        for m in range(P):
            if m % dim < half:
                rot[m + half, m] = -1.0
            else:
                rot[m - half, m] = 1.0
        parts[f"rot{dim}"] = rot
    cend = np.arange(NCMP) * CMP_STRIDE + CMP_LEN - 1
    cm = np.zeros((P, NT, NSA_HEADS, NCMP), np.float32)
    valid = np.zeros((P, NT), np.float32)
    for i in range(NT):
        t = i * P + r
        cm[:, i] = np.where(cend[None, :] <= t[:, None], 0.0, NEG)[:, None, :]
        valid[:, i] = t >= cend[0]
    parts["cmp_mask"] = cm.reshape(P, -1)
    parts["cmp_valid"] = valid
    blk = np.zeros((P, NSA_HEADS, HD), np.float32)
    for h in range(NSA_HEADS):
        blk[h * NCMP:(h + 1) * NCMP, h] = 1.0
    parts["cmp_block"] = blk.reshape(P, -1)
    later["iota"] = np.broadcast_to(r[None, :], (P, P)).astype(np.float32)
    lv = np.zeros((P, 7, P), np.float32)
    for s in range(7):
        b = 1 << s
        lv[:, s] = -1.0 * ((col // (2 * b) == row // (2 * b)) & ((col // b) % 2 == 1) & ((row // b) % 2 == 0))
    later["levels"] = lv.reshape(P, -1)
    later["level0"] = lv[:, 0].T.copy()
    at = {}
    for group in (parts, later):
        n = 0
        for k, v in group.items():
            at[k] = (n, n + v.shape[1])
            n += v.shape[1]
    return at, *(np.concatenate(list(g.values()), 1).astype(np.float32) for g in (parts, later))


CONST_AT, _CONST, _CONST2 = constants()
NCONST, NCONST2 = _CONST.shape[1], _CONST2.shape[1]


CONST2 = ("tri_le", "tri_lt", "iota", "levels", "level0")
NORMS = 6


class Job:

    def __init__(self, bank, fill, free_before, free_after):
        self.bank, self.fill, self.free_before, self.free_after = bank, fill, free_before, free_after


class Jobs:

    def __init__(self):
        self.fills, self.frees, self.of = [0] * 8, [0] * 8, {}

    def add(self, name, bank, frees=1):
        self.fills[bank] += 1
        before = self.frees[bank]
        self.frees[bank] += frees
        self.of[name] = Job(bank, self.fills[bank], before, self.frees[bank])

    def __getitem__(self, name):
        return self.of[name]


def attention_groups():
    out = []
    for kind in ("fox", "cmp", "win", "slc", "dsa"):
        if kind == "cmp":
            out += [(kind, i, list(range(NSA_HEADS)), NCMP) for i in range(NT)]
        elif kind == "dsa":
            out += [(kind, 0, [0, 1, 2, 3], P), (kind, 1, [0, 1], T), (kind, 1, [2, 3], T)]
        else:
            out += [(kind, 0, [0, 1, 2], P), (kind, 0, [3, 4, 5], P)]
            out += [(kind, 1, [h, h + 1], T) for h in range(0, 6, 2)]
    return out


GROUPS = attention_groups()
NG = len(GROUPS)
MIX_COL = {"dsa": 0, "fox": 256, "cmp": 640, "win": 640, "slc": 640}
GATE_OF = {"cmp": 0, "slc": 1, "win": 2}
ROPES = [("iq", 2, P, IDX_DIM), ("ik", 1, IDX_DIM, IDX_DIM), ("dq", 2, P, HD), ("dk", 1, HD, HD),
         ("nq01", 2, P, HD), ("nq2", 1, P, HD), ("ks", 1, P, HD), ("kw", 1, P, HD)]
PROJECTED = {"iq": "iq", "ik": "ikw", "dq": "dq", "dk": "dkv", "nq01": "nq01", "nq2": "nq2", "ks": "ks", "kw": "kwg"}
ROPE_AT = {r[0]: n for n, r in enumerate(ROPES)}
NR = len(ROPES)
ISCORES = [(i, [q, q + 4]) for i in range(NT) for q in range(4)]
NIS = len(ISCORES)


def plan_first(jobs, l):
    def add(name, bank, frees=1):
        jobs.add((l, name), bank, frees)
    add("ada", 7)
    for m in range(4):
        add(f"xT{m}", m)
    add("iq", 4); add("ikw", 5); add("dq", 6)
    add("rot_iq", 0); add("dkv", 7); add("rot_ik", 1)
    add("fv0", 2); add("fv1", 3); add("ff", 4)
    add("rot_dq", 5); add("rot_dk", 6)
    for n in range(len(ISCORES)):
        add(f"is{n}", [7, 0, 1][n % 3])
    add("fq01", 2); add("fq2", 3); add("fk01", 4); add("fk2", 5)
    add("nq01", 6); add("nq2", 2); add("kcvc", 3)
    add("rot_nq01", 4); add("ks", 5); add("rot_nq2", 6)
    add("vsw", 2); add("kwg", 7); add("rot_ks", 4); add("ch", 3); add("rot_kw", 5)
    for c in range(2):
        for i in range(NT):
            add(f"gt{c}{i}", [6, 2][i])
    add("ckv", 3, 2)
    add("gb0", 4); add("gb1", 5)
    for k in range(NG + 2):
        if k < NG:
            add(f"S{k}", [0, 1, 7][k % 3])
        if 1 <= k <= NG:
            add(f"T{k - 1}", [2, 3][(k - 1) % 2])
        if k >= 2:
            add(f"O{k - 2}", [4, 5][(k - 2) % 2])
    for i in range(NT):
        for half in range(2):
            add(f"yT{i}{half}", [0, 1, 2, 3][2 * i + half])
    for i in range(NT):
        for c in range(2):
            add(f"wo{i}{c}", [4, 5, 6, 7][2 * i + c])


LAST_USE = {"ada0": "ada", "ada1": "ada", "ada2": "ada", "ada3": "ada", "ada4": "gb0", "ada5": "gb1",
            "idx_q": "ikw", "dsa_q": "dkv", "fox_v": "ff", "fox_q": "fq2", "fox_k": "fk2", "nsa_q": "nq2",
            "nsa_kc": "ks", "nsa_vs": "kwg", "cmp_w1": "ch", "gate0": "gt01", "gate1": "gt11",
            "wout0": "wo10", "wout1": "wo11"}


W_IN2 = [("k", 1536), ("q", 1024), ("v", 2048), ("c_gate", 512), ("c_val", 0), ("z", 2560)]
LOGITS2 = 3072
MIX_SMALL = 9
QKV = ["k", "q", "v"]
QKV_CHUNK = {"q": 0, "k": DH, "v": 2 * DH}
LEVELS = 7
FF_PART = 256
NFF = D_FF // FF_PART
NDOWN = -(-KF // 4)


def plan_mixer(jobs, m):
    def add(name, bank, frees=1):
        jobs.add(("mix", m, name), bank, frees)
    add("vw", 7)
    for n in range(4):
        add(f"xT{n}", n)
    add("ba", 4)
    for n, name in enumerate(("k01", "k23", "q01", "q23", "v01", "v23")):
        add(name, [5, 6, 0, 1, 2, 3][n])
    add("c_gate01", 4); add("c_gate23", 5); add("c_val01", 6); add("c_val23", 7)
    add("z0", 0); add("z1", 1)
    add("gc", 2); add("dm0", 3); add("dm1", 4)
    add("kt0", 6); add("kt1", 7); add("vt0", 0); add("vt1", 1)
    add("ss", 5)
    add("kn0", 2); add("kn1", 5)
    add("A0", 6); add("A1", 7); add("at0", 3); add("at1", 4)
    add("LT0", 0); add("LT1", 1); add("aT0", 2); add("aT1", 5)
    for s in range(1, LEVELS):
        for name, b in (("Y0", 6), ("Y1", 7), ("D0", 0), ("E0", 3), ("D1", 1), ("E1", 4)):
            if s < LEVELS - 1 or name[0] != "D":
                add(f"{name}.{s}", b)
    add("ct0", 2); add("ct1", 5)
    add("vn0", 6); add("S1", 7); add("o0", 0)
    add("kS", 1); add("qS", 3)
    add("cb0", 4); add("cb1", 2)
    add("vn1", 5); add("o1", 6)
    add("yd0", 7); add("yd1", 1)
    for i in range(NT):
        for c in range(2):
            add(f"wo{i}{c}", [0, 3, 4, 2][2 * i + c])


def plan_dense(jobs):
    def add(name, bank, frees=1):
        jobs.add(("ffn", 0, name), bank, frees)
    for n in range(4):
        add(f"xT{n}", n)
    for n in range(NFF):
        add(f"g{n}", 2 * (n % 2)); add(f"u{n}", 2 * (n % 2) + 1)
    for i in range(NT):
        for c in range(2):
            add(f"d{i}{c}", 4 + 2 * i + c)


def plan_router(jobs):
    def add(name, bank, frees=1):
        jobs.add(("moe", 0, name), bank, frees)
    for n in range(4):
        add(f"xT{n}", n)
    add("logits", 4); add("places", 5)


LAST_USE.update({"k": "k23", "q": "q23", "v": "v23", "c_gate": "c_gate23", "c_val": "c_val23", "z": "z1",
                 "w_out0": "wo10", "w_out1": "wo11"})
LAST_USE.update({f"gu{n}": f"u{n}" for n in range(NFF)})
LAST_USE.update({f"down{n}": "d11" for n in range(NDOWN)})


def build(nc, A, out_dram):
    fp32 = mybir.dt.float32
    ALU = mybir.AluOpType
    ACT = mybir.ActivationFunctionType
    AX = mybir.AxisListType.X

    jobs = Jobs()
    for l in range(DEPTH):
        plan_first(jobs, l)
    for m in range(DEPTH):
        plan_mixer(jobs, m)
        if m == 0:
            plan_dense(jobs)
    plan_router(jobs)

    loads, load_at, loaded, counts = [], {}, {}, [0] * RING

    def add_load(name, k, width, *src):
        n = len(loads)
        load_at[name] = n
        counts[n % RING] += 16 * len(src)
        loaded[name] = counts[n % RING]
        loads.append((name, k, width, src))

    def cols(w, a, b):
        return w[:, a:b].rearrange("(k p) n -> p k n", p=P)

    for l in range(DEPTH):
        for j in range(4):
            add_load((l, f"ada{j}"), KD, 512, cols(A["w_ada"][l], 512 * j, 512 * j + 512))
        for a, b in W_IN_PARTS:
            c0, c1 = COL[a][0], COL[b][1]
            add_load((l, a), KD, c1 - c0, cols(A["w_in"][l], c0, c1))
            if a == "nsa_kc":
                add_load((l, "cmp_w1"), 2 * CMP_LEN // 2, HD, A["cmp_w1"][l].rearrange("v (j p) m -> p (v j) m", p=P))
        for c in range(2):
            g0 = COL["gate"][0] + 512 * c
            add_load((l, f"gate{c}"), KD, 512, cols(A["w_in"][l], g0, g0 + 512))
        for c in range(2):
            add_load((l, f"ada{4 + c}"), KD, 512, cols(A["w_ada"][l], 512 * (4 + c), 512 * (5 + c)))
        for c in range(2):
            add_load((l, f"wout{c}"), KD, 512, cols(A["w_out"][l], 512 * c, 512 * c + 512))
    for m in range(DEPTH):
        for name, c0 in W_IN2:
            add_load(("mix", m, name), KD, 512, cols(A["w_in_2"][m], c0, c0 + 512))
        for c in range(2):
            add_load(("mix", m, f"w_out{c}"), KD, 512, cols(A["w_out_2"][m], 512 * c, 512 * c + 512))
        if m == 0:
            for n in range(NFF):
                add_load(("ffn", 0, f"gu{n}"), KD, 2 * FF_PART,
                         *(cols(A[w][0], n * FF_PART, (n + 1) * FF_PART) for w in ("ffn_w_gate_2", "ffn_w_up_2")))
            for n in range(NDOWN):
                k = min(4, KF - 4 * n)
                add_load(("ffn", 0, f"down{n}"), k, D,
                         A["ffn_w_down_2"][0][4 * n * P:(4 * n + k) * P, :].rearrange("(k p) n -> p k n", p=P))

    ctx = ExitStack()
    with ctx:
        def sb(name, shape, dtype=fp32):
            return place[0].enter_context(nc.sbuf_tensor(name, shape, dtype))

        place = [ctx]
        semaphores = {}

        def S(name):
            if name not in semaphores:
                semaphores[name] = ctx.enter_context(nc.semaphore(name))
            return semaphores[name]

        ring = sb("ring", [P, RING, SLOT])
        const, const2 = sb("const", [P, NCONST]), sb("const2", [P, NCONST2])
        x = sb("x", [P, NT, D])
        uT = sb("uT", [P, KD, T])
        rows = sb("rows", [P, P])
        vecs = sb("vecs", [P, P])
        lng, lnb = sb("lng", [P, D]), sb("lnb", [P, D])
        lnst = sb("lnst", [P, NT, 2, 6])
        lnmv = sb("lnmv", [P, NT, 4])
        router_w = sb("router_w", [P, KD, NE])
        items = sb("items", [P, 4 * NE + 1], mybir.dt.int32)

        first = ExitStack()
        place[0] = first
        perow = sb("perow", [P, HD])
        pe_sb = sb("pe_sb", [P, DEPTH, 2, CMP_LEN])
        w2 = sb("w2", [HD, DEPTH, 2, HD])
        b_f = sb("b_f", [FOX_HEADS, DEPTH])
        gate1p = sb("gate1p", [P, D])
        adac = sb("adac", [P, 16])
        raw = {n: sb(f"raw_{n}", [P, k, T]) for n, k, _, _ in ROPES}
        rope_t2 = sb("rope_t2", [P, 2, 2 * T])
        rot = {n: sb(f"rot_{n}", [P, k, T]) for n, k, _, _ in ROPES}
        ksS, kwS = sb("ksS", [P, T]), sb("kwS", [P, T])
        iw = sb("iw", [P, NT, IDX_HEADS])
        dv = sb("dv", [P, NT, HD])
        fq, fk = sb("fq", [P, 3, T]), sb("fk", [P, 3, T])
        fv = sb("fv", [P, NT, FOX_HEADS * HD])
        vsw = sb("vsw", [P, NT, 2, P])
        ff = sb("ff", [FOX_HEADS, 5, T])
        sgate = sb("sgate", [P, NT, 18])
        blk = sb("blk", [P, 2, CMP_LEN // 2, NSA_GROUPS, NCMP])
        ch = sb("ch", [HD, 3, 2, NSA_GROUPS * NCMP])
        chrep = sb("chrep", [HD, NSA_GROUPS, NSA_HPG, NCMP])
        kcT = sb("kcT", [P, NSA_GROUPS, NCMP])
        vblk = sb("vblk", [NHC, NSA_HEADS, HD])
        sg = sb("sg", [P, NT, D])
        mix = sb("mix", [P, NT, D])
        isc = sb("isc", [P, NT, T])
        isw = sb("isw", [P, NT, T])
        m8 = sb("m8", [P, NT, 8])
        p_sb, pT = sb("p_sb", [P, 2, 512]), sb("pT", [P, 2, 512])
        relu, rope_t1 = p_sb, pT
        cmp_s = sb("cmp_s", [P, NT, NSA_HEADS, NCMP])
        otmp = sb("otmp", [P, NSA_HEADS * HD])
        stat = sb("stat", [P, 4, 4, 8])
        first.close()

        second = ExitStack()
        place[0] = second
        wba = sb("wba", [P, KD, 2 * DH])
        cvrow = sb("cvrow", [P, 2, P])
        cvec = sb("cvec", [P, 2, P])
        decay_in = sb("decay_in", [P, 2, DH])
        ong = sb("ong", [P, DK])
        hpad = sb("hpad", [P, 4, T + CONV_WIN - 1])
        cacc = sb("cacc", [P, 4, T])
        sig = sb("sig", [P, 4, T])
        cn = sig[:, :, :].rearrange("p f t -> p (f t)").rearrange("p (i n) -> p i n", i=NT)
        ptap = sb("ptap", [P, 2, T])
        qkvpad = sb("qkvpad", [P, 12, T + SHORT - 1])
        over = qkvpad[:, :, :].rearrange("p f t -> p (f t)")
        Lw, LT, attn = (over[:, 1024 * n:1024 * n + 1024].rearrange("p (i n) -> p i n", i=NT) for n in range(3))
        qkv = sb("qkv", [P, 12, T])
        sq = sb("sq", [P, 8, T])
        X, XT = (sq[:, 4 * n:4 * n + 4, :].rearrange("p f t -> p (f t)").rearrange("p (i n) -> p i n", i=NT) for n in range(2))
        sz = sb("sz", [P, NT, 512])
        ktok = sb("ktok", [P, NT, 512])
        vnew = ktok
        kT = sb("kT", [P, DH, T])
        vb = sb("vb", [P, NT, 512])
        kdec = sb("kdec", [P, 512])
        decay = sb("decay", [P, NT, 512])
        attnT = sb("attnT", [P, NT, 512])
        lev = sb("lev", [P, 4, 512])
        NsT, Y = lev[:, 0:2, :], lev[:, 2:4, :]
        z2 = lev[:, :, :].rearrange("p a n -> p (a n)").rearrange("p (i n) -> p i n", i=NT)
        S1 = sb("S1", [P, 512])
        oi = Lw[:, 1, :]
        o = attn
        sm = {n: sb(f"sm_{n}", [P, NT, 2 * DH]) for n in
              ("logit", "eb", "beta", "z", "za", "ze", "zl", "soft", "ea", "g", "ncum", "rest", "coef", "nbe",
               "ss", "lss", "rnorm", "rq", "osum", "oln", "orstd")}
        cstat, cmv = sb("cstat", [P, NT, 6]), sb("cmv", [P, NT, 4])
        osq, eps_col = sb("osq", [P, DK]), sb("eps_col", [P, 1])
        second.close()

        third = ExitStack()
        place[0] = third
        hT = sb("hT", [P, KF, T])
        hs = sb("hs", [P, 2, 512])
        z3 = sb("z3", [P, NT, D])
        third.close()

        fourth = ExitStack()
        place[0] = fourth
        more_slots = sb("more_slots", [P, MOE_RING - RING, SLOT])
        xe = sb("xe", [P, KD, P])
        he = sb("he", [P, KE, P])
        hse = sb("hse", [P, 2, 4 * P])
        ye = sb("ye", [P, D])
        total = sb("total", [P, NT, D])
        pick, pickc = sb("pick", [P, NT, P]), sb("pickc", [P, NT, P])
        pickT = sb("pickT", [P, NT, P])
        logits, best = sb("logits", [P, NT, NE]), sb("best", [P, NT, 8])
        best_at, best_f = sb("best_at", [P, NT, 8], mybir.dt.uint32), sb("best_f", [P, NT, 8])
        gates = sb("gates", [P, NT, 4])
        hot = sb("hot", [P, 2, NT, NE])
        chosen = sb("chosen", [P, NT, NE])
        places, comb = sb("places", [P, NT, 2 * NE]), sb("comb", [P, NT, 2 * NE])
        long = sb("long", [P, 4, NE])
        item_f = sb("item_f", [P, 4 * NE + 1])
        fourth.close()
        place[0] = ctx
        bank = [ctx.enter_context(nc.psum_tensor(f"bank{b}", [P, 512], fp32)) for b in range(8)]

        def C(name, n=P):
            a, b = CONST_AT[name]
            return (const2 if name in CONST2 else const)[0:n, a:b]

        bank_full = [S(f"bank_full{b}") for b in range(8)]
        bank_free = [S(f"bank_free{b}") for b in range(8)]
        slot_loaded = [S(f"slot_loaded{s}") for s in range(RING)]

        def take(pe, job):
            if job.free_before:
                pe.wait_ge(bank_free[job.bank], job.free_before)
            return bank[job.bank]

        def filled(eng, job):
            eng.wait_ge(bank_full[job.bank], job.fill)
            return bank[job.bank]

        def weights(pe, name):
            n = load_at[name]
            pe.wait_ge(slot_loaded[n % RING], loaded[name])
            _, k, width, _ = loads[n]
            return ring[:, n % RING, 0:k * width].rearrange("p (k n) -> p k n", k=k)

        first_ring = len(loads) % RING
        moe_loaded = [S(f"moe_loaded{n}") for n in range(MOE_RING)]

        def moe_slot(p):
            n = p % MOE_RING
            flat = ring[:, (first_ring + n) % RING, :] if n < RING else more_slots[:, n - RING, :]
            return flat.rearrange("p (k n) -> p k n", k=KD if p < 2 * NQ else 4)

        def moe_weights(pe, n, p):
            pe.wait_ge(moe_loaded[p % MOE_RING], n * 48 + 16 * (p // MOE_RING + 1))
            return moe_slot(p)

        def copied(eng, job):
            eng.wait_ge(bank_free[job.bank], job.free_after)

        def chain(eng, sem):
            count = [0]

            def link(ins):
                count[0] += 1
                ins.then_inc(sem, 1)
                eng.wait_ge(sem, count[0])
            return link

        vec_c = lambda k: vecs[:, k:k + 1]
        vec_bada = lambda l: vecs[:, 8 + 16 * l:24 + 16 * l]

        block = ctx.enter_context(nc.Block())

        @block.sync
        def _(sp):
            def slot_free(sp, name):
                what = name[-1]
                if what.startswith("down") and what != f"down{NDOWN - 1}":
                    sp.wait_ge(S("down_used"), int(what[4:]) + 1)
                else:
                    j = jobs[(*name[:-1], LAST_USE[what])]
                    sp.wait_ge(bank_full[j.bank], j.fill)

            def norm_rows(sp, q, g, b):
                if q:
                    sp.wait_ge(S("x_ready"), NT * q)
                sp.dma_start(lng[:, :], g.partition_broadcast(P)).then_inc(S("norm_rows"), 16)
                sp.dma_start(lnb[:, :], b.partition_broadcast(P)).then_inc(S("norm_rows"), 16)

            sp.dma_start(rows[0:8, :], A["c"].rearrange("o (k p) -> (o k) p", p=P)).then_inc(S("rows_loaded"), 16)
            for l in range(DEPTH):
                sp.dma_start(rows[8 + 16 * l:24 + 16 * l, :],
                             A["b_ada"][l, 0:2 * D].rearrange("(k p) -> k p", p=P)).then_inc(S("rows_loaded"), 16)
            sp.dma_start(const[:, :], A["const"]).then_inc(S("const_loaded"), 16)
            sp.dma_start(perow[:, :], A["cmp_pe"].rearrange("l v i d -> (l v i) d")).then_inc(S("small_loaded"), 16)
            sp.dma_start(w2[:, :, :, :], A["cmp_w2"].rearrange("l v a b -> a l v b")).then_inc(S("small_loaded"), 16)
            with nc.allow_non_contiguous_dma(reason="12 numbers"):
                sp.dma_start(b_f[:, :], A["b_f"].rearrange("l h -> h l")).then_inc(S("small_loaded"), 16)
            sp.dma_start(const2[:, :], A["const2"]).then_inc(S("const2_loaded"), 16)
            sp.dma_start(router_w[:, :, :], A["router_w_2"][0].rearrange("(k p) e -> p k e", p=P)).then_inc(S("router_loaded"), 16)
            sp.dma_start(x[:, :, :], A["x"][0].rearrange("(i p) d -> p i d", p=P)).then_inc(S("x_loaded"), 16)
            for n, (name, k, width, src) in enumerate(loads):
                s = n % RING
                if n >= RING:
                    slot_free(sp, loads[n - RING][0])
                dst = ring[:, s, 0:k * width].rearrange("p (k n) -> p k n", k=k)
                w = width // len(src)
                for q, piece in enumerate(src):
                    sp.dma_start(dst[:, :, q * w:(q + 1) * w], piece).then_inc(slot_loaded[s], 16)
                if name[-1] == "nsa_vs":
                    l = name[0]
                    if l:
                        sp.wait_ge(S("x_ready"), NT * l)
                    sp.dma_start(gate1p[:, :], A["b_ada"][l, 2 * D:3 * D].partition_broadcast(P)).then_inc(S("gate_bias"), 16)
                    norm_rows(sp, l, A["ln_g"][l], A["ln_b"][l])
                if name[-1] == "v":
                    m = name[1]
                    q = DEPTH + 2 * m
                    sp.wait_ge(S("x_ready"), NT * q)
                    sp.dma_start(wba[:, :, :], cols(A["w_in_2"][m], LOGITS2, LOGITS2 + 2 * DH)).then_inc(S("mix_small"), 16)
                    sp.dma_start(cvrow[0:CONV_WIN * 4, 0, :], A["conv_dw_w_2"][m].rearrange("j (f p) -> (j f) p", p=P)).then_inc(S("mix_small"), 16)
                    sp.dma_start(cvrow[0:SHORT * 12, 1, :], A["short_conv_w_2"][m].rearrange("j (f p) -> (j f) p", p=P)).then_inc(S("mix_small"), 16)
                    for r, w in enumerate(("conv_dw_b_2", "conv_ln_g_2", "conv_ln_b_2")):
                        sp.dma_start(cvrow[SHORT * 12 + 4 * r:SHORT * 12 + 4 * r + 4, 1, :],
                                     A[w][m].rearrange("(f p) -> f p", p=P)).then_inc(S("mix_small"), 16)
                    sp.dma_start(decay_in[:, 0, :], A["a_log_2"][m].partition_broadcast(P)).then_inc(S("mix_small"), 16)
                    sp.dma_start(decay_in[:, 1, :], A["dt_bias_2"][m].partition_broadcast(P)).then_inc(S("mix_small"), 16)
                    sp.dma_start(ong[:, :], A["out_norm_g_2"][m].partition_broadcast(P)).then_inc(S("mix_small"), 16)
                    norm_rows(sp, q, A["ln_mix_g_2"][m], A["ln_mix_b_2"][m])
                if name[-1] == "gu5":
                    norm_rows(sp, DEPTH + 1, A["ln_ffn_g_2"][0], A["ln_ffn_b_2"][0])
            def moe_load(p, e):
                dst = moe_slot(p)
                if p < 2 * NQ:
                    src = A["moe_w_gate_2" if p % 2 == 0 else "moe_w_up_2"][0]
                    c = p // 2 * FE_PART
                    src = src[e, :, c:c + FE_PART].rearrange("o (k p) n -> p (o k) n", p=P)
                else:
                    r = (p - 2 * NQ) * 4 * P
                    src = A["moe_w_down_2"][0][e, r:r + 4 * P, :].rearrange("o (k p) n -> p (o k) n", p=P)
                sp.dma_start(dst, src).then_inc(moe_loaded[p % MOE_RING], 16)

            def moe_slot_used(n, p):
                if p < MOE_RING:
                    sp.wait_ge(S("moe_down_used"), n * NQ + (p + 1 - NQ))
                else:
                    q = p - MOE_RING
                    sp.wait_ge(S("gate_full" if q % 2 == 0 else "up_full"), n * NQ + (q // 2 + 1))

            for p in range(3 * NQ):
                if p < RING:
                    slot_free(sp, loads[len(loads) - RING + p][0])
                elif p < MOE_RING:
                    sp.wait_ge(S("x_ready"), NT * (NORMS - 1))
                else:
                    moe_slot_used(0, p)
                moe_load(p, bass.ds(0, 1))
                if p == MOE_RING - 1:
                    norm_rows(sp, NORMS - 1, A["ln_ffn_g_2"][1], A["ln_ffn_b_2"][1])
            sp.wait_ge(S("items_ready"), 1)
            nitems = sp.value_load(items[0:1, 4 * NE:4 * NE + 1], min_val=NE, max_val=2 * NE - 1)
            with sp.Fori(1, nitems) as n:
                e = sp.value_load(items[0:1, bass.ds(n + 2 * NE, 1)], min_val=0, max_val=NE - 1)
                for p in range(3 * NQ):
                    moe_slot_used(n, p)
                    moe_load(p, bass.ds(e, 1))
            sp.wait_ge(S("x_ready"), NT * NORMS)
            sp.dma_start(out_dram[0].rearrange("(i p) d -> p i d", p=P), x[:, :, :]).then_inc(S("stored"), 16)
            sp.wait_ge(S("stored"), 16)

        @block.tensor
        def _(pe):
            mm = nc.tensor.matmul

            def at(name):
                return COL[name][0] - COL[PART_OF[name]][0]

            def feat(b, l, name, c0, n, to):
                w = weights(pe, (l, PART_OF[name]))
                a = at(name) + c0
                for k in range(KD):
                    last = mm(b[0:n, to:to + T], w[:, k, a:a + n], uT[:, k, :], start=(k == 0), stop=(k == KD - 1))
                return last

            def tok(b, l, part, a, n, i, to):
                w = weights(pe, (l, part))
                for k in range(KD):
                    last = mm(b[:, to:to + n], uT[:, k, i * P:(i + 1) * P], w[:, k, a:a + n],
                              start=(k == 0), stop=(k == KD - 1))
                return last

            def done(ins, j):
                ins.then_inc(bank_full[j.bank], 1)

            def feats(l, job, *parts):
                j = jobs[l, job]
                b = take(pe, j)
                for n, (name, c0, width) in enumerate(parts):
                    last = feat(b, l, name, c0, width, n * T)
                done(last, j)

            def rotate(l, name):
                n = ROPE_AT[name]
                _, tiles, r, dim = ROPES[n]
                j = jobs[l, f"rot_{name}"]
                b = take(pe, j)
                copied(pe, jobs[l, PROJECTED[name]])
                done(mm(b[0:r, 0:tiles * T], C(f"rot{dim}", r)[:, 0:r], raw[name][0:r, :, :], start=True, stop=True), j)

            pe.wait_ge(S("const_loaded"), 16)
            pe.wait_ge(S("rows_loaded"), 48)
            nc.tensor.transpose(bank[6][:, 0:40], rows[0:40, :], C("ident", 40)[:, 0:40]).then_inc(S("vecs_T"), 1)
            pe.wait_ge(S("small_loaded"), 48)
            nc.tensor.transpose(bank[5][0:HD, 0:P], perow[:, :], C("ident")).then_inc(S("pe_T"), 1)
            pe.wait_ge(S("vecs_ready"), 1)
            pe.wait_ge(S("pe_ready"), 2)

            for l in range(DEPTH):
                j = jobs[l, "ada"]
                b = take(pe, j)
                for q in range(4):
                    w = weights(pe, (l, f"ada{q}"))
                    for m in range(4):
                        for k in range(KD):
                            last = mm(b[:, 4 * q + m:4 * q + m + 1], w[:, k, m * P:(m + 1) * P], vec_c(k),
                                      start=(k == 0), stop=(k == KD - 1))
                done(last, j)
                if l == 0:
                    pe.wait_ge(S("x_loaded"), 16)
                else:
                    pe.wait_ge(S("x_ready"), NT * l)
                for m in range(4):
                    j = jobs[l, f"xT{m}"]
                    b = take(pe, j)
                    for kk in range(2):
                        for i in range(NT):
                            last = nc.tensor.transpose(b[:, kk * T + i * P:kk * T + (i + 1) * P],
                                                       x[:, i, (2 * m + kk) * P:(2 * m + kk + 1) * P], C("ident"))
                    done(last, j)
                for m in range(4):
                    copied(pe, jobs[l, f"xT{m}"])
                feats(l, "iq", ("idx_q", 0, P), ("idx_q", P, P))
                j = jobs[l, "ikw"]
                b = take(pe, j)
                feat(b, l, "idx_k", 0, IDX_DIM, 0)
                for i in range(NT):
                    last = tok(b, l, "idx_q", at("idx_w"), IDX_HEADS, i, T + IDX_HEADS * i)
                done(last, j)
                feats(l, "dq", ("dsa_q", 0, P), ("dsa_q", P, P))
                rotate(l, "iq")
                j = jobs[l, "dkv"]
                b = take(pe, j)
                feat(b, l, "dsa_k", 0, HD, 0)
                for i in range(NT):
                    last = tok(b, l, "dsa_q", at("dsa_v"), HD, i, T + HD * i)
                done(last, j)
                rotate(l, "ik")
                for i in range(NT):
                    j = jobs[l, f"fv{i}"]
                    done(tok(take(pe, j), l, "fox_v", 0, FOX_HEADS * HD, i, 0), j)
                feats(l, "ff", ("fox_f", 0, FOX_HEADS))
                rotate(l, "dq")
                rotate(l, "dk")
                pe.wait_ge(S("rope_done"), NR * l + 2)
                for n, (i, heads) in enumerate(ISCORES):
                    j = jobs[l, f"is{n}"]
                    b = take(pe, j)
                    keys = (i + 1) * P
                    for m, h in enumerate(heads):
                        r = slice(IDX_DIM * (h % 4), IDX_DIM * (h % 4 + 1))
                        last = mm(b[:, m * keys:(m + 1) * keys], rot["iq"][r, h // 4, i * P:(i + 1) * P],
                                  rot["ik"][r, 0, 0:keys], start=True, stop=True)
                    done(last, j)
                feats(l, "fq01", ("fox_q", 0, P), ("fox_q", P, P))
                feats(l, "fq2", ("fox_q", 2 * P, P))
                feats(l, "fk01", ("fox_k", 0, P), ("fox_k", P, P))
                feats(l, "fk2", ("fox_k", 2 * P, P))
                feats(l, "nq01", ("nsa_q", 0, P), ("nsa_q", P, P))
                feats(l, "nq2", ("nsa_q", 2 * P, P))
                feats(l, "kcvc", ("nsa_kc", 0, P), ("nsa_vc", 0, P))
                rotate(l, "nq01")
                feats(l, "ks", ("nsa_ks", 0, P))
                rotate(l, "nq2")
                j = jobs[l, "vsw"]
                b = take(pe, j)
                for i in range(NT):
                    for m, name in enumerate(("nsa_vs", "nsa_vw")):
                        last = tok(b, l, "nsa_vs", at(name), P, i, (2 * i + m) * P)
                done(last, j)
                j = jobs[l, "kwg"]
                b = take(pe, j)
                feat(b, l, "nsa_kw", 0, P, 0)
                for i in range(NT):
                    last = tok(b, l, "nsa_vs", at("nsa_g"), 18, i, T + 18 * i)
                done(last, j)
                rotate(l, "ks")
                j = jobs[l, "ch"]
                b = take(pe, j)
                w1 = weights(pe, (l, "cmp_w1"))
                copied(pe, jobs[l, "kcvc"])
                for v in range(2):
                    for t in range(CMP_LEN // 2):
                        last = mm(b[0:HD, 30 * v:30 * v + 30], w1[:, CMP_LEN // 2 * v + t, :], blk[:, v, t, :, :],
                                  start=(t == 0), stop=(t == CMP_LEN // 2 - 1))
                done(last, j)
                rotate(l, "kw")
                for c in range(2):
                    for i in range(NT):
                        j = jobs[l, f"gt{c}{i}"]
                        b = take(pe, j)
                        w = weights(pe, (l, f"gate{c}"))
                        for k in range(KD):
                            last = mm(b[:, :], uT[:, k, i * P:(i + 1) * P], w[:, k, :], start=(k == 0), stop=(k == KD - 1))
                        done(last, j)
                j = jobs[l, "ckv"]
                b = take(pe, j)
                pe.wait_ge(S("ch_ready"), l + 1)
                mm(b[0:HD, 0:30], w2[:, l, 0, :], ch[:, 2, 0, :], start=True, stop=True)
                done(mm(b[0:NHC, HD:2 * HD], chrep[:, :, :, :], w2[:, l, 1, :], start=True, stop=True), j)
                for c in range(2):
                    j = jobs[l, f"gb{c}"]
                    b = take(pe, j)
                    w = weights(pe, (l, f"ada{4 + c}"))
                    for k in range(KD):
                        last = mm(b[:, :], vec_c(k).broadcast_to([P, P]), w[:, k, :], start=(k == 0), stop=(k == KD - 1))
                    done(last, j)

                def head_qk(kind, h):
                    r = slice(HD * (h % 2), HD * (h % 2 + 1))
                    if kind == "dsa":
                        return rot["dq"][r, h // 2, :], rot["dk"][r, 0, :]
                    if kind == "fox":
                        return fq[r, h // 2, :], fk[r, h // 2, :]
                    g = h // NSA_HPG
                    if kind == "cmp":
                        src = raw["nq01"][r, h // 2, :] if h < 4 else raw["nq2"][r, 0, :]
                        return src, kcT[r, g, :]
                    q = rot["nq01"][r, h // 2, :] if h < 4 else rot["nq2"][r, 0, :]
                    straight, swapped = (rot["ks"][:, 0, :], ksS) if kind == "slc" else (rot["kw"][:, 0, :], kwS)
                    return q, (straight if g == h % 2 else swapped)[r, :]

                def scores(n):
                    kind, i, heads, keys = GROUPS[n]
                    j = jobs[l, f"S{n}"]
                    b = take(pe, j)
                    nh = len(heads)
                    if n == 0:
                        for need in ("fq01", "fq2", "fk01", "fk2", "fv0", "fv1"):
                            copied(pe, jobs[l, need])
                        pe.wait_ge(S("fox_ready"), l + 1)
                        copied(pe, jobs[l, "ckv"])
                        copied(pe, jobs[l, "vsw"])
                        copied(pe, jobs[l, "dkv"])
                        pe.wait_ge(S("rope_done"), NR * (l + 1))
                    if kind == "dsa" and heads[0] == 0:
                        pe.wait_ge(S("sel_ready"), NT * l + i + 1)
                    first = [True]

                    def add(o, w, m):
                        ins = mm(o, w, m, start=first[0], stop=False, skip_group_check=True)
                        first[0] = False
                        return ins

                    def head(m):
                        q, k = head_qk(kind, heads[m])
                        return add(b[:, m * keys:(m + 1) * keys], q[:, i * P:(i + 1) * P], k[:, 0:keys])

                    for m, h in enumerate(heads):
                        if kind == "fox":
                            add(b[:, m * keys:(m + 1) * keys], C("ident", FOX_HEADS)[:, h:h + 1].broadcast_to([FOX_HEADS, P]),
                                ff[:, 4, 0:keys])
                        if h % 2 == 0:
                            upper = head(m)
                    upper.then_inc(S("upper_heads"), 1)
                    view = b[:, 0:nh * keys].rearrange("p (h s) -> p h s", h=nh)
                    if kind == "cmp":
                        m0 = CONST_AT["cmp_mask"][0] + i * NHC
                        last = add(b[:, 0:NHC], C("ident"), const[:, m0:m0 + NHC])
                    elif kind == "dsa":
                        last = add(view, C("ident"), isw[:, i, 0:keys].unsqueeze(1).broadcast_to([P, nh, keys]))
                    else:
                        last = add(view[:, :, keys - P:keys], C("ident"), C("causal").unsqueeze(1).broadcast_to([P, nh, P]))
                    pe.wait_ge(S("upper_heads"), NG * l + n + 1)
                    for m, h in enumerate(heads):
                        if h % 2:
                            last = head(m)
                    done(last, j)

                def transposes(n):
                    kind, i, heads, keys = GROUPS[n]
                    j = jobs[l, f"T{n}"]
                    b = take(pe, j)
                    if kind == "cmp":
                        pe.wait_ge(S("cmp_p_ready"), NT * l + i + 1)
                    else:
                        copied(pe, jobs[l, f"S{n}"])
                    if kind == "cmp":
                        last = nc.tensor.transpose(b[0:NHC, 0:P], p_sb[:, n % 2, 0:NHC], C("ident"))
                    else:
                        for c in range(len(heads) * keys // P):
                            last = nc.tensor.transpose(b[:, c * P:(c + 1) * P], p_sb[:, n % 2, c * P:(c + 1) * P], C("ident"))
                    done(last, j)

                def outputs(n):
                    kind, i, heads, keys = GROUPS[n]
                    j = jobs[l, f"O{n}"]
                    b = take(pe, j)
                    copied(pe, jobs[l, f"T{n}"])
                    if kind == "cmp":
                        last = mm(b[:, 0:NSA_HEADS * HD], pT[0:NHC, n % 2, 0:P], vblk[:, :, :], start=True, stop=True)
                    else:
                        nk = keys // P
                        for m, h in enumerate(heads):
                            for c in range(nk):
                                if kind == "dsa":
                                    v = dv[:, c, :]
                                elif kind == "fox":
                                    v = fv[:, c, h * HD:(h + 1) * HD]
                                else:
                                    g = h // NSA_HPG
                                    v = vsw[:, c, 0 if kind == "slc" else 1, g * HD:(g + 1) * HD]
                                last = mm(b[:, m * HD:(m + 1) * HD], pT[:, n % 2, (m * nk + c) * P:(m * nk + c + 1) * P], v,
                                          start=(c == 0), stop=(c == nk - 1))
                    done(last, j)

                for n in range(NG + 2):
                    if n < NG:
                        scores(n)
                    if 1 <= n <= NG:
                        transposes(n - 1)
                    if n >= 2:
                        outputs(n - 2)
                for i in range(NT):
                    pe.wait_ge(S("mix_ready"), NT * l + i + 1)
                    for half in range(2):
                        j = jobs[l, f"yT{i}{half}"]
                        b = take(pe, j)
                        for kk in range(4):
                            k = 4 * half + kk
                            last = nc.tensor.transpose(b[:, kk * P:(kk + 1) * P], mix[:, i, k * P:(k + 1) * P], C("ident"))
                        done(last, j)
                for i in range(NT):
                    for half in range(2):
                        copied(pe, jobs[l, f"yT{i}{half}"])
                    for c in range(2):
                        j = jobs[l, f"wo{i}{c}"]
                        b = take(pe, j)
                        w = weights(pe, (l, f"wout{c}"))
                        for k in range(KD):
                            last = mm(b[:, :], uT[:, k, i * P:(i + 1) * P], w[:, k, :], start=(k == 0), stop=(k == KD - 1))
                        done(last, j)

            def transpose_x(key, q):
                pe.wait_ge(S("x_ready"), NT * q)
                for m in range(4):
                    j = jobs[(*key, f"xT{m}")]
                    b = take(pe, j)
                    for kk in range(2):
                        for i in range(NT):
                            last = nc.tensor.transpose(b[:, kk * T + i * P:kk * T + (i + 1) * P],
                                                       x[:, i, (2 * m + kk) * P:(2 * m + kk + 1) * P], C("ident"))
                    done(last, j)
                for m in range(4):
                    copied(pe, jobs[(*key, f"xT{m}")])

            def heads4(b, lhsT, rhs):
                for h in range(DH):
                    last = mm(b[:, h * P:(h + 1) * P], lhsT(h), rhs(h), start=True, stop=True)
                return last

            def transposes4(b, src):
                for h in range(4):
                    last = nc.tensor.transpose(b[:, h * P:(h + 1) * P], src(h), C("ident"))
                return last

            pe.wait_ge(S("const2_loaded"), 16)

            def mixer(m):
                q = DEPTH + 2 * m
                J = lambda name: jobs["mix", m, name]
                hs_ = lambda h: slice(h * P, (h + 1) * P)
                tile = lambda i: slice(i * P, (i + 1) * P)
                pe.wait_ge(S("mix_small"), 16 * MIX_SMALL * (m + 1))
                j = J("vw")
                b = take(pe, j)
                n0, n1 = CONV_WIN * 4, SHORT * 12 + 12
                nc.tensor.transpose(b[:, 0:n0], cvrow[0:n0, 0, :], C("ident", n0)[:, 0:n0])
                done(nc.tensor.transpose(b[:, P:P + n1], cvrow[0:n1, 1, :], C("ident", n1)[:, 0:n1]), j)
                transpose_x(("mix", m), q)
                j = J("ba")
                b = take(pe, j)
                for i in range(NT):
                    for k in range(KD):
                        last = mm(b[:, 8 * i:8 * i + 8], uT[:, k, tile(i)], wba[:, k, :], start=(k == 0), stop=(k == KD - 1))
                done(last, j)
                for name in ("k", "q", "v", "c_gate", "c_val"):
                    w = weights(pe, ("mix", m, name))
                    for half in range(2):
                        j = J(f"{name}{2 * half}{2 * half + 1}")
                        b = take(pe, j)
                        for f in range(2):
                            a = (2 * half + f) * P
                            for k in range(KD):
                                last = mm(b[:, f * T:(f + 1) * T], w[:, k, a:a + P], uT[:, k, :], start=(k == 0), stop=(k == KD - 1))
                        done(last, j)
                w = weights(pe, ("mix", m, "z"))
                for i in range(NT):
                    j = J(f"z{i}")
                    b = take(pe, j)
                    for k in range(KD):
                        last = mm(b[:, :], uT[:, k, tile(i)], w[:, k, :], start=(k == 0), stop=(k == KD - 1))
                    done(last, j)
                pe.wait_ge(S("g_ready"), m + 1)
                j = J("gc")
                b = take(pe, j)
                for i in range(NT):
                    mm(b[:, DH * i:DH * i + DH], C("tri_le"), sm["g"][:, i, 0:DH], start=True, stop=True)
                    last = mm(b[:, 8 + DH * i:8 + DH * i + DH], C("ones"), sm["g"][:, i, 0:DH], start=True, stop=True)
                done(last, j)
                for i in range(NT):
                    j = J(f"dm{i}")
                    b = take(pe, j)
                    for h in range(DH):
                        mm(b[:, hs_(h)], sm["g"][:, i, h:h + 1].broadcast_to([P, P]), C("tri_le"), start=(h == 0), stop=False,
                           skip_group_check=True)
                    done(mm(b[:, :].rearrange("p (h c) -> p h c", h=DH), C("ident"),
                            C("causal").unsqueeze(1).broadcast_to([P, DH, P]), start=False, stop=True, skip_group_check=True), j)
                pe.wait_ge(S("squares"), 4 * (m + 1))
                j = J("ss")
                b = take(pe, j)
                for i in range(NT):
                    for f in range(8):
                        last = mm(b[:, 8 * i + f:8 * i + f + 1], sq[:, f, tile(i)], C("ones")[:, 0:1], start=True, stop=True)
                done(last, j)
                for i in range(NT):
                    j = J(f"kt{i}")
                    done(transposes4(take(pe, j), lambda h: qkv[:, h, tile(i)]), j)
                pe.wait_ge(S("qkv_silu"), 6 * (m + 1))
                for i in range(NT):
                    j = J(f"vt{i}")
                    done(transposes4(take(pe, j), lambda h: qkv[:, 8 + h, tile(i)]), j)
                for i in range(NT):
                    j = J(f"kn{i}")
                    b = take(pe, j)
                    copied(pe, J(f"kt{i}"))
                    done(transposes4(b, lambda h: ktok[:, i, hs_(h)]), j)
                for i in range(NT):
                    copied(pe, J(f"kn{i}"))
                    j = J(f"A{i}")
                    done(heads4(take(pe, j), lambda h: kT[:, h, tile(i)], lambda h: kT[:, h, tile(i)]), j)
                for i in range(NT):
                    j = J(f"at{i}")
                    done(heads4(take(pe, j), lambda h: qkv[:, 4 + h, tile(i)], lambda h: kT[:, h, tile(i)]), j)
                for i in range(NT):
                    j = J(f"LT{i}")
                    b = take(pe, j)
                    copied(pe, J(f"A{i}"))
                    done(transposes4(b, lambda h: Lw[:, i, hs_(h)]), j)
                for i in range(NT):
                    j = J(f"aT{i}")
                    b = take(pe, j)
                    copied(pe, J(f"at{i}"))
                    done(transposes4(b, lambda h: attn[:, i, hs_(h)]), j)
                for s in range(1, LEVELS):
                    for i in range(NT):
                        if s == 1:
                            pe.wait_ge(S("x_first"), NT * m + i + 1)
                        else:
                            copied(pe, J(f"D{i}.{s - 1}"))
                            copied(pe, J(f"E{i}.{s - 1}"))
                        j = J(f"Y{i}.{s}")
                        b = take(pe, j)
                        pe.wait_ge(S("level_ready"), NT * ((LEVELS - 1) * m + s - 1) + i + 1)
                        done(heads4(b, lambda h: NsT[:, i, hs_(h)], lambda h: X[:, i, hs_(h)]), j)
                    for i in range(NT):
                        copied(pe, J(f"Y{i}.{s}"))
                        if s < LEVELS - 1:
                            j = J(f"D{i}.{s}")
                            done(heads4(take(pe, j), lambda h: XT[:, i, hs_(h)], lambda h: Y[:, i, hs_(h)]), j)
                        j = J(f"E{i}.{s}")
                        done(heads4(take(pe, j), lambda h: Y[:, i, hs_(h)], lambda h: XT[:, i, hs_(h)]), j)
                pe.wait_ge(S("conv_dve"), m + 1)
                pe.wait_ge(S("conv_pool"), m + 1)
                for i in range(NT):
                    j = J(f"ct{i}")
                    done(transposes4(take(pe, j), lambda f: cacc[:, f, tile(i)]), j)
                copied(pe, J(f"E0.{LEVELS - 1}"))
                copied(pe, J("vt0"))
                j = J("vn0")
                done(heads4(take(pe, j), lambda h: XT[:, 0, hs_(h)], lambda h: vb[:, 0, hs_(h)]), j)
                copied(pe, J("vn0"))
                pe.wait_ge(S("kdec_ready"), m + 1)
                j = J("S1")
                done(heads4(take(pe, j), lambda h: kdec[:, hs_(h)], lambda h: vnew[:, 0, hs_(h)]), j)
                copied(pe, J("aT0"))
                j = J("o0")
                done(heads4(take(pe, j), lambda h: attnT[:, 0, hs_(h)], lambda h: vnew[:, 0, hs_(h)]), j)
                copied(pe, J("S1"))
                j = J("kS")
                done(heads4(take(pe, j), lambda h: kT[:, h, tile(1)], lambda h: S1[:, hs_(h)]), j)
                j = J("qS")
                done(heads4(take(pe, j), lambda h: qkv[:, 4 + h, tile(1)], lambda h: S1[:, hs_(h)]), j)
                for i in range(NT):
                    j = J(f"cb{i}")
                    b = take(pe, j)
                    copied(pe, J(f"ct{i}"))
                    done(transposes4(b, lambda f: cn[:, i, hs_(f)]), j)
                copied(pe, J(f"E1.{LEVELS - 1}"))
                copied(pe, J("kS"))
                j = J("vn1")
                done(heads4(take(pe, j), lambda h: XT[:, 1, hs_(h)], lambda h: vb[:, 1, hs_(h)]), j)
                copied(pe, J("vn1"))
                copied(pe, J("aT1"))
                j = J("o1")
                done(heads4(take(pe, j), lambda h: attnT[:, 1, hs_(h)], lambda h: vnew[:, 1, hs_(h)]), j)
                for i in range(NT):
                    pe.wait_ge(S("delta_ready"), NT * m + i + 1)
                    j = J(f"yd{i}")
                    done(transposes4(take(pe, j), lambda h: o[:, i, hs_(h)]), j)
                for i in range(NT):
                    copied(pe, J(f"cb{i}"))
                    copied(pe, J(f"yd{i}"))
                    for c in range(2):
                        w = weights(pe, ("mix", m, f"w_out{c}"))
                        j = J(f"wo{i}{c}")
                        b = take(pe, j)
                        for k in range(KD):
                            last = mm(b[:, :], uT[:, k, tile(i)], w[:, k, :], start=(k == 0), stop=(k == KD - 1))
                        done(last, j)

            def dense():
                J = lambda name: jobs["ffn", 0, name]
                transpose_x(("ffn", 0), DEPTH + 1)
                for n in range(NFF):
                    w = weights(pe, ("ffn", 0, f"gu{n}"))
                    for side, name in enumerate("gu"):
                        j = J(f"{name}{n}")
                        b = take(pe, j)
                        for f in range(2):
                            a = FF_PART * side + f * P
                            for k in range(KD):
                                last = mm(b[:, f * T:(f + 1) * T], w[:, k, a:a + P], uT[:, k, :], start=(k == 0), stop=(k == KD - 1))
                        done(last, j)
                out = {(i, c): take(pe, J(f"d{i}{c}")) for i in range(NT) for c in range(2)}
                for n in range(NFF):
                    copied(pe, J(f"u{n}"))
                for n in range(NDOWN):
                    w = weights(pe, ("ffn", 0, f"down{n}"))
                    for kk in range(loads[load_at["ffn", 0, f"down{n}"]][1]):
                        k = 4 * n + kk
                        for (i, c), b in out.items():
                            last = mm(b[:, :], hT[:, k, i * P:(i + 1) * P], w[:, kk, 512 * c:512 * c + 512],
                                      start=(k == 0), stop=(k == KF - 1))
                            if k == KF - 1:
                                done(last, J(f"d{i}{c}"))
                    if n < NDOWN - 1:
                        last.then_inc(S("down_used"), 1)

            def gather():
                for half in range(2):
                    for f in range(4):
                        for i in range(NT):
                            last = mm(bank[4 + half][:, f * P:(f + 1) * P], x[:, i, (4 * half + f) * P:(4 * half + f + 1) * P],
                                      pick[:, i, :], start=(i == 0), stop=(i == NT - 1))
                    last.then_inc(S("gathered"), 1)

            def turn_picks():
                for i in range(NT):
                    last = nc.tensor.transpose(bank[6][:, i * P:(i + 1) * P], pickc[:, i, :], C("ident"))
                last.then_inc(S("picks_full"), 1)

            def experts():
                transpose_x(("moe", 0), NORMS - 1)
                pe.wait_ge(S("router_loaded"), 16)
                j = jobs["moe", 0, "logits"]
                b = take(pe, j)
                for i in range(NT):
                    for k in range(KD):
                        last = mm(b[:, NE * i:NE * i + NE], uT[:, k, i * P:(i + 1) * P], router_w[:, k, :],
                                  start=(k == 0), stop=(k == KD - 1))
                done(last, j)
                pe.wait_ge(S("chosen_ready"), 1)
                j = jobs["moe", 0, "places"]
                b = take(pe, j)
                mm(b[:, 0:NE], C("tri_lt"), chosen[:, 0, :], start=True, stop=True)
                for to, w in ((NE, "tri_lt"), (2 * NE, "ones")):
                    mm(b[:, to:to + NE], C("ones"), chosen[:, 0, :], start=True, stop=False)
                    last = mm(b[:, to:to + NE], C(w), chosen[:, 1, :], start=False, stop=True)
                done(last, j)
                copied(pe, jobs["moe", 0, "logits"])
                copied(pe, j)
                pe.wait_ge(S("picked"), 1)
                gather()
                turn_picks()
                pe.wait_ge(S("items_ready"), 1)
                nitems = pe.value_load(items[0:1, 4 * NE:4 * NE + 1], min_val=NE, max_val=2 * NE - 1)
                with pe.Fori(0, nitems) as n:
                    pe.wait_ge(S("xe_low"), n + 1)
                    pe.wait_ge(S("xe_high"), n + 1)
                    for q in range(NQ):
                        if q < 2:
                            pe.wait_ge(S("acc_added"), n * 4 + (2 * q + 2))
                        else:
                            pe.wait_ge(S("hidden_ready"), n * NQ + (q - 1))
                        for side, full in enumerate(("gate_full", "up_full")):
                            w = moe_weights(pe, n, 2 * q + side)
                            b = bank[2 * (q % 2) + side]
                            for f in range(4):
                                for k in range(KD):
                                    last = mm(b[:, f * P:(f + 1) * P], w[:, k, f * P:(f + 1) * P], xe[:, k, :],
                                              start=(k == 0), stop=(k == KD - 1))
                            last.then_inc(S(full), 1)
                    pe.wait_ge(S("picks_copied"), n + 1)
                    for r in range(NQ):
                        w = moe_weights(pe, n, 2 * NQ + r)
                        pe.wait_ge(S("hidden_ready"), n * NQ + (r + 1))
                        for kk in range(4):
                            k = 4 * r + kk
                            for c in range(2):
                                last = mm(bank[6 + c][:, :], he[:, k, :], w[:, kk, 512 * c:512 * c + 512],
                                          start=(k == 0), stop=(k == KE - 1))
                        last.then_inc(S("moe_down_used"), 1)
                    pe.wait_ge(S("picked"), n + 2)
                    gather()
                    pe.wait_ge(S("ye_copied"), n + 1)
                    for i in range(NT):
                        for c in range(2):
                            mm(bank[2 * i + c][:, :], pickT[:, i, :], ye[:, 512 * c:512 * c + 512], start=True, stop=True)\
                                .then_inc(S("scattered"), 1)
                    turn_picks()

            mixer(0)
            dense()
            mixer(1)
            experts()

        @block.scalar
        def _(act):
            link = chain(act, S("act_chain"))
            go = nc.scalar.activation

            def free(ins, j):
                ins.then_inc(bank_free[j.bank], 1)

            def copy(out, in_, scale=1.0):
                return go(out, in_, ACT.Copy, scale=scale)

            def norm_scale(q):
                for i in range(NT):
                    act.wait_ge(S("var_ready"), NT * q + i + 1)
                    link(go(lnmv[:, i, 2:3], lnmv[:, i, 1:2], ACT.Ln))
                    go(lnmv[:, i, 3:4], lnmv[:, i, 2:3], ACT.Exp, scale=-0.5).then_inc(S("rstd_ready"), 1)

            act.wait_ge(S("pe_T"), 1)
            for v in range(2):
                go(pe_sb[v * HD:(v + 1) * HD, :, :, :], bank[5][0:HD, 0:P], ACT.Copy).then_inc(S("pe_ready"), 1)
            for l in range(DEPTH):
                copied(act, jobs[l, "ada"])
                for m in (1, 3):
                    j = jobs[l, f"xT{m}"]
                    b = filled(act, j)
                    for k in (2 * m, 2 * m + 1):
                        last = go(uT[:, k, :], b[:, (k % 2) * T:(k % 2 + 1) * T], ACT.Identity, bias=adac[:, k:k + 1],
                                  scale=adac[:, 8 + k:9 + k])
                    free(last, j)
                j = jobs[l, "iq"]
                free(copy(raw["iq"][:, :, :], filled(act, j)[:, :]), j)
                j = jobs[l, "ikw"]
                b = filled(act, j)
                copy(raw["ik"][0:IDX_DIM, 0, :], b[0:IDX_DIM, 0:T])
                free(copy(iw[:, :, :], b[:, T:T + 16], IDX_HEADS ** -0.5), j)
                j = jobs[l, "dq"]
                free(copy(raw["dq"][:, :, :], filled(act, j)[:, :], HD ** -0.5), j)
                j = jobs[l, "dkv"]
                b = filled(act, j)
                copy(raw["dk"][0:HD, 0, :], b[0:HD, 0:T])
                free(copy(dv[:, :, :], b[:, T:T + NT * HD]), j)
                for i in range(NT):
                    j = jobs[l, f"fv{i}"]
                    free(copy(fv[:, i, :], filled(act, j)[:, 0:FOX_HEADS * HD]), j)
                copied(act, jobs[l, "ff"])
                link(go(ff[:, 1, :], ff[:, 0, :], ACT.Abs))
                link(go(ff[:, 2, :], ff[:, 1, :], ACT.Exp, scale=-1.0))
                go(ff[:, 1, :], ff[:, 2, :], ACT.Ln, bias=1.0).then_inc(S("log1p_ready"), 1)
                for n in range(NIS):
                    j = jobs[l, f"is{n}"]
                    b = filled(act, j)
                    if NIS * l + n >= 2:
                        act.wait_ge(S("isc_steps"), NIS * l + n - 1)
                    w = 2 * (ISCORES[n][0] + 1) * P
                    free(go(relu[:, n % 2, 0:w], b[:, 0:w], ACT.Relu), j)
                for name, dst, tiles in (("fq01", fq, (0, 2)), ("fq2", fq, (2, 3)), ("fk01", fk, (0, 2)), ("fk2", fk, (2, 3))):
                    j = jobs[l, name]
                    free(copy(dst[:, tiles[0]:tiles[1], :], filled(act, j)[:, 0:(tiles[1] - tiles[0]) * T],
                              HD ** -0.5 if dst is fq else 1.0), j)
                j = jobs[l, "nq01"]
                free(copy(raw["nq01"][:, :, :], filled(act, j)[:, :], HD ** -0.5), j)
                j = jobs[l, "nq2"]
                free(copy(raw["nq2"][:, 0, :], filled(act, j)[:, 0:T], HD ** -0.5), j)
                j = jobs[l, "ks"]
                free(copy(raw["ks"][:, 0, :], filled(act, j)[:, 0:T]), j)
                j = jobs[l, "vsw"]
                free(copy(vsw[:, :, :, :], filled(act, j)[:, :]), j)
                j = jobs[l, "kwg"]
                b = filled(act, j)
                copy(raw["kw"][:, 0, :], b[:, 0:T])
                free(go(sgate[:, :, :], b[:, T:T + 36], ACT.Exp, scale=-1.0), j)
                j = jobs[l, "ch"]
                go(ch[:, 0, :, :], filled(act, j)[0:HD, 0:60], ACT.Exp, scale=-1.0).then_inc(S("ch_exp"), 1)
                for c in range(2):
                    for i in range(NT):
                        j = jobs[l, f"gt{c}{i}"]
                        free(go(sg[:, i, 512 * c:512 * c + 512], filled(act, j)[:, :], ACT.Silu), j)
                j = jobs[l, "ckv"]
                b = filled(act, j)
                copy(kcT[0:HD, :, :], b[0:HD, 0:30])
                free(copy(kcT[HD:P, :, :], b[0:HD, 0:30]), j)
                for n, (kind, i, heads, keys) in enumerate(GROUPS):
                    if n >= 2:
                        act.wait_ge(bank_full[jobs[l, f"T{n - 2}"].bank], jobs[l, f"T{n - 2}"].fill)
                    if kind == "cmp":
                        copied(act, jobs[l, f"S{n}"])
                        go(p_sb[:, n % 2, 0:NHC], cmp_s[:, i, :, :], ACT.Exp).then_inc(S("cmp_p_ready"), 1)
                        continue
                    j = jobs[l, f"S{n}"]
                    act.wait_ge(S("max_ready"), NG * l + n + 1)
                    b = filled(act, j)
                    for m in range(len(heads)):
                        last = go(p_sb[:, n % 2, m * keys:(m + 1) * keys], b[:, m * keys:(m + 1) * keys], ACT.Exp,
                                  bias=stat[:, n % 4, 0, m:m + 1], accum_out=stat[:, n % 4, 1, m:m + 1])
                    free(last, j)
                for i in range(NT):
                    for half in range(2):
                        j = jobs[l, f"yT{i}{half}"]
                        free(copy(uT[:, 4 * half:4 * half + 4, i * P:(i + 1) * P], filled(act, j)[:, :]), j)
                norm_scale(l)

            def copy_xT(key):
                for m in (1, 3):
                    j = jobs[(*key, f"xT{m}")]
                    free(copy(uT[:, 2 * m:2 * m + 2, :], filled(act, j)[:, :]), j)

            def mixer(m):
                q = DEPTH + 2 * m
                J = lambda name: jobs["mix", m, name]
                hs_ = lambda h: slice(h * P, (h + 1) * P)
                tile = lambda i: slice(i * P, (i + 1) * P)
                two = lambda a: a.rearrange("p (f t) -> p f t", f=2)
                copy_xT(("mix", m))
                act.wait_ge(S("pads_ready"), m + 1)
                for n, name in enumerate(QKV):
                    for half in range(2):
                        j = J(f"{name}{2 * half}{2 * half + 1}")
                        f = 4 * n + 2 * half
                        free(copy(qkvpad[:, f:f + 2, SHORT - 1:], two(filled(act, j)[:, :])), j)
                go(sm["ea"][:, 0, 0:DH], decay_in[:, 0, :], ACT.Exp)
                copied(act, J("ba"))
                go(sm["eb"][:, :, 0:DH], sm["logit"][:, :, 0:DH], ACT.Exp, scale=-1.0)
                act.wait_ge(S("dt_ready"), m + 1)
                link(go(sm["za"][:, :, 0:DH], sm["z"][:, :, 0:DH], ACT.Abs))
                link(go(sm["ze"][:, :, 0:DH], sm["za"][:, :, 0:DH], ACT.Exp, scale=-1.0))
                go(sm["zl"][:, :, 0:DH], sm["ze"][:, :, 0:DH], ACT.Ln, bias=1.0).then_inc(S("soft_ready"), 1)
                for half in range(2):
                    j = J(f"c_gate{2 * half}{2 * half + 1}")
                    free(go(sig[:, 2 * half:2 * half + 2, :], two(filled(act, j)[:, :]), ACT.Sigmoid), j)
                for n in range(6):
                    act.wait_ge(S("short_done"), 6 * m + n + 1)
                    part = qkv[:, 2 * n:2 * n + 2, :]
                    go(part, part, ACT.Silu).then_inc(S("qkv_silu"), 1)
                    if n < 4:
                        act.wait_ge(S("qkv_silu"), 6 * m + n + 1)
                        go(sq[:, 2 * n:2 * n + 2, :], part, ACT.Square).then_inc(S("squares"), 1)
                for i in range(NT):
                    j = J(f"z{i}")
                    free(go(sz[:, i, :], filled(act, j)[:, :], ACT.Silu), j)
                copied(act, J("gc"))
                go(sm["coef"][:, 0, 0:DH], sm["rest"][:, 0, 0:DH], ACT.Exp, scale=-1.0)
                go(sm["coef"][:, 1, 0:DH], sm["ncum"][:, 1, 0:DH], ACT.Exp).then_inc(S("coef_ready"), 1)
                for i in range(NT):
                    j = J(f"dm{i}")
                    b = filled(act, j)
                    for h in range(DH):
                        last = go(decay[:, i, hs_(h)], b[:, hs_(h)], ACT.Exp, bias=sm["ncum"][:, i, h:h + 1])
                    free(last, j)
                copied(act, J("ss"))
                link(go(sm["lss"][:, :, :], sm["ss"][:, :, :], ACT.Ln))
                go(sm["rnorm"][:, :, :], sm["lss"][:, :, :], ACT.Exp, scale=-0.5).then_inc(S("rnorm_ready"), 1)
                for i in range(NT):
                    j = J(f"kn{i}")
                    free(copy(kT[:, :, tile(i)], filled(act, j)[:, :].rearrange("p (h t) -> p h t", h=DH)), j)
                for name, dst in (("LT", LT), ("aT", attnT)):
                    for i in range(NT):
                        j = J(f"{name}{i}")
                        free(copy(dst[:, i, :], filled(act, j)[:, :]), j)
                for s in range(1, LEVELS):
                    for i in range(NT):
                        j = J(f"Y{i}.{s}")
                        free(copy(Y[:, i, :], filled(act, j)[:, :]), j)
                for i in range(NT):
                    act.wait_ge(S("cvar_ready"), NT * m + i + 1)
                    link(go(cmv[:, i, 2:3], cmv[:, i, 1:2], ACT.Ln))
                    go(cmv[:, i, 3:4], cmv[:, i, 2:3], ACT.Exp, scale=-0.5).then_inc(S("crstd_ready"), 1)
                j = J("vn0")
                act.wait_ge(S("kdec_ready"), m + 1)
                free(copy(vnew[:, 0, :], filled(act, j)[:, :]), j)
                j = J("S1")
                free(copy(S1[:, :], filled(act, j)[:, :]), j)
                j = J("qS")
                b = filled(act, j)
                for h in range(DH):
                    last = copy(oi[:, hs_(h)], b[:, hs_(h)], sm["coef"][:, 1, h:h + 1])
                free(last, j)

                def rms(i):
                    if i == 0:
                        copied(act, J("o0"))
                    else:
                        act.wait_ge(S("o1_ready"), m + 1)
                    for h in range(DH):
                        link(go(osq[:, :], o[:, i, hs_(h)], ACT.Square, accum_out=sm["osum"][:, i, h:h + 1]))
                    link(go(sm["oln"][:, i, 0:DH], sm["osum"][:, i, 0:DH], ACT.Ln, scale=1.0 / DK, bias=eps_col[:, 0:1]))
                    go(sm["orstd"][:, i, 0:DH], sm["oln"][:, i, 0:DH], ACT.Exp, scale=-0.5).then_inc(S("orstd_ready"), 1)

                rms(0)
                j = J("vn1")
                free(copy(vnew[:, 1, :], filled(act, j)[:, :]), j)
                rms(1)
                for i in range(NT):
                    j = J(f"cb{i}")
                    b = filled(act, j)
                    for f in range(4):
                        last = go(uT[:, f, tile(i)], b[:, hs_(f)], ACT.Silu, scale=cvec[:, 1, 52 + f:53 + f],
                                  bias=cvec[:, 1, 56 + f:57 + f])
                    free(last, j)
                for i in range(NT):
                    j = J(f"yd{i}")
                    free(copy(uT[:, 4:8, tile(i)], filled(act, j)[:, :].rearrange("p (f t) -> p f t", f=4)), j)
                norm_scale(q)

            def dense():
                J = lambda name: jobs["ffn", 0, name]
                copy_xT(("ffn", 0))
                for n in range(NFF):
                    j = J(f"g{n}")
                    b = filled(act, j)
                    if n >= 2:
                        copied(act, J(f"u{n - 2}"))
                    free(go(hs[:, n % 2, :], b[:, :], ACT.Silu), j)
                norm_scale(DEPTH + 1)

            def experts():
                copy_xT(("moe", 0))
                act.wait_ge(S("gap_ready"), 1)
                go(gates[:, :, 1], gates[:, :, 0], ACT.Exp).then_inc(S("gap_exp"), 1)

                def evacuate(count):
                    act.wait_ge(S("gathered"), count * 2 + 1)
                    copy(xe[:, 0:4, :], bank[4][:, :].rearrange("p (f s) -> p f s", f=4)).then_inc(S("xe_low"), 1)
                    act.wait_ge(S("picks_full"), count + 1)
                    copy(pickT[:, :, :], bank[6][:, 0:NT * P].rearrange("p (i s) -> p i s", i=NT)).then_inc(S("picks_copied"), 1)

                evacuate(0)
                act.wait_ge(S("items_ready"), 1)
                nitems = act.value_load(items[0:1, 4 * NE:4 * NE + 1], min_val=NE, max_val=2 * NE - 1)
                with act.Fori(0, nitems) as n:
                    for q in range(NQ):
                        act.wait_ge(S("gate_full"), n * NQ + (q + 1))
                        go(hse[:, q % 2, :], bank[2 * (q % 2)][:, :], ACT.Silu).then_inc(S("gate_silu"), 1)
                    act.wait_ge(S("moe_down_used"), n * NQ + NQ)
                    copy(ye[:, 0:512], bank[6][:, :])
                    copy(ye[:, 512:D], bank[7][:, :]).then_inc(S("ye_copied"), 1)
                    evacuate(n + 1)
                norm_scale(NORMS - 1)

            mixer(0)
            dense()
            mixer(1)
            experts()

        @block.gpsimd
        def _(pool):
            pool.wait_ge(S("const_loaded"), 16)
            for l in range(DEPTH):
                for n, (name, tiles, r, dim) in enumerate(ROPES):
                    copied(pool, jobs[l, PROJECTED[name]])
                    if NR * l + n >= 2:
                        pool.wait_ge(S("rope_done"), NR * l + n - 1)
                    nc.gpsimd.tensor_tensor(rope_t2[0:r, n % 2, 0:tiles * T].rearrange("p (a t) -> p a t", a=tiles),
                                            raw[name][0:r, :, :], C(f"cos{dim}", r).unsqueeze(1).broadcast_to([r, tiles, T]),
                                            ALU.mult).then_inc(S("cos_half"), 1)

            link = chain(pool, S("pool_chain"))

            def mixer(m):
                J = lambda name: jobs["mix", m, name]
                pool.wait_ge(S("x_ready"), NT * (DEPTH + 2 * m))
                nc.gpsimd.memset(eps_col[:, :], RMS_EPS)
                nc.gpsimd.memset(hpad[:, :, 0:CONV_WIN - 1], 0.0)
                nc.gpsimd.memset(qkvpad[:, :, 0:SHORT - 1], 0.0).then_inc(S("pads_ready"), 1)
                f = 3
                copied(pool, J("vw"))
                copied(pool, J("c_val23"))
                acc = cacc[:, f, :]
                link(nc.gpsimd.tensor_scalar(acc, hpad[:, f, 0:T], cvec[:, 0, f:f + 1], cvec[:, 1, 48 + f:49 + f],
                                             ALU.mult, ALU.add))
                for t in range(1, CONV_WIN):
                    link(nc.gpsimd.tensor_scalar(ptap[:, t % 2, :], hpad[:, f, t:t + T], cvec[:, 0, 4 * t + f:4 * t + f + 1], None,
                                                 ALU.mult))
                    ins = nc.gpsimd.tensor_tensor(acc, acc, ptap[:, t % 2, :], ALU.add)
                    if t < CONV_WIN - 1:
                        link(ins)
                ins.then_inc(S("conv_pool"), 1)
                for s in range(1, LEVELS):
                    a = CONST_AT["levels"][0] + s * P
                    for i in range(NT):
                        copied(pool, J(f"LT{i}"))
                        if s > 1:
                            jy = J(f"Y{i}.{s - 1}")
                            pool.wait_ge(bank_full[jy.bank], jy.fill)
                        nc.gpsimd.tensor_tensor(NsT[:, i, :].rearrange("p (h c) -> p h c", h=DH),
                                                LT[:, i, :].rearrange("p (h c) -> p h c", h=DH),
                                                const2[:, a:a + P].unsqueeze(1).broadcast_to([P, DH, P]),
                                                ALU.mult).then_inc(S("level_ready"), 1)

            pool.wait_ge(S("const2_loaded"), 16)
            for m in range(DEPTH):
                mixer(m)

        @block.vector
        def _(dve):
            link = chain(dve, S("dve_chain"))
            tt, ts, stt = nc.vector.tensor_tensor, nc.vector.tensor_scalar, nc.vector.scalar_tensor_tensor

            def free(ins, j):
                ins.then_inc(bank_free[j.bank], 1)

            def rope(l, name):
                n = ROPE_AT[name]
                _, tiles, r, dim = ROPES[n]
                w = tiles * T
                j = jobs[l, f"rot_{name}"]
                b = filled(dve, j)
                free(tt(rope_t1[0:r, n % 2, 0:w].rearrange("p (a t) -> p a t", a=tiles),
                        b[0:r, 0:w].rearrange("p (a t) -> p a t", a=tiles),
                        C(f"sin{dim}", r).unsqueeze(1).broadcast_to([r, tiles, T]), ALU.mult), j)
                copied(dve, j)
                dve.wait_ge(S("cos_half"), NR * l + n + 1)
                t1, t2 = rope_t1[:, n % 2, 0:w], rope_t2[:, n % 2, 0:w]
                outs = [(rot[name][0:r, :, :], 0, r)]
                if name == "ik":
                    outs = [(rot[name][32 * q:32 * q + 32, :, :], 0, r) for q in range(4)]
                elif name == "dk":
                    outs = [(rot[name][HD * q:HD * q + HD, :, :], 0, r) for q in range(2)]
                elif name in ("ks", "kw"):
                    other = ksS if name == "ks" else kwS
                    outs += [(other[HD:P, :], 0, HD), (other[0:HD, :], HD, P)]
                for o, a, z in outs:
                    last = tt(o, t1[a:z], t2[a:z], ALU.add)
                last.then_inc(S("rope_done"), 1)

            def norm_stats(i, z):
                for c in range(2):
                    link(nc.vector.bn_stats(lnst[:, i, c, :], z[:, i, 512 * c:512 * c + 512]))
                link(nc.vector.bn_aggr(lnmv[:, i, 0:2], lnst[:, i, :, :]))
                ts(lnmv[:, i, 1:2], lnmv[:, i, 1:2], LN_EPS, None, ALU.add).then_inc(S("var_ready"), 1)

            def norm(q, i, z):
                dve.wait_ge(S("rstd_ready"), NT * q + i + 1)
                link(ts(x[:, i, :], z[:, i, :], lnmv[:, i, 0:1], lnmv[:, i, 3:4], ALU.subtract, ALU.mult))
                dve.wait_ge(S("norm_rows"), 32 * (q + 1))
                link(tt(x[:, i, :], x[:, i, :], lng[:, :], ALU.mult))
                tt(x[:, i, :], x[:, i, :], lnb[:, :], ALU.add).then_inc(S("x_ready"), 1)

            def residual(q, key, name, z):
                for i in range(NT):
                    for c in range(2):
                        j = jobs[(*key, f"{name}{i}{c}")]
                        b = filled(dve, j)
                        cs = slice(512 * c, 512 * c + 512)
                        free(stt(z[:, i, cs], x[:, i, cs], ALPHA, b[:, :], ALU.mult, ALU.add), j)
                        copied(dve, j)
                    norm_stats(i, z)
                for i in range(NT):
                    norm(q, i, z)

            dve.wait_ge(S("const_loaded"), 16)
            dve.wait_ge(S("vecs_T"), 1)
            nc.vector.tensor_copy(vecs[:, 0:40], bank[6][:, 0:40]).then_inc(S("vecs_ready"), 1)
            dve.wait_ge(S("vecs_ready"), 1)
            dve.wait_ge(S("pe_ready"), 2)
            dve.wait_ge(S("small_loaded"), 48)
            for l in range(DEPTH):
                j = jobs[l, "ada"]
                b = filled(dve, j)
                tt(adac[:, 0:8], b[:, 0:8], vec_bada(l)[:, 0:8], ALU.add)
                free(stt(adac[:, 8:16], b[:, 8:16], 1.0, vec_bada(l)[:, 8:16], ALU.add, ALU.add), j)
                copied(dve, j)
                for m in (0, 2):
                    j = jobs[l, f"xT{m}"]
                    b = filled(dve, j)
                    for k in (2 * m, 2 * m + 1):
                        last = ts(uT[:, k, :], b[:, (k % 2) * T:(k % 2 + 1) * T], adac[:, 8 + k:9 + k], adac[:, k:k + 1],
                                  ALU.mult, ALU.add)
                    free(last, j)
                rope(l, "iq")
                rope(l, "ik")
                j = jobs[l, "ff"]
                b = filled(dve, j)
                free(ts(ff[:, 0, :], b[0:FOX_HEADS, 0:T], b_f[:, l:l + 1], None, ALU.add), j)
                rope(l, "dq")
                rope(l, "dk")
                copied(dve, jobs[l, "ff"])
                dve.wait_ge(S("log1p_ready"), l + 1)
                link(stt(ff[:, 3, :], ff[:, 0, :], 0.0, ff[:, 1, :], ALU.min, ALU.subtract))
                nc.vector.tensor_tensor_scan(ff[:, 4, :], C("ones", FOX_HEADS)[:, 0:1].broadcast_to([FOX_HEADS, T]),
                                             ff[:, 3, :], 0.0, ALU.mult, ALU.subtract).then_inc(S("fox_ready"), 1)
                copied(dve, jobs[l, "ikw"])
                for n, (i, heads) in enumerate(ISCORES):
                    copied(dve, jobs[l, f"is{n}"])
                    keys = (i + 1) * P
                    for m, h in enumerate(heads):
                        r = relu[:, n % 2, m * keys:(m + 1) * keys]
                        acc = isc[:, i, 0:keys]
                        if h == 0:
                            ins = ts(acc, r, iw[:, i, h:h + 1], None, ALU.mult)
                        else:
                            ins = stt(acc, r, iw[:, i, h:h + 1], acc, ALU.mult, ALU.add)
                        if m < len(heads) - 1:
                            link(ins)
                    ins.then_inc(S("isc_steps"), 1)
                    dve.wait_ge(S("isc_steps"), NIS * l + n + 1)
                rope(l, "nq01")
                j = jobs[l, "kcvc"]
                b = filled(dve, j)
                for v in range(2):
                    for g in range(NSA_GROUPS):
                        rows_g = slice(HD * g, HD * g + HD)
                        taps = b[rows_g, v * T:(v + 1) * T].rearrange("p (c r) -> p r c", r=CMP_STRIDE)
                        for par in range(2):
                            for hi in range(2):
                                last = tt(blk[HD * par:HD * par + HD, v, 8 * hi:8 * hi + 8, g, :],
                                          taps[:, par:CMP_STRIDE:2, hi:hi + NCMP],
                                          pe_sb[rows_g, l, v, CMP_STRIDE * hi + par:CMP_STRIDE * (hi + 1):2]
                                          .unsqueeze(2).broadcast_to([HD, 8, NCMP]), ALU.add)
                free(last, j)
                rope(l, "nq2")
                rope(l, "ks")
                j = jobs[l, "ch"]
                b = filled(dve, j)
                dve.wait_ge(S("ch_exp"), l + 1)
                link(ts(ch[:, 1, :, :], ch[:, 0, :, :], 1.0, None, ALU.add))
                link(nc.vector.reciprocal(ch[:, 0, :, :], ch[:, 1, :, :]))
                free(tt(ch[:, 2, :, :], b[0:HD, 0:60].rearrange("p (v c) -> p v c", v=2), ch[:, 0, :, :], ALU.mult), j)
                copied(dve, j)
                nc.vector.tensor_copy(chrep[:, :, :, :], ch[:, 2, 1, :].rearrange("p (g c) -> p g c", g=2)
                                      .unsqueeze(2).broadcast_to([HD, NSA_GROUPS, NSA_HPG, NCMP])).then_inc(S("ch_ready"), 1)
                rope(l, "kw")
                copied(dve, jobs[l, "kwg"])
                link(ts(sgate[:, :, :], sgate[:, :, :], 1.0, None, ALU.add))
                link(nc.vector.reciprocal(sgate[:, :, :], sgate[:, :, :]))
                for i in range(NT):
                    keys = (i + 1) * P
                    link(tt(isc[:, i, keys - P:keys], isc[:, i, keys - P:keys], C("causal"), ALU.add))
                    cur, nxt = isc, isw
                    for k in range(TOPK // 8):
                        link(nc.vector.max(m8[:, i, :], cur[:, i, 0:keys]))
                        link(nc.vector.match_replace(nxt[:, i, 0:keys], m8[:, i, :], cur[:, i, 0:keys], TAKEN))
                        cur, nxt = nxt, cur
                    link(ts(isw[:, i, 0:keys], cur[:, i, 0:keys], TAKEN / 2, NEG, ALU.is_gt, ALU.mult))
                    tt(isw[:, i, keys - P:keys], isw[:, i, keys - P:keys], C("causal"), ALU.add).then_inc(S("sel_ready"), 1)
                j = jobs[l, "ckv"]
                b = filled(dve, j)
                dve.wait_ge(bank_free[j.bank], j.free_before + 1)
                free(tt(vblk[:, :, :], b[0:NHC, HD:2 * HD].unsqueeze(1).broadcast_to([NHC, NSA_HEADS, HD]),
                        C("cmp_block", NHC).rearrange("p (h d) -> p h d", h=NSA_HEADS), ALU.mult), j)
                dve.wait_ge(S("gate_bias"), 16 * (l + 1))
                for c in range(2):
                    j = jobs[l, f"gb{c}"]
                    b = filled(dve, j)
                    gc = gate1p[:, 512 * c:512 * c + 512]
                    free(stt(gc, b[:, :], 1.0, gc, ALU.add, ALU.add), j)

                def row_max(n):
                    kind, i, heads, keys = GROUPS[n]
                    j = jobs[l, f"S{n}"]
                    b = filled(dve, j)
                    nh = len(heads)
                    nmax = stat[:, n % 4, 0, 0:nh]
                    view = b[:, 0:nh * keys].rearrange("p (h s) -> p h s", h=nh)
                    ins = nc.vector.tensor_reduce(nmax, view, AX, ALU.max, negate=True)
                    ins.then_inc(S("max_ready"), 1)
                    if kind == "cmp":
                        dve.wait_ge(S("max_ready"), NG * l + n + 1)
                        free(tt(cmp_s[:, i, :, :], view, nmax.unsqueeze(2).broadcast_to([P, nh, keys]), ALU.add), j)

                def copy_pT(n):
                    kind, i, heads, keys = GROUPS[n]
                    j = jobs[l, f"T{n}"]
                    b = filled(dve, j)
                    if kind == "cmp":
                        dve.wait_ge(S("cmp_p_ready"), NT * l + i + 1)
                        link(nc.vector.tensor_reduce(stat[:, n % 4, 1, 0:NSA_HEADS],
                                                     p_sb[:, n % 2, 0:NHC].rearrange("p (h c) -> p h c", h=NSA_HEADS), AX, ALU.add))
                        free(nc.vector.tensor_copy(pT[0:NHC, n % 2, 0:P], b[0:NHC, 0:P]), j)
                    else:
                        w = len(heads) * keys
                        free(nc.vector.tensor_copy(pT[:, n % 2, 0:w], b[:, 0:w]), j)

                def mixed(n):
                    kind, i, heads, keys = GROUPS[n]
                    j = jobs[l, f"O{n}"]
                    nh = len(heads)
                    rinv, cf = stat[:, n % 4, 2, 0:nh], stat[:, n % 4, 3, 0:nh]
                    if kind in ("dsa", "fox"):
                        link(nc.vector.reciprocal(cf, stat[:, n % 4, 1, 0:nh]))
                    else:
                        link(nc.vector.reciprocal(rinv, stat[:, n % 4, 1, 0:nh]))
                        g0 = GATE_OF[kind] * NSA_HEADS + heads[0]
                        g = sgate[:, i, g0:g0 + nh]
                        if kind == "cmp":
                            v0 = CONST_AT["cmp_valid"][0] + i
                            link(stt(cf, rinv, const[:, v0:v0 + 1], g, ALU.mult, ALU.mult))
                        else:
                            link(tt(cf, rinv, g, ALU.mult))
                    b = filled(dve, j)
                    o = b[:, 0:nh * HD].rearrange("p (h d) -> p h d", h=nh)
                    c0 = MIX_COL[kind] + heads[0] * HD
                    dst = mix[:, i, c0:c0 + nh * HD]
                    by = cf.unsqueeze(2).broadcast_to([P, nh, HD])
                    if kind in ("win", "slc"):
                        tmp = otmp[:, 0:nh * HD]
                        free(tt(tmp.rearrange("p (h d) -> p h d", h=nh), o, by, ALU.mult), j)
                        copied(dve, j)
                        link(tt(dst, dst, tmp, ALU.add))
                    else:
                        free(tt(dst.rearrange("p (h d) -> p h d", h=nh), o, by, ALU.mult), j)
                        copied(dve, j)

                for n in range(NG + 2):
                    if n < NG:
                        row_max(n)
                    if 1 <= n <= NG:
                        copy_pT(n - 1)
                    if n >= 2:
                        mixed(n - 2)
                for c in range(2):
                    for i in range(NT):
                        copied(dve, jobs[l, f"gt{c}{i}"])
                for i in range(NT):
                    tt(mix[:, i, :], mix[:, i, :], sg[:, i, :], ALU.mult).then_inc(S("mix_ready"), 1)
                for i in range(NT):
                    for c in range(2):
                        j = jobs[l, f"wo{i}{c}"]
                        b = filled(dve, j)
                        cs = slice(512 * c, 512 * c + 512)
                        free(tt(mix[:, i, cs], b[:, :], gate1p[:, cs], ALU.mult), j)
                        copied(dve, j)
                        link(stt(mix[:, i, cs], x[:, i, cs], ALPHA, mix[:, i, cs], ALU.mult, ALU.add))
                    norm_stats(i, mix)
                for i in range(NT):
                    norm(l, i, mix)

            def copy_xT(key):
                for m in (0, 2):
                    j = jobs[(*key, f"xT{m}")]
                    b = filled(dve, j)
                    free(nc.vector.tensor_copy(uT[:, 2 * m:2 * m + 2, :], b[:, :].rearrange("p (k t) -> p k t", k=2)), j)

            dve.wait_ge(S("const2_loaded"), 16)

            def mixer(m):
                q = DEPTH + 2 * m
                J = lambda name: jobs["mix", m, name]
                hs_ = lambda h: slice(h * P, (h + 1) * P)
                by_head = lambda a: a.rearrange("p (h d) -> p h d", h=DH)
                per_head = lambda a: a.unsqueeze(2).broadcast_to([P, DH, P])
                all_heads = lambda a: a.unsqueeze(1).broadcast_to([P, DH, P])
                j = J("vw")
                b = filled(dve, j)
                nc.vector.tensor_copy(cvec[:, 0, 0:CONV_WIN * 4], b[:, 0:CONV_WIN * 4])
                free(nc.vector.tensor_copy(cvec[:, 1, 0:60], b[:, P:P + 60]), j)
                copy_xT(("mix", m))
                dve.wait_ge(S("mix_small"), 16 * MIX_SMALL * (m + 1))
                j = J("ba")
                b = filled(dve, j)
                free(nc.vector.tensor_copy(sm["logit"][:, :, :], b[:, 0:16].rearrange("p (i n) -> p i n", i=NT)), j)
                copied(dve, j)
                tt(sm["z"][:, :, 0:DH], sm["logit"][:, :, DH:2 * DH], decay_in[:, 1, :].unsqueeze(1).broadcast_to([P, NT, DH]),
                   ALU.add).then_inc(S("dt_ready"), 1)
                copied(dve, J("vw"))
                for n, name in enumerate(QKV):
                    for half in range(2):
                        copied(dve, J(f"{name}{2 * half}{2 * half + 1}"))
                        for t in range(SHORT):
                            for f in range(4 * n + 2 * half, 4 * n + 2 * half + 2):
                                w = 12 * t + QKV_CHUNK[name] + f - 4 * n
                                src, tap = qkvpad[:, f, t:t + T], cvec[:, 1, w:w + 1]
                                if t == 0:
                                    ins = ts(qkv[:, f, :], src, tap, None, ALU.mult)
                                else:
                                    ins = stt(qkv[:, f, :], src, tap, qkv[:, f, :], ALU.mult, ALU.add)
                            if t < SHORT - 1:
                                link(ins)
                        ins.then_inc(S("short_done"), 1)
                dve.wait_ge(S("soft_ready"), m + 1)
                link(ts(sm["eb"][:, :, 0:DH], sm["eb"][:, :, 0:DH], 1.0, None, ALU.add))
                link(nc.vector.reciprocal(sm["beta"][:, :, 0:DH], sm["eb"][:, :, 0:DH]))
                link(stt(sm["soft"][:, :, 0:DH], sm["z"][:, :, 0:DH], 0.0, sm["zl"][:, :, 0:DH], ALU.max, ALU.add))
                tt(sm["g"][:, :, 0:DH], sm["soft"][:, :, 0:DH], sm["ea"][:, 0:1, 0:DH].broadcast_to([P, NT, DH]), ALU.mult)\
                    .then_inc(S("g_ready"), 1)
                for half in range(2):
                    copied(dve, J(f"c_gate{2 * half}{2 * half + 1}"))
                    j = J(f"c_val{2 * half}{2 * half + 1}")
                    b = filled(dve, j)
                    free(tt(hpad[:, 2 * half:2 * half + 2, CONV_WIN - 1:], b[:, :].rearrange("p (f t) -> p f t", f=2),
                            sig[:, 2 * half:2 * half + 2, :], ALU.mult), j)
                copied(dve, J("c_val01"))
                copied(dve, J("c_val23"))
                dve.wait_ge(S("pads_ready"), m + 1)
                tap = [0]

                def taps(n):
                    for t in range(tap[0], min(tap[0] + n, CONV_WIN)):
                        for f in range(3):
                            src, w = hpad[:, f, t:t + T], cvec[:, 0, 4 * t + f:4 * t + f + 1]
                            if t == 0:
                                ins = ts(cacc[:, f, :], src, w, cvec[:, 1, 48 + f:49 + f], ALU.mult, ALU.add)
                            else:
                                ins = stt(cacc[:, f, :], src, w, cacc[:, f, :], ALU.mult, ALU.add)
                        if t < CONV_WIN - 1:
                            link(ins)
                        else:
                            ins.then_inc(S("conv_dve"), 1)
                    tap[0] += n

                taps(8)
                j = J("gc")
                b = filled(dve, j)
                link(ts(sm["ncum"][:, :, 0:DH], b[:, 0:8].rearrange("p (i h) -> p i h", i=NT), -1.0, None, ALU.mult))
                free(tt(sm["rest"][:, 0, 0:DH], b[:, 8:12], sm["ncum"][:, 0, 0:DH], ALU.add), j)
                j = J("ss")
                free(ts(sm["ss"][:, :, :], filled(dve, j)[:, 0:16].rearrange("p (i n) -> p i n", i=NT), L2_EPS, None, ALU.add), j)
                dve.wait_ge(S("rnorm_ready"), m + 1)
                for i in range(NT):
                    j = J(f"kt{i}")
                    b = filled(dve, j)
                    free(tt(by_head(ktok[:, i, :]), by_head(b[:, :]), per_head(sm["rnorm"][:, i, 0:DH]), ALU.mult), j)
                link(ts(sm["rq"][:, :, 0:DH], sm["rnorm"][:, :, DH:], DK ** -0.5, None, ALU.mult))
                for i in range(NT):
                    j = J(f"vt{i}")
                    b = filled(dve, j)
                    free(tt(by_head(vb[:, i, :]), by_head(b[:, :]), per_head(sm["beta"][:, i, 0:DH]), ALU.mult), j)
                dve.wait_ge(S("coef_ready"), m + 1)
                copied(dve, J("kt0"))
                tt(by_head(kdec[:, :]), by_head(ktok[:, 0, :]), per_head(sm["coef"][:, 0, 0:DH]), ALU.mult)\
                    .then_inc(S("kdec_ready"), 1)
                link(stt(sm["nbe"][:, 1, 0:DH], sm["beta"][:, 1, 0:DH], -1.0, sm["coef"][:, 1, 0:DH], ALU.mult, ALU.mult))
                for i in range(NT):
                    copied(dve, J(f"dm{i}"))
                    j = J(f"A{i}")
                    b = filled(dve, j)
                    for h in range(DH):
                        last = stt(Lw[:, i, hs_(h)], b[:, hs_(h)], sm["beta"][:, i, h:h + 1], decay[:, i, hs_(h)], ALU.mult, ALU.mult)
                    free(last, j)
                for i in range(NT):
                    j = J(f"at{i}")
                    b = filled(dve, j)
                    free(tt(attn[:, i, :], b[:, :], decay[:, i, :], ALU.mult), j)
                lv = CONST_AT["levels"][0]
                for i in range(NT):
                    copied(dve, J(f"A{i}"))
                    link(tt(by_head(X[:, i, :]), by_head(Lw[:, i, :]), all_heads(C("level0")), ALU.mult))
                    link(tt(by_head(X[:, i, :]), by_head(X[:, i, :]), all_heads(C("ident")), ALU.add))
                    copied(dve, J(f"LT{i}"))
                    link(tt(by_head(XT[:, i, :]), by_head(LT[:, i, :]), all_heads(const2[:, lv:lv + P]), ALU.mult))
                    tt(by_head(XT[:, i, :]), by_head(XT[:, i, :]), all_heads(C("ident")), ALU.add).then_inc(S("x_first"), 1)
                dve.wait_ge(S("x_first"), NT * (m + 1))
                for s in range(1, LEVELS):
                    taps(4)
                    for i in range(NT):
                        for name, dst in (("D", X), ("E", XT)):
                            if s < LEVELS - 1 or name == "E":
                                j = J(f"{name}{i}.{s}")
                                b = filled(dve, j)
                                if s > 1:
                                    copied(dve, J(f"{name}{i}.{s - 1}"))
                                free(tt(dst[:, i, :], dst[:, i, :], b[:, :], ALU.add), j)
                for i in range(NT):
                    b = filled(dve, J(f"ct{i}"))
                    link(nc.vector.bn_stats(cstat[:, i, :], b[:, :]))
                    link(nc.vector.bn_aggr(cmv[:, i, 0:2], cstat[:, i, :]))
                    ts(cmv[:, i, 1:2], cmv[:, i, 1:2], LN_EPS, None, ALU.add).then_inc(S("cvar_ready"), 1)
                for i in range(NT):
                    dve.wait_ge(S("crstd_ready"), NT * m + i + 1)
                    j = J(f"ct{i}")
                    b = filled(dve, j)
                    free(ts(cn[:, i, :], b[:, :], cmv[:, i, 0:1], cmv[:, i, 3:4], ALU.subtract, ALU.mult), j)
                j = J("kS")
                b = filled(dve, j)
                copied(dve, J("vt1"))
                for h in range(DH):
                    last = stt(vb[:, 1, hs_(h)], b[:, hs_(h)], sm["nbe"][:, 1, h:h + 1], vb[:, 1, hs_(h)], ALU.mult, ALU.add)
                free(last, j)
                j = J("o0")
                b = filled(dve, j)
                free(tt(by_head(o[:, 0, :]), by_head(b[:, :]), per_head(sm["rq"][:, 0, 0:DH]), ALU.mult), j)
                j = J("o1")
                b = filled(dve, j)
                copied(dve, J("qS"))
                free(tt(o[:, 1, :], b[:, :], oi[:, :], ALU.add), j)
                copied(dve, j)
                tt(by_head(o[:, 1, :]), by_head(o[:, 1, :]), per_head(sm["rq"][:, 1, 0:DH]), ALU.mult)\
                    .then_inc(S("o1_ready"), 1)
                for i in range(NT):
                    if i == 0:
                        copied(dve, J("o0"))
                    else:
                        dve.wait_ge(S("o1_ready"), m + 1)
                    dve.wait_ge(S("orstd_ready"), NT * m + i + 1)
                    copied(dve, J(f"z{i}"))
                    link(tt(by_head(o[:, i, :]), by_head(o[:, i, :]), per_head(sm["orstd"][:, i, 0:DH]), ALU.mult))
                    link(tt(by_head(o[:, i, :]), by_head(o[:, i, :]), all_heads(ong[:, :]), ALU.mult))
                    tt(o[:, i, :], o[:, i, :], sz[:, i, :], ALU.mult).then_inc(S("delta_ready"), 1)
                residual(q, ("mix", m), "wo", z2)

            def dense():
                J = lambda name: jobs["ffn", 0, name]
                copy_xT(("ffn", 0))
                for n in range(NFF):
                    copied(dve, J(f"g{n}"))
                    j = J(f"u{n}")
                    b = filled(dve, j)
                    free(tt(hT[:, 2 * n:2 * n + 2, :], b[:, :].rearrange("p (f t) -> p f t", f=2),
                            hs[:, n % 2, :].rearrange("p (f t) -> p f t", f=2), ALU.mult), j)
                residual(DEPTH + 1, ("ffn", 0), "d", z3)

            def experts():
                copy_xT(("moe", 0))
                j = jobs["moe", 0, "logits"]
                b = filled(dve, j)
                free(nc.vector.tensor_copy(logits[:, :, :], b[:, 0:NT * NE].rearrange("p (i e) -> p i e", i=NT)), j)
                copied(dve, j)
                for i in range(NT):
                    link(nc.vector.max(out=best[:, i, :], in_=logits[:, i, :]))
                    link(nc.vector.max_index(out=best_at[:, i, :], in_max=best[:, i, :], in_values=logits[:, i, :]))
                link(nc.vector.tensor_copy(best_f[:, :, :], best_at[:, :, :]))
                for i in range(NT):
                    for n in range(2):
                        last = ts(hot[:, n, i, :], C("iota")[:, 0:NE], best_f[:, i, n:n + 1], None, ALU.is_equal)
                link(last)
                tt(chosen[:, :, :], hot[:, 0, :, :], hot[:, 1, :, :], ALU.add).then_inc(S("chosen_ready"), 1)
                tt(gates[:, :, 0], best[:, :, 1], best[:, :, 0], ALU.subtract).then_inc(S("gap_ready"), 1)
                dve.wait_ge(S("gap_exp"), 1)
                link(ts(gates[:, :, 3], gates[:, :, 1], 1.0, None, ALU.add))
                link(nc.vector.reciprocal(gates[:, :, 2], gates[:, :, 3]))
                link(tt(gates[:, :, 3], gates[:, :, 1], gates[:, :, 2], ALU.mult))
                for i in range(NT):
                    link(ts(comb[:, i, 0:NE], hot[:, 0, i, :], gates[:, i, 2:3], None, ALU.mult))
                    link(stt(comb[:, i, 0:NE], hot[:, 1, i, :], gates[:, i, 3:4], comb[:, i, 0:NE], ALU.mult, ALU.add))
                link(nc.vector.tensor_copy(comb[:, :, NE:], comb[:, :, 0:NE]))
                dve.wait_ge(S("chosen_ready"), 1)
                link(ts(places[:, :, 0:NE], chosen[:, :, :], FAR, -FAR, ALU.mult, ALU.add))
                j = jobs["moe", 0, "places"]
                b = filled(dve, j)
                link(tt(places[:, :, 0:NE], places[:, :, 0:NE], b[:, 0:NT * NE].rearrange("p (i e) -> p i e", i=NT), ALU.add))
                link(ts(places[:, :, NE:], places[:, :, 0:NE], -float(P), None, ALU.add))
                free(nc.vector.tensor_copy(long[:, 0, :], b[:, NT * NE:NT * NE + NE]), j)
                copied(dve, j)
                link(ts(long[:, 1, :], long[:, 0, :], float(P), None, ALU.is_gt))
                link(tt(long[:, 2, :], long[:, 1, :], C("iota")[:, NE:2 * NE], ALU.mult))
                link(nc.vector.max(out=long[:, 3, :], in_=long[:, 2, :]))
                link(nc.vector.tensor_reduce(out=item_f[:, 4 * NE:4 * NE + 1], in_=long[:, 1, :], axis=AX, op=ALU.add))
                link(ts(item_f[:, 4 * NE:4 * NE + 1], item_f[:, 4 * NE:4 * NE + 1], float(NE), None, ALU.add))
                nc.vector.tensor_copy(item_f[:, 0:NE], C("iota")[:, 0:NE])
                nc.vector.tensor_copy(item_f[:, NE:2 * NE], long[:, 3, :])
                nc.vector.tensor_copy(item_f[:, 2 * NE:3 * NE], C("iota")[:, 0:NE])
                link(ts(item_f[:, 3 * NE:4 * NE], long[:, 3, :], float(NE), 0.0, ALU.subtract, ALU.max))
                nc.vector.tensor_copy(items[:, :], item_f[:, :]).then_inc(S("items_ready"), 1)
                dve.wait_ge(S("items_ready"), 1)

                def pick_tokens(n):
                    c = dve.value_load(items[0:1, bass.ds(n, 1)], min_val=0, max_val=2 * NE - 1)
                    for i in range(NT):
                        ts(pick[:, i, :], C("iota"), places[:, i, bass.ds(c, 1)], None, ALU.is_equal)
                        last = ts(pickc[:, i, :], C("iota"), places[:, i, bass.ds(c, 1)], comb[:, i, bass.ds(c, 1)],
                                  ALU.is_equal, ALU.mult)
                    last.then_inc(S("picked"), 1)

                def evacuate(count):
                    dve.wait_ge(S("gathered"), count * 2 + 2)
                    nc.vector.tensor_copy(xe[:, 4:8, :], bank[5][:, :].rearrange("p (f s) -> p f s", f=4)).then_inc(S("xe_high"), 1)

                pick_tokens(0)
                for i in range(NT):
                    for c in range(2):
                        cs = slice(512 * c, 512 * c + 512)
                        ts(total[:, i, cs], x[:, i, cs], ALPHA, None, ALU.mult).then_inc(S("acc_added"), 1)
                evacuate(0)
                dve.wait_ge(S("picks_full"), 1)
                pick_tokens(1)
                nitems = dve.value_load(items[0:1, 4 * NE:4 * NE + 1], min_val=NE, max_val=2 * NE - 1)
                with dve.Fori(0, nitems) as n:
                    for q in range(NQ):
                        dve.wait_ge(S("gate_silu"), n * NQ + (q + 1))
                        dve.wait_ge(S("up_full"), n * NQ + (q + 1))
                        tt(he[:, 4 * q:4 * q + 4, :], bank[2 * (q % 2) + 1][:, :].rearrange("p (f s) -> p f s", f=4),
                           hse[:, q % 2, :].rearrange("p (f s) -> p f s", f=4), ALU.mult).then_inc(S("hidden_ready"), 1)
                    evacuate(n + 1)
                    for i in range(NT):
                        for c in range(2):
                            b, cs = 2 * i + c, slice(512 * c, 512 * c + 512)
                            dve.wait_ge(S("scattered"), n * 4 + (b + 1))
                            dve.wait_ge(S("acc_added"), n * 4 + (b + 1))
                            tt(total[:, i, cs], total[:, i, cs], bank[b][:, :], ALU.add).then_inc(S("acc_added"), 1)
                    dve.wait_ge(S("picks_full"), n + 2)
                    pick_tokens(n + 2)
                dve.wait_ge(S("acc_added"), nitems * 4 + 4)
                for i in range(NT):
                    norm_stats(i, total)
                for i in range(NT):
                    norm(NORMS - 1, i, total)

            mixer(0)
            dense()
            mixer(1)
            experts()


def kernel(**inputs):
    import numpy as _np
    import concourse.bacc as _bacc
    from concourse import mybir as _mybir
    from concourse.bass_utils import run_bass_kernel_spmd as _run

    nc = _bacc.Bacc("TRN2", target_bir_lowering=False, num_devices=1)
    arrays, A = {}, {}
    for name in _INS:
        a = _np.ascontiguousarray(inputs[name])
        arrays[f"in_{name}_dram"] = a
        A[name] = nc.dram_tensor(f"in_{name}_dram", a.shape, _mybir.dt.from_np(a.dtype), kind="ExternalInput").ap()
    for name, a in (("const", _CONST), ("const2", _CONST2)):
        arrays[f"in_{name}_dram"] = a
        A[name] = nc.dram_tensor(f"in_{name}_dram", a.shape, _mybir.dt.float32, kind="ExternalInput").ap()
    out = nc.dram_tensor("out_0_dram", (1, T, D), _mybir.dt.float32, kind="ExternalOutput").ap()
    build(nc, A, out)
    r = _run(nc, [arrays], core_ids=[0])
    return r.results[0]["out_0_dram"]

_INS = ["x", "c", "w_ada", "b_ada", "w_in", "b_f", "cmp_pe", "cmp_w1", "cmp_w2", "w_out", "ln_g", "ln_b",
        "w_in_2", "conv_dw_w_2", "conv_dw_b_2", "conv_ln_g_2", "conv_ln_b_2", "short_conv_w_2", "a_log_2", "dt_bias_2",
        "out_norm_g_2", "w_out_2", "ln_mix_g_2", "ln_mix_b_2", "ffn_w_gate_2", "ffn_w_up_2", "ffn_w_down_2",
        "router_w_2", "moe_w_gate_2", "moe_w_up_2", "moe_w_down_2", "ln_ffn_g_2", "ln_ffn_b_2"]
```

```python
import math
from contextlib import ExitStack

import numpy as np
import concourse.bass as bass
from concourse import mybir

P = 128
D = 1024
T = 256
NT = T // P
KD = D // P
DEPTH = 2
HD = 64
DSA_HEADS, FOX_HEADS, NSA_HEADS, NSA_GROUPS = 4, 6, 6, 2
NSA_HPG = NSA_HEADS // NSA_GROUPS
IDX_HEADS, IDX_DIM = 8, 32
TOPK = min(256, T // 4)
CMP_LEN, CMP_STRIDE = 32, 16
NCMP = (T - CMP_LEN) // CMP_STRIDE + 1
NHC = NSA_HEADS * NCMP
ALPHA = (2.0 * DEPTH) ** 0.25
LN_EPS = 1e-5
RMS_EPS = 1e-6
L2_EPS = 1e-6
NEG = -1e30
TAKEN = -3e38
ROPE_THETA = 10000.0

_names = [("dsa_q", 256), ("dsa_k", 64), ("dsa_v", 64), ("idx_q", 256), ("idx_k", 32), ("idx_w", 8),
          ("fox_q", 384), ("fox_k", 384), ("fox_v", 384), ("fox_f", 6), ("nsa_q", 384),
          ("nsa_kc", 128), ("nsa_vc", 128), ("nsa_ks", 128), ("nsa_vs", 128), ("nsa_kw", 128),
          ("nsa_vw", 128), ("nsa_g", 18), ("gate", 1024)]
COL = {}
_at = 0
for _n, _w in _names:
    COL[_n] = (_at, _at + _w)
    _at += _w

W_IN_PARTS = [("idx_q", "idx_w"), ("dsa_q", "dsa_v"), ("fox_v", "fox_f"), ("fox_q", "fox_q"), ("fox_k", "fox_k"),
              ("nsa_q", "nsa_q"), ("nsa_kc", "nsa_ks"), ("nsa_vs", "nsa_g")]
PART_OF = {}
for _a, _b in W_IN_PARTS:
    for _n, _ in _names:
        if COL[_a][0] <= COL[_n][0] < COL[_b][1]:
            PART_OF[_n] = _a

CW = 512
CONV_WIN = 31
SHORT = 4
DH = 4
DK = 128
D_FF = 2816
KF = D_FF // P
NE = 8
D_FE = 3584
KE = D_FE // P

RING = 5
SLOT = KD * 512
FE_PART = 512
NQ = D_FE // FE_PART
PIECE = SLOT // 2
NPIECE_UP = 4 * NQ
NPIECE = NPIECE_UP + D_FE // 256
MOE_RING = 7
FAR = 1e4


def constants():
    r = np.arange(P)
    row, col = r[:, None], r[None, :]
    parts, later = {}, {}
    parts["ident"] = (row == col).astype(np.float32)
    parts["causal"] = np.where(col <= row, 0.0, NEG).astype(np.float32)
    later["tri_le"] = (row <= col).astype(np.float32)
    later["tri_lt"] = (row < col).astype(np.float32)
    parts["ones"] = np.ones((P, P), np.float32)
    for dim in (HD, IDX_DIM):
        half = dim // 2
        inv = np.float32(ROPE_THETA) ** (-np.arange(half, dtype=np.float32) / np.float32(half))
        ang = np.arange(T, dtype=np.float32)[None, :] * inv.astype(np.float32)[r % half][:, None]
        parts[f"cos{dim}"] = np.cos(ang).astype(np.float32)
        parts[f"sin{dim}"] = np.sin(ang).astype(np.float32)
        rot = np.zeros((P, P), np.float32)
        for m in range(P):
            if m % dim < half:
                rot[m + half, m] = -1.0
            else:
                rot[m - half, m] = 1.0
        parts[f"rot{dim}"] = rot
    cend = np.arange(NCMP) * CMP_STRIDE + CMP_LEN - 1
    cm = np.zeros((P, NT, NSA_HEADS, NCMP), np.float32)
    valid = np.zeros((P, NT), np.float32)
    for i in range(NT):
        t = i * P + r
        cm[:, i] = np.where(cend[None, :] <= t[:, None], 0.0, NEG)[:, None, :]
        valid[:, i] = t >= cend[0]
    parts["cmp_mask"] = cm.reshape(P, -1)
    parts["cmp_valid"] = valid
    blk = np.zeros((P, NSA_HEADS, HD), np.float32)
    for h in range(NSA_HEADS):
        blk[h * NCMP:(h + 1) * NCMP, h] = 1.0
    parts["cmp_block"] = blk.reshape(P, -1)
    later["iota"] = np.broadcast_to(r[None, :], (P, P)).astype(np.float32)
    lv = np.zeros((P, 7, P), np.float32)
    for s in range(7):
        b = 1 << s
        lv[:, s] = -1.0 * ((col // (2 * b) == row // (2 * b)) & ((col // b) % 2 == 1) & ((row // b) % 2 == 0))
    later["levels"] = lv.reshape(P, -1)
    later["level0"] = lv[:, 0].T.copy()
    at = {}
    for group in (parts, later):
        n = 0
        for k, v in group.items():
            at[k] = (n, n + v.shape[1])
            n += v.shape[1]
    return at, *(np.concatenate(list(g.values()), 1).astype(np.float32) for g in (parts, later))


CONST_AT, _CONST, _CONST2 = constants()
NCONST, NCONST2 = _CONST.shape[1], _CONST2.shape[1]


CONST2 = ("tri_le", "tri_lt", "iota", "levels", "level0")
NORMS = 6


class Job:

    def __init__(self, bank, fill, free_before, free_after):
        self.bank, self.fill, self.free_before, self.free_after = bank, fill, free_before, free_after


class Jobs:

    def __init__(self):
        self.fills, self.frees, self.of = [0] * 8, [0] * 8, {}

    def add(self, name, bank, frees=1):
        self.fills[bank] += 1
        before = self.frees[bank]
        self.frees[bank] += frees
        self.of[name] = Job(bank, self.fills[bank], before, self.frees[bank])

    def __getitem__(self, name):
        return self.of[name]


def attention_groups():
    out = []
    for kind in ("fox", "cmp", "win", "slc", "dsa"):
        if kind == "cmp":
            out += [(kind, i, list(range(NSA_HEADS)), NCMP) for i in range(NT)]
        elif kind == "dsa":
            out += [(kind, 0, [0, 1, 2, 3], P), (kind, 1, [0, 1], T), (kind, 1, [2, 3], T)]
        else:
            out += [(kind, 0, [0, 1, 2], P), (kind, 0, [3, 4, 5], P)]
            out += [(kind, 1, [h, h + 1], T) for h in range(0, 6, 2)]
    return out


GROUPS = attention_groups()
NG = len(GROUPS)
GATE_AT = {7: 0, 9: 1}
NEXT_AT = {14: 0, 16: 1, 18: 2, 21: 3}
GATE_BY, NEXT_FROM, NEXT_BY = 7, 4, 16
MIX_COL = {"dsa": 0, "fox": 256, "cmp": 640, "win": 640, "slc": 640}
GATE_OF = {"cmp": 0, "slc": 1, "win": 2}
ROPES = [("iq", 2, P, IDX_DIM), ("ik", 1, IDX_DIM, IDX_DIM), ("dq", 2, P, HD), ("dk", 1, HD, HD),
         ("nq01", 2, P, HD), ("nq2", 1, P, HD), ("ks", 1, P, HD), ("kw", 1, P, HD)]
PROJECTED = {"iq": "iq", "ik": "ikw", "dq": "dq", "dk": "dkv", "nq01": "nq01", "nq2": "nq2", "ks": "ks", "kw": "kwg"}
ROPE_AT = {r[0]: n for n, r in enumerate(ROPES)}
NR = len(ROPES)
ISCORES = [(i, [q, q + 4]) for i in range(NT) for q in range(4)]
NIS = len(ISCORES)


def plan_first(jobs, l):
    def add(name, bank, frees=1):
        jobs.add((l, name), bank, frees)
    if l == 0:
        for q in range(4):
            add(f"ada{q}", [7, 4, 5, 6][q])
    for m in range(4):
        add(f"xT{m}", m)
    add("iq", 4); add("ikw", 5); add("dq", 6)
    add("rot_iq", 0); add("dkv", 7); add("rot_ik", 1)
    add("fv0", 2); add("fv1", 3); add("ff", 4)
    add("rot_dq", 5); add("rot_dk", 6)
    for n in range(len(ISCORES)):
        add(f"is{n}", [7, 0, 1][n % 3])
    add("fq01", 2); add("fq2", 3); add("fk01", 4); add("fk2", 5)
    add("nq01", 6); add("nq2", 2); add("kcvc", 3)
    add("rot_nq01", 4); add("ks", 5); add("rot_nq2", 6)
    add("vsw", 2); add("kwg", 7); add("rot_ks", 4); add("ch", 3); add("rot_kw", 5)
    for c in range(2):
        for i in range(NT):
            add(f"gt{c}{i}", [6, 2][i])
    add("ckv", 3, 2)
    for k in range(NG + 2):
        if k < NG:
            add(f"S{k}", [0, 1, 7][k % 3])
        if 1 <= k <= NG:
            add(f"T{k - 1}", [2, 3][(k - 1) % 2])
        if k >= 2:
            add(f"O{k - 2}", [4, 5][(k - 2) % 2])
        if k in GATE_AT:
            add(f"gb{GATE_AT[k]}", 6)
        if l + 1 < DEPTH and k in NEXT_AT:
            jobs.add((l + 1, f"ada{NEXT_AT[k]}"), 6)
    for i in range(NT):
        for half in range(2):
            add(f"yT{i}{half}", [0, 1, 2, 3][2 * i + half])
    for i in range(NT):
        for c in range(2):
            add(f"wo{i}{c}", [4, 5, 6, 7][2 * i + c])


LAST_USE = {"ada0": "ada0", "ada1": "ada1", "ada2": "ada2", "ada3": "ada3", "ada4": "gb0", "ada5": "gb1",
            "idx_q": "ikw", "dsa_q": "dkv", "fox_v": "ff", "fox_q": "fq2", "fox_k": "fk2", "nsa_q": "nq2",
            "nsa_kc": "ks", "nsa_vs": "kwg", "cmp_w1": "ch", "gate0": "gt01", "gate1": "gt11",
            "wout0": "wo10", "wout1": "wo11"}


W_IN2 = [("c_gate", 512), ("c_val", 0), ("k", 1536), ("q", 1024), ("v", 2048), ("z", 2560)]
LOGITS2 = 3072
MIX_SMALL = 9
QKV = ["k", "q", "v"]
QKV_CHUNK = {"q": 0, "k": DH, "v": 2 * DH}
LEVELS = 7
FF_PART = 256
NFF = D_FF // FF_PART
NDOWN = -(-KF // 4)


def plan_mixer(jobs, m):
    def add(name, bank, frees=1):
        jobs.add(("mix", m, name), bank, frees)
    for n in range(4):
        add(f"xT{n}", n)
    add("c_gate01", 4); add("c_gate23", 5); add("c_val01", 6); add("c_val23", 7)
    add("vw", 0); add("ba", 1)
    for n, name in enumerate(("k01", "k23", "q01", "q23", "v01", "v23")):
        add(name, n + 2)
    add("z0", 0); add("z1", 1)
    add("gc", 2); add("dm0", 3); add("dm1", 4)
    add("kt0", 6); add("kt1", 7); add("vt0", 0); add("vt1", 1)
    add("ss", 5)
    add("kn0", 2); add("kn1", 5)
    add("A0", 6); add("A1", 7); add("at0", 3); add("at1", 4)
    add("LT0", 0); add("LT1", 1); add("aT0", 2); add("aT1", 5)
    add("ct0", 2); add("ct1", 5)
    for s in range(1, LEVELS):
        if s == 3:
            add("cb0", 2); add("cb1", 5)
        for name, b in (("Y0", 6), ("Y1", 7), ("D0", 0), ("E0", 3), ("D1", 1), ("E1", 4)):
            if s < LEVELS - 1 or name[0] != "D":
                add(f"{name}.{s}", b)
    add("vn0", 6); add("S1", 7); add("o0", 0)
    add("kS", 1); add("qS", 3)
    add("vn1", 5); add("o1", 6)
    add("yd0", 7); add("yd1", 1)
    for i in range(NT):
        for c in range(2):
            add(f"wo{i}{c}", [0, 3, 4, 2][2 * i + c])


def plan_dense(jobs):
    def add(name, bank, frees=1):
        jobs.add(("ffn", 0, name), bank, frees)
    for n in range(4):
        add(f"xT{n}", n)
    for n in range(NFF):
        add(f"g{n}", 2 * (n % 2)); add(f"u{n}", 2 * (n % 2) + 1)
    for i in range(NT):
        for c in range(2):
            add(f"d{i}{c}", 4 + 2 * i + c)


def plan_router(jobs):
    def add(name, bank, frees=1):
        jobs.add(("moe", 0, name), bank, frees)
    for n in range(4):
        add(f"xT{n}", n)
    add("logits", 4); add("places", 5)


LAST_USE.update({"k": "k23", "q": "q23", "v": "v23", "c_gate": "c_gate23", "c_val": "c_val23", "z": "z1",
                 "w_out0": "wo10", "w_out1": "wo11"})
LAST_USE.update({f"gu{n}": f"u{n}" for n in range(NFF)})
LAST_USE.update({f"down{n}": "d11" for n in range(NDOWN)})


def build(nc, A, out_dram):
    fp32, fp32r = mybir.dt.float32, mybir.dt.float32r
    ALU = mybir.AluOpType
    ACT = mybir.ActivationFunctionType
    AX = mybir.AxisListType.X

    jobs = Jobs()
    for l in range(DEPTH):
        plan_first(jobs, l)
    for m in range(DEPTH):
        plan_mixer(jobs, m)
        if m == 0:
            plan_dense(jobs)
    plan_router(jobs)

    loads, load_at, loaded, counts = [], {}, {}, [0] * RING

    def add_load(name, k, width, *src):
        n = len(loads)
        load_at[name] = n
        counts[n % RING] += 16 * len(src)
        loaded[name] = counts[n % RING]
        loads.append((name, k, width, src))

    def cols(w, a, b):
        return w[:, a:b].rearrange("(k p) n -> p k n", p=P)

    def add_ada(l, *parts):
        for j in parts:
            add_load((l, f"ada{j}"), KD, 512, cols(A["w_ada"][l], 512 * j, 512 * j + 512))

    add_ada(0, *range(4))
    for l in range(DEPTH):
        for a, b in W_IN_PARTS:
            c0, c1 = COL[a][0], COL[b][1]
            add_load((l, a), KD, c1 - c0, cols(A["w_in"][l], c0, c1))
            if a == "nsa_kc":
                add_load((l, "cmp_w1"), 2 * CMP_LEN // 2, HD, A["cmp_w1"][l].rearrange("v (j p) m -> p (v j) m", p=P))
        for c in range(2):
            g0 = COL["gate"][0] + 512 * c
            add_load((l, f"gate{c}"), KD, 512, cols(A["w_in"][l], g0, g0 + 512))
        add_ada(l, 4, 5)
        if l + 1 < DEPTH:
            add_ada(l + 1, *range(4))
        for c in range(2):
            add_load((l, f"wout{c}"), KD, 512, cols(A["w_out"][l], 512 * c, 512 * c + 512))
    for m in range(DEPTH):
        for name, c0 in W_IN2:
            add_load(("mix", m, name), KD, 512, cols(A["w_in_2"][m], c0, c0 + 512))
        for c in range(2):
            add_load(("mix", m, f"w_out{c}"), KD, 512, cols(A["w_out_2"][m], 512 * c, 512 * c + 512))
        if m == 0:
            for n in range(NFF):
                add_load(("ffn", 0, f"gu{n}"), KD, 2 * FF_PART,
                         *(cols(A[w][0], n * FF_PART, (n + 1) * FF_PART) for w in ("ffn_w_gate_2", "ffn_w_up_2")))
            for n in range(NDOWN):
                k = min(4, KF - 4 * n)
                add_load(("ffn", 0, f"down{n}"), k, D,
                         A["ffn_w_down_2"][0][4 * n * P:(4 * n + k) * P, :].rearrange("(k p) n -> p k n", p=P))

    ctx = ExitStack()
    with ctx:
        def sb(name, shape, dtype=fp32):
            return place[0].enter_context(nc.sbuf_tensor(name, shape, dtype))

        place = [ctx]
        semaphores = {}

        def S(name):
            if name not in semaphores:
                semaphores[name] = ctx.enter_context(nc.semaphore(name))
            return semaphores[name]

        shared = ExitStack()
        place[0] = shared
        ring = sb("ring", [P, RING, SLOT])
        uT = sb("uT", [P, KD, T])
        shared.close()
        place[0] = ctx
        ring_r = sb("ring_r", [P, RING, SLOT], fp32r)
        uT_r = sb("uT_r", [P, KD, T], fp32r)
        const, const2 = sb("const", [P, NCONST]), sb("const2", [P, NCONST2])
        x = sb("x", [P, NT, D])
        rows = sb("rows", [P, P])
        vecs = sb("vecs", [P, P])
        lng, lnb = sb("lng", [P, D]), sb("lnb", [P, D])
        lnst = sb("lnst", [P, NT, 2, 6])
        lnmv = sb("lnmv", [P, NT, 4])
        router_w = sb("router_w", [P, KD, NE])
        items = sb("items", [P, 4 * NE + 1], mybir.dt.int32)

        first = ExitStack()
        place[0] = first
        perow = sb("perow", [P, HD])
        pe_sb = sb("pe_sb", [P, DEPTH, 2, CMP_LEN])
        w2 = sb("w2", [HD, DEPTH, 2, HD])
        b_f = sb("b_f", [FOX_HEADS, DEPTH])
        gate1p = sb("gate1p", [P, D])
        adac = sb("adac", [P, 16])
        raw = {n: sb(f"raw_{n}", [P, k, T]) for n, k, _, _ in ROPES}
        rope_t2 = sb("rope_t2", [P, 2, 2 * T])
        rot = {n: sb(f"rot_{n}", [P, k, T]) for n, k, _, _ in ROPES}
        ksS, kwS = sb("ksS", [P, T]), sb("kwS", [P, T])
        iw = sb("iw", [P, NT, IDX_HEADS])
        dv = sb("dv", [P, NT, HD])
        fq, fk = sb("fq", [P, 3, T]), sb("fk", [P, 3, T])
        fv = sb("fv", [P, NT, FOX_HEADS * HD])
        vsw = sb("vsw", [P, NT, 2, P])
        ff = sb("ff", [FOX_HEADS, 5, T])
        sgate = sb("sgate", [P, NT, 18])
        blk = sb("blk", [P, 2, CMP_LEN // 2, NSA_GROUPS, NCMP])
        ch = sb("ch", [HD, 3, 2, NSA_GROUPS * NCMP])
        chrep = sb("chrep", [HD, NSA_GROUPS, NSA_HPG, NCMP])
        kcT = sb("kcT", [P, NSA_GROUPS, NCMP])
        vblk = sb("vblk", [NHC, NSA_HEADS, HD])
        sg = sb("sg", [P, NT, D])
        mix = sb("mix", [P, NT, D])
        isc = sb("isc", [P, NT, T])
        isw = sb("isw", [P, NT, T])
        m8 = sb("m8", [P, NT, 8])
        p_sb, pT = sb("p_sb", [P, 2, 512]), sb("pT", [P, 2, 512])
        relu, rope_t1 = p_sb, pT
        cmp_s = sb("cmp_s", [P, NT, NSA_HEADS, NCMP])
        otmp = sb("otmp", [P, NSA_HEADS * HD])
        stat = sb("stat", [P, 4, 4, 8])
        first.close()

        second = ExitStack()
        place[0] = second
        wba = sb("wba", [P, KD, 2 * DH])
        cvrow = sb("cvrow", [P, 2, P])
        cvec = sb("cvec", [P, 2, P])
        decay_in = sb("decay_in", [P, 2, DH])
        ong = sb("ong", [P, DK])
        hpad = sb("hpad", [P, 4, T + CONV_WIN - 1])
        cacc = sb("cacc", [P, 4, T])
        sig = sb("sig", [P, 4, T])
        cn = sig[:, :, :].rearrange("p f t -> p (f t)").rearrange("p (i n) -> p i n", i=NT)
        ptap = sb("ptap", [P, 2, T])
        qkvpad = sb("qkvpad", [P, 12, T + SHORT - 1])
        over = qkvpad[:, :, :].rearrange("p f t -> p (f t)")
        Lw, LT, attn = (over[:, 1024 * n:1024 * n + 1024].rearrange("p (i n) -> p i n", i=NT) for n in range(3))
        qkv = sb("qkv", [P, 12, T])
        sq = sb("sq", [P, 8, T])
        X, XT = (sq[:, 4 * n:4 * n + 4, :].rearrange("p f t -> p (f t)").rearrange("p (i n) -> p i n", i=NT) for n in range(2))
        sz = sb("sz", [P, NT, 512])
        ktok = sb("ktok", [P, NT, 512])
        vnew = ktok
        kT = sb("kT", [P, DH, T])
        vb = sb("vb", [P, NT, 512])
        kdec = sb("kdec", [P, 512])
        decay = sb("decay", [P, NT, 512])
        attnT = sb("attnT", [P, NT, 512])
        lev = sb("lev", [P, 4, 512])
        NsT, Y = lev[:, 0:2, :], lev[:, 2:4, :]
        z2 = lev[:, :, :].rearrange("p a n -> p (a n)").rearrange("p (i n) -> p i n", i=NT)
        S1 = sb("S1", [P, 512])
        oi = Lw[:, 1, :]
        o = attn
        sm = {n: sb(f"sm_{n}", [P, NT, 2 * DH]) for n in
              ("logit", "eb", "beta", "z", "za", "ze", "zl", "soft", "ea", "g", "ncum", "rest", "coef", "nbe",
               "ss", "norm", "rnorm", "rq", "osum", "orms", "orstd")}
        cstat, cmv = sb("cstat", [P, NT, 6]), sb("cmv", [P, NT, 4])
        osq, eps_col = sb("osq", [P, DK]), sb("eps_col", [P, 1])
        second.close()

        third = ExitStack()
        place[0] = third
        ff_hi = sb("ff_hi", [P, 2, SLOT], fp32r)
        u_hi, u_lo = uT_r, sb("u_lo", [P, KD, T], fp32r)
        h_hi, h_lo = sb("h_hi", [P, KF, T], fp32r), sb("h_lo", [P, KF, T], fp32r)
        hs = sb("hs", [P, 2, 512])
        z3 = uT[:, :, :].rearrange("p k t -> p (k t)").rearrange("p (i n) -> p i n", i=NT)
        third.close()

        fourth = ExitStack()
        place[0] = fourth
        more_his = sb("more_his", [P, 2 * MOE_RING - 2 * RING, PIECE], fp32r)
        xe_hi, xe_lo = sb("xe_hi", [P, KD, P], fp32r), sb("xe_lo", [P, KD, P], fp32r)
        he_hi, he_lo = sb("he_hi", [P, KE, P], fp32r), sb("he_lo", [P, KE, P], fp32r)
        hse, ht = (uT[:, 4 * n:4 * n + 4, :].rearrange("p k t -> p (k t)").rearrange("p (a f) -> p a f", a=2) for n in range(2))
        ye = sb("ye", [P, D])
        total = sb("total", [P, NT, D])
        pick, pickc = sb("pick", [P, NT, P]), sb("pickc", [P, NT, P])
        pickT = sb("pickT", [P, NT, P])
        logits, best = sb("logits", [P, NT, NE]), sb("best", [P, NT, 8])
        best_at, best_f = sb("best_at", [P, NT, 8], mybir.dt.uint32), sb("best_f", [P, NT, 8])
        gates = sb("gates", [P, NT, 4])
        hot = sb("hot", [P, 2, NT, NE])
        chosen = sb("chosen", [P, NT, NE])
        places, comb = sb("places", [P, NT, 2 * NE]), sb("comb", [P, NT, 2 * NE])
        long = sb("long", [P, 4, NE])
        item_f = sb("item_f", [P, 4 * NE + 1])
        fourth.close()
        place[0] = ctx
        bank = [ctx.enter_context(nc.psum_tensor(f"bank{b}", [P, 512], fp32)) for b in range(8)]

        def C(name, n=P):
            a, b = CONST_AT[name]
            return (const2 if name in CONST2 else const)[0:n, a:b]

        bank_full = [S(f"bank_full{b}") for b in range(8)]
        bank_free = [S(f"bank_free{b}") for b in range(8)]
        slot_loaded = [S(f"slot_loaded{s}") for s in range(RING)]

        def take(pe, job):
            if job.free_before:
                pe.wait_ge(bank_free[job.bank], job.free_before)
            return bank[job.bank]

        def filled(eng, job):
            eng.wait_ge(bank_full[job.bank], job.fill)
            return bank[job.bank]

        def weights(pe, name):
            n = load_at[name]
            pe.wait_ge(slot_loaded[n % RING], loaded[name])
            _, k, width, _ = loads[n]
            return ring[:, n % RING, 0:k * width].rearrange("p (k n) -> p k n", k=k)

        first_ring = len(loads) % RING
        piece_loaded = [S(f"piece_loaded{n}") for n in range(MOE_RING)]

        FF = [f"gu{n}" for n in range(NFF)] + [f"down{n}" for n in range(NDOWN)]

        def ff_parts(m):
            n = load_at["ffn", 0, FF[m]]
            _, k, width, _ = loads[n]
            return [a[:, 0:k * width].rearrange("p (k n) -> p k n", k=k) for a in (ff_hi[:, m % 2, :], ring_r[:, n % RING, :])]

        def half_slot(memory, j, p):
            if j < 2 * RING:
                flat = memory[:, (first_ring + j // 2) % RING, j % 2 * PIECE:(j % 2 + 1) * PIECE]
            else:
                flat = more_his[:, j - 2 * RING, :]
            return flat.rearrange("p (k n) -> p k n", n=FE_PART if p < NPIECE_UP else D)

        def piece_raw(p):
            return half_slot(ring, p % MOE_RING, p)

        def piece_lo(p):
            return half_slot(ring_r, p % MOE_RING, p)

        def piece_hi(p):
            return half_slot(ring_r, MOE_RING + p % MOE_RING, p)

        def copied(eng, job):
            eng.wait_ge(bank_free[job.bank], job.free_after)

        def chain(eng, sem):
            count = [0]

            def link(ins):
                count[0] += 1
                ins.then_inc(sem, 1)
                eng.wait_ge(sem, count[0])
            return link

        vec_c = lambda k: vecs[:, k:k + 1]

        vec_bada = lambda l: vecs[:, 8 + 16 * l:24 + 16 * l]

        block = ctx.enter_context(nc.Block())

        @block.sync
        def _(sp):
            def slot_free(sp, name):
                what = name[-1]
                if what.startswith("down") and what != f"down{NDOWN - 1}":
                    sp.wait_ge(S("down_used"), int(what[4:]) + 1)
                else:
                    j = jobs[(*name[:-1], LAST_USE[what])]
                    sp.wait_ge(bank_full[j.bank], j.fill)

            def norm_rows(sp, q, g, b):
                if q:
                    sp.wait_ge(S("x_ready"), NT * q)
                sp.dma_start(lng[:, :], g.partition_broadcast(P)).then_inc(S("norm_rows"), 16)
                sp.dma_start(lnb[:, :], b.partition_broadcast(P)).then_inc(S("norm_rows"), 16)

            sp.dma_start(rows[0:8, :], A["c"].rearrange("o (k p) -> (o k) p", p=P)).then_inc(S("rows_loaded"), 16)
            for l in range(DEPTH):
                sp.dma_start(rows[8 + 16 * l:24 + 16 * l, :],
                             A["b_ada"][l, 0:2 * D].rearrange("(k p) -> k p", p=P)).then_inc(S("rows_loaded"), 16)
            sp.dma_start(const[:, :], A["const"]).then_inc(S("const_loaded"), 16)
            sp.dma_start(perow[:, :], A["cmp_pe"].rearrange("l v i d -> (l v i) d")).then_inc(S("small_loaded"), 16)
            sp.dma_start(w2[:, :, :, :], A["cmp_w2"].rearrange("l v a b -> a l v b")).then_inc(S("small_loaded"), 16)
            with nc.allow_non_contiguous_dma(reason="12 numbers"):
                sp.dma_start(b_f[:, :], A["b_f"].rearrange("l h -> h l")).then_inc(S("small_loaded"), 16)
            sp.dma_start(const2[:, :], A["const2"]).then_inc(S("const2_loaded"), 16)
            sp.dma_start(router_w[:, :, :], A["router_w_2"][0].rearrange("(k p) e -> p k e", p=P)).then_inc(S("router_loaded"), 16)
            sp.dma_start(x[:, :, :], A["x"][0].rearrange("(i p) d -> p i d", p=P)).then_inc(S("x_loaded"), 16)
            for n, (name, k, width, src) in enumerate(loads):
                s = n % RING
                if n >= RING:
                    slot_free(sp, loads[n - RING][0])
                dst = ring[:, s, 0:k * width].rearrange("p (k n) -> p k n", k=k)
                w = width // len(src)
                for q, piece in enumerate(src):
                    sp.dma_start(dst[:, :, q * w:(q + 1) * w], piece).then_inc(slot_loaded[s], 16)
                if name[-1] == "nsa_vs":
                    l = name[0]
                    if l:
                        sp.wait_ge(S("x_ready"), NT * l)
                    sp.dma_start(gate1p[:, :], A["b_ada"][l, 2 * D:3 * D].partition_broadcast(P)).then_inc(S("gate_bias"), 16)
                    norm_rows(sp, l, A["ln_g"][l], A["ln_b"][l])
                if name[-1] == "k":
                    m = name[1]
                    q = DEPTH + 2 * m
                    sp.wait_ge(S("x_ready"), NT * q)
                    sp.dma_start(wba[:, :, :], cols(A["w_in_2"][m], LOGITS2, LOGITS2 + 2 * DH)).then_inc(S("mix_small"), 16)
                    sp.dma_start(cvrow[0:CONV_WIN * 4, 0, :], A["conv_dw_w_2"][m].rearrange("j (f p) -> (j f) p", p=P)).then_inc(S("mix_small"), 16)
                    sp.dma_start(cvrow[0:SHORT * 12, 1, :], A["short_conv_w_2"][m].rearrange("j (f p) -> (j f) p", p=P)).then_inc(S("mix_small"), 16)
                    for r, w in enumerate(("conv_dw_b_2", "conv_ln_g_2", "conv_ln_b_2")):
                        sp.dma_start(cvrow[SHORT * 12 + 4 * r:SHORT * 12 + 4 * r + 4, 1, :],
                                     A[w][m].rearrange("(f p) -> f p", p=P)).then_inc(S("mix_small"), 16)
                    sp.dma_start(decay_in[:, 0, :], A["a_log_2"][m].partition_broadcast(P)).then_inc(S("mix_small"), 16)
                    sp.dma_start(decay_in[:, 1, :], A["dt_bias_2"][m].partition_broadcast(P)).then_inc(S("mix_small"), 16)
                    sp.dma_start(ong[:, :], A["out_norm_g_2"][m].partition_broadcast(P)).then_inc(S("mix_small"), 16)
                    norm_rows(sp, q, A["ln_mix_g_2"][m], A["ln_mix_b_2"][m])
                if name[-1] == "gu5":
                    norm_rows(sp, DEPTH + 1, A["ln_ffn_g_2"][0], A["ln_ffn_b_2"][0])
            def load_piece(p, e):
                if p < NPIECE_UP:
                    q, side, half = p // 4, p % 4 // 2, p % 2
                    src = A["moe_w_up_2" if side else "moe_w_gate_2"][0]
                    src = src[e, 512 * half:512 * half + 512, q * FE_PART:(q + 1) * FE_PART]
                else:
                    r = (p - NPIECE_UP) * 256
                    src = A["moe_w_down_2"][0][e, r:r + 256, :]
                sp.dma_start(piece_raw(p), src.rearrange("o (k p) n -> p (o k) n", p=P)).then_inc(piece_loaded[p % MOE_RING], 16)

            for p in range(NPIECE):
                if p < MOE_RING:
                    slot_free(sp, loads[len(loads) - RING + p // 2][0])
                else:
                    sp.wait_ge(S("piece_used"), p - MOE_RING + 1)
                load_piece(p, bass.ds(0, 1))
                if p == MOE_RING - 1:
                    norm_rows(sp, NORMS - 1, A["ln_ffn_g_2"][1], A["ln_ffn_b_2"][1])
            sp.wait_ge(S("items_ready"), 1)
            nitems = sp.value_load(items[0:1, 4 * NE:4 * NE + 1], min_val=NE, max_val=2 * NE - 1)
            with sp.Fori(1, nitems) as n:
                e = sp.value_load(items[0:1, bass.ds(n + 2 * NE, 1)], min_val=0, max_val=NE - 1)
                for p in range(NPIECE):
                    sp.wait_ge(S("piece_used"), n * NPIECE + (p - MOE_RING + 1))
                    load_piece(p, bass.ds(e, 1))
            sp.wait_ge(S("x_ready"), NT * NORMS)
            sp.dma_start(out_dram[0].rearrange("(i p) d -> p i d", p=P), x[:, :, :]).then_inc(S("stored"), 16)
            sp.wait_ge(S("stored"), 16)

        @block.tensor
        def _(pe):
            mm = nc.tensor.matmul

            def at(name):
                return COL[name][0] - COL[PART_OF[name]][0]

            def feat(b, l, name, c0, n, to):
                w = weights(pe, (l, PART_OF[name]))
                a = at(name) + c0
                for k in range(KD):
                    last = mm(b[0:n, to:to + T], w[:, k, a:a + n], uT[:, k, :], start=(k == 0), stop=(k == KD - 1))
                return last

            def tok(b, l, part, a, n, i, to):
                w = weights(pe, (l, part))
                for k in range(KD):
                    last = mm(b[:, to:to + n], uT[:, k, i * P:(i + 1) * P], w[:, k, a:a + n],
                              start=(k == 0), stop=(k == KD - 1))
                return last

            def done(ins, j):
                ins.then_inc(bank_full[j.bank], 1)

            def feats(l, job, *parts):
                j = jobs[l, job]
                b = take(pe, j)
                for n, (name, c0, width) in enumerate(parts):
                    last = feat(b, l, name, c0, width, n * T)
                done(last, j)

            def rotate(l, name):
                n = ROPE_AT[name]
                _, tiles, r, dim = ROPES[n]
                j = jobs[l, f"rot_{name}"]
                b = take(pe, j)
                copied(pe, jobs[l, PROJECTED[name]])
                done(mm(b[0:r, 0:tiles * T], C(f"rot{dim}", r)[:, 0:r], raw[name][0:r, :, :], start=True, stop=True), j)

            pe.wait_ge(S("const_loaded"), 16)
            pe.wait_ge(S("rows_loaded"), 48)
            nc.tensor.transpose(bank[6][:, 0:40], rows[0:40, :], C("ident", 40)[:, 0:40]).then_inc(S("vecs_T"), 1)
            pe.wait_ge(S("small_loaded"), 48)
            nc.tensor.transpose(bank[5][0:HD, 0:P], perow[:, :], C("ident")).then_inc(S("pe_T"), 1)
            pe.wait_ge(S("vecs_ready"), 1)
            pe.wait_ge(S("pe_ready"), 2)

            def shift_scale(l, q):
                j = jobs[l, f"ada{q}"]
                b = take(pe, j)
                pe.wait_ge(S("ada_summed" if l == 0 else "ada_next"), q + 1)
                w = weights(pe, (l, f"ada{q}"))
                for m in range(4):
                    last = mm(b[:, m:m + 1], w[:, 0, m * P:(m + 1) * P], C("ones")[:, 0:1], start=True, stop=True)
                done(last, j)

            for q in range(4):
                shift_scale(0, q)
            for l in range(DEPTH):
                if l == 0:
                    pe.wait_ge(S("x_loaded"), 16)
                else:
                    pe.wait_ge(S("x_ready"), NT * l)
                for m in range(4):
                    j = jobs[l, f"xT{m}"]
                    b = take(pe, j)
                    for kk in range(2):
                        for i in range(NT):
                            last = nc.tensor.transpose(b[:, kk * T + i * P:kk * T + (i + 1) * P],
                                                       x[:, i, (2 * m + kk) * P:(2 * m + kk + 1) * P], C("ident"))
                    done(last, j)
                for m in range(4):
                    copied(pe, jobs[l, f"xT{m}"])
                feats(l, "iq", ("idx_q", 0, P), ("idx_q", P, P))
                j = jobs[l, "ikw"]
                b = take(pe, j)
                feat(b, l, "idx_k", 0, IDX_DIM, 0)
                for i in range(NT):
                    last = tok(b, l, "idx_q", at("idx_w"), IDX_HEADS, i, T + IDX_HEADS * i)
                done(last, j)
                feats(l, "dq", ("dsa_q", 0, P), ("dsa_q", P, P))
                rotate(l, "iq")
                j = jobs[l, "dkv"]
                b = take(pe, j)
                feat(b, l, "dsa_k", 0, HD, 0)
                for i in range(NT):
                    last = tok(b, l, "dsa_q", at("dsa_v"), HD, i, T + HD * i)
                done(last, j)
                rotate(l, "ik")
                for i in range(NT):
                    j = jobs[l, f"fv{i}"]
                    done(tok(take(pe, j), l, "fox_v", 0, FOX_HEADS * HD, i, 0), j)
                feats(l, "ff", ("fox_f", 0, FOX_HEADS))
                rotate(l, "dq")
                rotate(l, "dk")
                pe.wait_ge(S("rope_done"), NR * l + 2)
                for n, (i, heads) in enumerate(ISCORES):
                    j = jobs[l, f"is{n}"]
                    b = take(pe, j)
                    keys = (i + 1) * P
                    for m, h in enumerate(heads):
                        r = slice(IDX_DIM * (h % 4), IDX_DIM * (h % 4 + 1))
                        last = mm(b[:, m * keys:(m + 1) * keys], rot["iq"][r, h // 4, i * P:(i + 1) * P],
                                  rot["ik"][r, 0, 0:keys], start=True, stop=True)
                    done(last, j)
                feats(l, "fq01", ("fox_q", 0, P), ("fox_q", P, P))
                feats(l, "fq2", ("fox_q", 2 * P, P))
                feats(l, "fk01", ("fox_k", 0, P), ("fox_k", P, P))
                feats(l, "fk2", ("fox_k", 2 * P, P))
                feats(l, "nq01", ("nsa_q", 0, P), ("nsa_q", P, P))
                feats(l, "nq2", ("nsa_q", 2 * P, P))
                feats(l, "kcvc", ("nsa_kc", 0, P), ("nsa_vc", 0, P))
                rotate(l, "nq01")
                feats(l, "ks", ("nsa_ks", 0, P))
                rotate(l, "nq2")
                j = jobs[l, "vsw"]
                b = take(pe, j)
                for i in range(NT):
                    for m, name in enumerate(("nsa_vs", "nsa_vw")):
                        last = tok(b, l, "nsa_vs", at(name), P, i, (2 * i + m) * P)
                done(last, j)
                j = jobs[l, "kwg"]
                b = take(pe, j)
                feat(b, l, "nsa_kw", 0, P, 0)
                for i in range(NT):
                    last = tok(b, l, "nsa_vs", at("nsa_g"), 18, i, T + 18 * i)
                done(last, j)
                rotate(l, "ks")
                j = jobs[l, "ch"]
                b = take(pe, j)
                w1 = weights(pe, (l, "cmp_w1"))
                copied(pe, jobs[l, "kcvc"])
                for v in range(2):
                    for t in range(CMP_LEN // 2):
                        last = mm(b[0:HD, 30 * v:30 * v + 30], w1[:, CMP_LEN // 2 * v + t, :], blk[:, v, t, :, :],
                                  start=(t == 0), stop=(t == CMP_LEN // 2 - 1))
                done(last, j)
                rotate(l, "kw")
                for c in range(2):
                    for i in range(NT):
                        j = jobs[l, f"gt{c}{i}"]
                        b = take(pe, j)
                        w = weights(pe, (l, f"gate{c}"))
                        for k in range(KD):
                            last = mm(b[:, :], uT[:, k, i * P:(i + 1) * P], w[:, k, :], start=(k == 0), stop=(k == KD - 1))
                        done(last, j)
                j = jobs[l, "ckv"]
                b = take(pe, j)
                pe.wait_ge(S("ch_ready"), l + 1)
                mm(b[0:HD, 0:30], w2[:, l, 0, :], ch[:, 2, 0, :], start=True, stop=True)
                done(mm(b[0:NHC, HD:2 * HD], chrep[:, :, :, :], w2[:, l, 1, :], start=True, stop=True), j)
                def ada_gate(c):
                    j = jobs[l, f"gb{c}"]
                    b = take(pe, j)
                    pe.wait_ge(S("ada_summed"), 4 + 2 * l + c + 1)
                    w = weights(pe, (l, f"ada{4 + c}"))
                    done(mm(b[:, :], C("ones"), w[:, 0, :], start=True, stop=True), j)

                def head_qk(kind, h):
                    r = slice(HD * (h % 2), HD * (h % 2 + 1))
                    if kind == "dsa":
                        return rot["dq"][r, h // 2, :], rot["dk"][r, 0, :]
                    if kind == "fox":
                        return fq[r, h // 2, :], fk[r, h // 2, :]
                    g = h // NSA_HPG
                    if kind == "cmp":
                        src = raw["nq01"][r, h // 2, :] if h < 4 else raw["nq2"][r, 0, :]
                        return src, kcT[r, g, :]
                    q = rot["nq01"][r, h // 2, :] if h < 4 else rot["nq2"][r, 0, :]
                    straight, swapped = (rot["ks"][:, 0, :], ksS) if kind == "slc" else (rot["kw"][:, 0, :], kwS)
                    return q, (straight if g == h % 2 else swapped)[r, :]

                def scores(n):
                    kind, i, heads, keys = GROUPS[n]
                    j = jobs[l, f"S{n}"]
                    b = take(pe, j)
                    nh = len(heads)
                    if n == 0:
                        for need in ("fq01", "fq2", "fk01", "fk2", "fv0", "fv1"):
                            copied(pe, jobs[l, need])
                        pe.wait_ge(S("fox_ready"), l + 1)
                        copied(pe, jobs[l, "ckv"])
                        copied(pe, jobs[l, "vsw"])
                        copied(pe, jobs[l, "dkv"])
                        pe.wait_ge(S("rope_done"), NR * (l + 1))
                    if kind == "dsa" and heads[0] == 0:
                        pe.wait_ge(S("sel_ready"), NT * l + i + 1)
                    first = [True]

                    def add(o, w, m):
                        ins = mm(o, w, m, start=first[0], stop=False, skip_group_check=True)
                        first[0] = False
                        return ins

                    def head(m):
                        q, k = head_qk(kind, heads[m])
                        return add(b[:, m * keys:(m + 1) * keys], q[:, i * P:(i + 1) * P], k[:, 0:keys])

                    for m, h in enumerate(heads):
                        if kind == "fox":
                            add(b[:, m * keys:(m + 1) * keys], C("ident", FOX_HEADS)[:, h:h + 1].broadcast_to([FOX_HEADS, P]),
                                ff[:, 4, 0:keys])
                        if h % 2 == 0:
                            upper = head(m)
                    upper.then_inc(S("upper_heads"), 1)
                    view = b[:, 0:nh * keys].rearrange("p (h s) -> p h s", h=nh)
                    if kind == "cmp":
                        m0 = CONST_AT["cmp_mask"][0] + i * NHC
                        last = add(b[:, 0:NHC], C("ident"), const[:, m0:m0 + NHC])
                    elif kind == "dsa":
                        last = add(view, C("ident"), isw[:, i, 0:keys].unsqueeze(1).broadcast_to([P, nh, keys]))
                    else:
                        last = add(view[:, :, keys - P:keys], C("ident"), C("causal").unsqueeze(1).broadcast_to([P, nh, P]))
                    pe.wait_ge(S("upper_heads"), NG * l + n + 1)
                    for m, h in enumerate(heads):
                        if h % 2:
                            last = head(m)
                    done(last, j)

                def transposes(n):
                    kind, i, heads, keys = GROUPS[n]
                    j = jobs[l, f"T{n}"]
                    b = take(pe, j)
                    if kind == "cmp":
                        pe.wait_ge(S("cmp_p_ready"), NT * l + i + 1)
                    else:
                        copied(pe, jobs[l, f"S{n}"])
                    if kind == "cmp":
                        last = nc.tensor.transpose(b[0:NHC, 0:P], p_sb[:, n % 2, 0:NHC], C("ident"))
                    else:
                        for c in range(len(heads) * keys // P):
                            last = nc.tensor.transpose(b[:, c * P:(c + 1) * P], p_sb[:, n % 2, c * P:(c + 1) * P], C("ident"))
                    done(last, j)

                def outputs(n):
                    kind, i, heads, keys = GROUPS[n]
                    j = jobs[l, f"O{n}"]
                    b = take(pe, j)
                    copied(pe, jobs[l, f"T{n}"])
                    if kind == "cmp":
                        last = mm(b[:, 0:NSA_HEADS * HD], pT[0:NHC, n % 2, 0:P], vblk[:, :, :], start=True, stop=True)
                    else:
                        nk = keys // P
                        for m, h in enumerate(heads):
                            for c in range(nk):
                                if kind == "dsa":
                                    v = dv[:, c, :]
                                elif kind == "fox":
                                    v = fv[:, c, h * HD:(h + 1) * HD]
                                else:
                                    g = h // NSA_HPG
                                    v = vsw[:, c, 0 if kind == "slc" else 1, g * HD:(g + 1) * HD]
                                last = mm(b[:, m * HD:(m + 1) * HD], pT[:, n % 2, (m * nk + c) * P:(m * nk + c + 1) * P], v,
                                          start=(c == 0), stop=(c == nk - 1))
                    done(last, j)

                for n in range(NG + 2):
                    if n < NG:
                        scores(n)
                    if 1 <= n <= NG:
                        transposes(n - 1)
                    if n >= 2:
                        outputs(n - 2)
                    if n in GATE_AT:
                        ada_gate(GATE_AT[n])
                    if l + 1 < DEPTH and n in NEXT_AT:
                        shift_scale(l + 1, NEXT_AT[n])
                for i in range(NT):
                    pe.wait_ge(S("mix_ready"), NT * l + i + 1)
                    for half in range(2):
                        j = jobs[l, f"yT{i}{half}"]
                        b = take(pe, j)
                        for kk in range(4):
                            k = 4 * half + kk
                            last = nc.tensor.transpose(b[:, kk * P:(kk + 1) * P], mix[:, i, k * P:(k + 1) * P], C("ident"))
                        done(last, j)
                for i in range(NT):
                    for half in range(2):
                        copied(pe, jobs[l, f"yT{i}{half}"])
                    for c in range(2):
                        j = jobs[l, f"wo{i}{c}"]
                        b = take(pe, j)
                        w = weights(pe, (l, f"wout{c}"))
                        for k in range(KD):
                            last = mm(b[:, :], uT[:, k, i * P:(i + 1) * P], w[:, k, :], start=(k == 0), stop=(k == KD - 1))
                        done(last, j)

            def transpose_x(key, q):
                banks = [take(pe, jobs[(*key, f"xT{m}")]) for m in range(4)]
                for i in range(NT):
                    pe.wait_ge(S("x_ready"), NT * (q - 1) + i + 1)
                    for m in range(4):
                        for kk in range(2):
                            last = nc.tensor.transpose(banks[m][:, kk * T + i * P:kk * T + (i + 1) * P],
                                                       x[:, i, (2 * m + kk) * P:(2 * m + kk + 1) * P], C("ident"))
                        if i == NT - 1:
                            done(last, jobs[(*key, f"xT{m}")])
                for m in range(4):
                    copied(pe, jobs[(*key, f"xT{m}")])

            def heads4(b, lhsT, rhs):
                for h in range(DH):
                    last = mm(b[:, h * P:(h + 1) * P], lhsT(h), rhs(h), start=True, stop=True)
                return last

            def transposes4(b, src):
                for h in range(4):
                    last = nc.tensor.transpose(b[:, h * P:(h + 1) * P], src(h), C("ident"))
                return last

            pe.wait_ge(S("const2_loaded"), 16)

            def mixer(m):
                q = DEPTH + 2 * m
                J = lambda name: jobs["mix", m, name]
                hs_ = lambda h: slice(h * P, (h + 1) * P)
                tile = lambda i: slice(i * P, (i + 1) * P)
                transpose_x(("mix", m), q)

                def project(name):
                    w = weights(pe, ("mix", m, name))
                    for half in range(2):
                        j = J(f"{name}{2 * half}{2 * half + 1}")
                        b = take(pe, j)
                        for f in range(2):
                            a = (2 * half + f) * P
                            for k in range(KD):
                                last = mm(b[:, f * T:(f + 1) * T], w[:, k, a:a + P], uT[:, k, :], start=(k == 0), stop=(k == KD - 1))
                        done(last, j)

                project("c_gate")
                project("c_val")
                pe.wait_ge(S("mix_small"), 16 * MIX_SMALL * (m + 1))
                j = J("vw")
                b = take(pe, j)
                n0, n1 = CONV_WIN * 4, SHORT * 12 + 12
                nc.tensor.transpose(b[:, 0:n0], cvrow[0:n0, 0, :], C("ident", n0)[:, 0:n0])
                done(nc.tensor.transpose(b[:, P:P + n1], cvrow[0:n1, 1, :], C("ident", n1)[:, 0:n1]), j)
                j = J("ba")
                b = take(pe, j)
                for i in range(NT):
                    for k in range(KD):
                        last = mm(b[:, 8 * i:8 * i + 8], uT[:, k, tile(i)], wba[:, k, :], start=(k == 0), stop=(k == KD - 1))
                done(last, j)
                for name in QKV:
                    project(name)
                w = weights(pe, ("mix", m, "z"))
                for i in range(NT):
                    j = J(f"z{i}")
                    b = take(pe, j)
                    for k in range(KD):
                        last = mm(b[:, :], uT[:, k, tile(i)], w[:, k, :], start=(k == 0), stop=(k == KD - 1))
                    done(last, j)
                pe.wait_ge(S("g_ready"), m + 1)
                j = J("gc")
                b = take(pe, j)
                for i in range(NT):
                    mm(b[:, DH * i:DH * i + DH], C("tri_le"), sm["g"][:, i, 0:DH], start=True, stop=True)
                    last = mm(b[:, 8 + DH * i:8 + DH * i + DH], C("ones"), sm["g"][:, i, 0:DH], start=True, stop=True)
                done(last, j)
                for i in range(NT):
                    j = J(f"dm{i}")
                    b = take(pe, j)
                    for h in range(DH):
                        mm(b[:, hs_(h)], sm["g"][:, i, h:h + 1].broadcast_to([P, P]), C("tri_le"), start=(h == 0), stop=False,
                           skip_group_check=True)
                    done(mm(b[:, :].rearrange("p (h c) -> p h c", h=DH), C("ident"),
                            C("causal").unsqueeze(1).broadcast_to([P, DH, P]), start=False, stop=True, skip_group_check=True), j)
                pe.wait_ge(S("squares"), 4 * (m + 1))
                j = J("ss")
                b = take(pe, j)
                for i in range(NT):
                    for f in range(8):
                        last = mm(b[:, 8 * i + f:8 * i + f + 1], sq[:, f, tile(i)], C("ones")[:, 0:1], start=True, stop=True)
                done(last, j)
                for i in range(NT):
                    j = J(f"kt{i}")
                    done(transposes4(take(pe, j), lambda h: qkv[:, h, tile(i)]), j)
                pe.wait_ge(S("qkv_silu"), 6 * (m + 1))
                for i in range(NT):
                    j = J(f"vt{i}")
                    done(transposes4(take(pe, j), lambda h: qkv[:, 8 + h, tile(i)]), j)
                for i in range(NT):
                    j = J(f"kn{i}")
                    b = take(pe, j)
                    copied(pe, J(f"kt{i}"))
                    done(transposes4(b, lambda h: ktok[:, i, hs_(h)]), j)
                for i in range(NT):
                    copied(pe, J(f"kn{i}"))
                    j = J(f"A{i}")
                    done(heads4(take(pe, j), lambda h: kT[:, h, tile(i)], lambda h: kT[:, h, tile(i)]), j)
                for i in range(NT):
                    j = J(f"at{i}")
                    done(heads4(take(pe, j), lambda h: qkv[:, 4 + h, tile(i)], lambda h: kT[:, h, tile(i)]), j)
                for i in range(NT):
                    j = J(f"LT{i}")
                    b = take(pe, j)
                    copied(pe, J(f"A{i}"))
                    done(transposes4(b, lambda h: Lw[:, i, hs_(h)]), j)
                for i in range(NT):
                    j = J(f"aT{i}")
                    b = take(pe, j)
                    copied(pe, J(f"at{i}"))
                    done(transposes4(b, lambda h: attn[:, i, hs_(h)]), j)
                pe.wait_ge(S("conv_dve"), m + 1)
                pe.wait_ge(S("conv_pool"), m + 1)
                for i in range(NT):
                    j = J(f"ct{i}")
                    done(transposes4(take(pe, j), lambda f: cacc[:, f, tile(i)]), j)
                for s in range(1, LEVELS):
                    if s == 3:
                        for i in range(NT):
                            j = J(f"cb{i}")
                            b = take(pe, j)
                            copied(pe, J(f"ct{i}"))
                            done(transposes4(b, lambda f: cn[:, i, hs_(f)]), j)
                    for i in range(NT):
                        if s == 1:
                            pe.wait_ge(S("x_first"), NT * m + i + 1)
                        else:
                            copied(pe, J(f"D{i}.{s - 1}"))
                            copied(pe, J(f"E{i}.{s - 1}"))
                        j = J(f"Y{i}.{s}")
                        b = take(pe, j)
                        pe.wait_ge(S("level_ready"), NT * ((LEVELS - 1) * m + s - 1) + i + 1)
                        done(heads4(b, lambda h: NsT[:, i, hs_(h)], lambda h: X[:, i, hs_(h)]), j)
                    for i in range(NT):
                        copied(pe, J(f"Y{i}.{s}"))
                        if s < LEVELS - 1:
                            j = J(f"D{i}.{s}")
                            done(heads4(take(pe, j), lambda h: XT[:, i, hs_(h)], lambda h: Y[:, i, hs_(h)]), j)
                        j = J(f"E{i}.{s}")
                        done(heads4(take(pe, j), lambda h: Y[:, i, hs_(h)], lambda h: XT[:, i, hs_(h)]), j)
                copied(pe, J(f"E0.{LEVELS - 1}"))
                copied(pe, J("vt0"))
                j = J("vn0")
                done(heads4(take(pe, j), lambda h: XT[:, 0, hs_(h)], lambda h: vb[:, 0, hs_(h)]), j)
                copied(pe, J("vn0"))
                pe.wait_ge(S("kdec_ready"), m + 1)
                j = J("S1")
                done(heads4(take(pe, j), lambda h: kdec[:, hs_(h)], lambda h: vnew[:, 0, hs_(h)]), j)
                copied(pe, J("aT0"))
                j = J("o0")
                done(heads4(take(pe, j), lambda h: attnT[:, 0, hs_(h)], lambda h: vnew[:, 0, hs_(h)]), j)
                copied(pe, J("S1"))
                j = J("kS")
                done(heads4(take(pe, j), lambda h: kT[:, h, tile(1)], lambda h: S1[:, hs_(h)]), j)
                j = J("qS")
                done(heads4(take(pe, j), lambda h: qkv[:, 4 + h, tile(1)], lambda h: S1[:, hs_(h)]), j)
                copied(pe, J(f"E1.{LEVELS - 1}"))
                copied(pe, J("kS"))
                j = J("vn1")
                done(heads4(take(pe, j), lambda h: XT[:, 1, hs_(h)], lambda h: vb[:, 1, hs_(h)]), j)
                copied(pe, J("vn1"))
                copied(pe, J("aT1"))
                j = J("o1")
                done(heads4(take(pe, j), lambda h: attnT[:, 1, hs_(h)], lambda h: vnew[:, 1, hs_(h)]), j)
                for i in range(NT):
                    pe.wait_ge(S("delta_ready"), NT * m + i + 1)
                    j = J(f"yd{i}")
                    done(transposes4(take(pe, j), lambda h: o[:, i, hs_(h)]), j)
                for i in range(NT):
                    copied(pe, J(f"cb{i}"))
                    copied(pe, J(f"yd{i}"))
                    for c in range(2):
                        w = weights(pe, ("mix", m, f"w_out{c}"))
                        j = J(f"wo{i}{c}")
                        b = take(pe, j)
                        for k in range(KD):
                            last = mm(b[:, :], uT[:, k, tile(i)], w[:, k, :], start=(k == 0), stop=(k == KD - 1))
                        done(last, j)

            def dense():
                J = lambda name: jobs["ffn", 0, name]
                transpose_x(("ffn", 0), DEPTH + 1)
                for n in range(NFF):
                    pe.wait_ge(S("ff_split"), 2 * n + 2)
                    hi, lo = ff_parts(n)
                    for side, name in enumerate("gu"):
                        j = J(f"{name}{n}")
                        b = take(pe, j)
                        for f in range(2):
                            a, o = slice(FF_PART * side + f * P, FF_PART * side + f * P + P), b[:, f * T:(f + 1) * T]
                            for k in range(KD):
                                mm(o, hi[:, k, a], u_hi[:, k, :], start=(k == 0), stop=False)
                                mm(o, hi[:, k, a], u_lo[:, k, :], start=False, stop=False)
                                last = mm(o, lo[:, k, a], u_hi[:, k, :], start=False, stop=(k == KD - 1))
                        done(last, j)
                out = {(i, c): take(pe, J(f"d{i}{c}")) for i in range(NT) for c in range(2)}
                for n in range(NDOWN):
                    pe.wait_ge(S("ff_split"), 2 * (NFF + n) + 2)
                    hi, lo = ff_parts(NFF + n)
                    pe.wait_ge(S("h_ready"), min(2 * n + 2, NFF))
                    for kk in range(loads[load_at["ffn", 0, f"down{n}"]][1]):
                        k = 4 * n + kk
                        for i in range(NT):
                            for step, (a, w) in enumerate(((h_hi, hi), (h_hi, lo), (h_lo, hi))):
                                for c in range(2):
                                    last = mm(out[i, c][:, :], a[:, k, i * P:(i + 1) * P], w[:, kk, 512 * c:512 * c + 512],
                                              start=(k == 0 and step == 0), stop=(k == KF - 1 and step == 2))
                                    if k == KF - 1 and step == 2:
                                        done(last, J(f"d{i}{c}"))
                    if n < NDOWN - 1:
                        last.then_inc(S("down_used"), 1)

            def gather():
                for half in range(2):
                    for f in range(4):
                        for i in range(NT):
                            last = mm(bank[4 + half][:, f * P:(f + 1) * P], x[:, i, (4 * half + f) * P:(4 * half + f + 1) * P],
                                      pick[:, i, :], start=(i == 0), stop=(i == NT - 1))
                    last.then_inc(S("gathered"), 1)

            def turn_picks():
                for i in range(NT):
                    last = nc.tensor.transpose(bank[6][:, i * P:(i + 1) * P], pickc[:, i, :], C("ident"))
                last.then_inc(S("picks_full"), 1)

            def experts():
                transpose_x(("moe", 0), NORMS - 1)
                pe.wait_ge(S("router_loaded"), 16)
                j = jobs["moe", 0, "logits"]
                b = take(pe, j)
                for i in range(NT):
                    for k in range(KD):
                        last = mm(b[:, NE * i:NE * i + NE], uT[:, k, i * P:(i + 1) * P], router_w[:, k, :],
                                  start=(k == 0), stop=(k == KD - 1))
                done(last, j)
                pe.wait_ge(S("chosen_ready"), 1)
                j = jobs["moe", 0, "places"]
                b = take(pe, j)
                mm(b[:, 0:NE], C("tri_lt"), chosen[:, 0, :], start=True, stop=True)
                for to, w in ((NE, "tri_lt"), (2 * NE, "ones")):
                    mm(b[:, to:to + NE], C("ones"), chosen[:, 0, :], start=True, stop=False)
                    last = mm(b[:, to:to + NE], C(w), chosen[:, 1, :], start=False, stop=True)
                done(last, j)
                copied(pe, jobs["moe", 0, "logits"])
                copied(pe, j)
                pe.wait_ge(S("picked"), 1)
                gather()
                turn_picks()
                pe.wait_ge(S("items_ready"), 1)
                nitems = pe.value_load(items[0:1, 4 * NE:4 * NE + 1], min_val=NE, max_val=2 * NE - 1)
                def turn_hidden(n, q):
                    pe.wait_ge(S("hidden"), n * NQ + (q + 1))
                    if q >= 2:
                        pe.wait_ge(S("he_ready"), n * NQ + (q - 1))
                    for f in range(4):
                        last = nc.tensor.transpose(bank[4 + q % 2][:, f * P:(f + 1) * P], ht[:, q % 2, f * P:(f + 1) * P], C("ident"))
                    last.then_inc(S("hidden_turned"), 1)

                def split_ready(n, p):
                    pe.wait_ge(S("lo_odd" if p % 2 else "lo_even"), n * (NPIECE // 2) + (p // 2 + 1))
                    return piece_hi(p), piece_lo(p)

                with pe.Fori(0, nitems) as n:
                    pe.wait_ge(S("xe_ready"), n * 2 + 2)
                    for q in range(NQ):
                        if q < 2:
                            pe.wait_ge(S("acc_added"), n * 4 + (2 * q + 2))
                        else:
                            pe.wait_ge(S("hidden"), n * NQ + (q - 1))
                        for side in range(2):
                            b = bank[2 * (q % 2) + side]
                            for half in range(2):
                                hi, lo = split_ready(n, 4 * q + 2 * side + half)
                                for kk in range(4):
                                    k = 4 * half + kk
                                    mm(b[:, :], xe_hi[:, k, :], hi[:, kk, :], start=(k == 0), stop=False)
                                    mm(b[:, :], xe_hi[:, k, :], lo[:, kk, :], start=False, stop=False)
                                    last = mm(b[:, :], xe_lo[:, k, :], hi[:, kk, :], start=False, stop=(k == KD - 1))
                                last.then_inc(S("piece_used"), 1)
                        if q:
                            turn_hidden(n, q - 1)
                    pe.wait_ge(S("picks_copied"), n + 1)
                    for r in range(2 * NQ):
                        hi, lo = split_ready(n, NPIECE_UP + r)
                        if r % 2 == 0:
                            pe.wait_ge(S("he_ready"), n * NQ + (r // 2 + 1))
                        for kk in range(2):
                            k = 2 * r + kk
                            for a, w in ((he_hi, hi), (he_hi, lo), (he_lo, hi)):
                                for c in range(2):
                                    last = mm(bank[6 + c][:, :], a[:, k, :], w[:, kk, 512 * c:512 * c + 512],
                                              start=(k == 0 and a is he_hi and w is hi), stop=(k == KE - 1 and a is he_lo))
                        last.then_inc(S("piece_used"), 1)
                        if r == 3:
                            turn_hidden(n, NQ - 1)
                    pe.wait_ge(S("picked"), n + 2)
                    gather()
                    pe.wait_ge(S("ye_copied"), n + 1)
                    for i in range(NT):
                        for c in range(2):
                            mm(bank[2 * i + c][:, :], pickT[:, i, :], ye[:, 512 * c:512 * c + 512], start=True, stop=True)\
                                .then_inc(S("scattered"), 1)
                    turn_picks()

            mixer(0)
            dense()
            mixer(1)
            experts()

        @block.scalar
        def _(act):
            link = chain(act, S("act_chain"))
            go = nc.scalar.activation

            def free(ins, j):
                ins.then_inc(bank_free[j.bank], 1)

            def copy(out, in_, scale=1.0):
                return go(out, in_, ACT.Copy, scale=scale)

            def norm_scale(q):
                for i in range(NT):
                    act.wait_ge(S("var_ready"), NT * q + i + 1)
                    go(lnmv[:, i, 2:3], lnmv[:, i, 1:2], ACT.Sqrt).then_inc(S("std_ready"), 1)

            act.wait_ge(S("pe_T"), 1)
            for v in range(2):
                go(pe_sb[v * HD:(v + 1) * HD, :, :, :], bank[5][0:HD, 0:P], ACT.Copy).then_inc(S("pe_ready"), 1)
            for l in range(DEPTH):
                for q in range(4):
                    copied(act, jobs[l, f"ada{q}"])
                for m in (1, 3):
                    j = jobs[l, f"xT{m}"]
                    b = filled(act, j)
                    for k in (2 * m, 2 * m + 1):
                        last = go(uT[:, k, :], b[:, (k % 2) * T:(k % 2 + 1) * T], ACT.Identity, bias=adac[:, k:k + 1],
                                  scale=adac[:, 8 + k:9 + k])
                    free(last, j)
                j = jobs[l, "iq"]
                free(copy(raw["iq"][:, :, :], filled(act, j)[:, :]), j)
                j = jobs[l, "ikw"]
                b = filled(act, j)
                copy(raw["ik"][0:IDX_DIM, 0, :], b[0:IDX_DIM, 0:T])
                free(copy(iw[:, :, :], b[:, T:T + 16], IDX_HEADS ** -0.5), j)
                j = jobs[l, "dq"]
                free(copy(raw["dq"][:, :, :], filled(act, j)[:, :], HD ** -0.5), j)
                j = jobs[l, "dkv"]
                b = filled(act, j)
                copy(raw["dk"][0:HD, 0, :], b[0:HD, 0:T])
                free(copy(dv[:, :, :], b[:, T:T + NT * HD]), j)
                for i in range(NT):
                    j = jobs[l, f"fv{i}"]
                    free(copy(fv[:, i, :], filled(act, j)[:, 0:FOX_HEADS * HD]), j)
                copied(act, jobs[l, "ff"])
                link(go(ff[:, 1, :], ff[:, 0, :], ACT.Abs))
                link(go(ff[:, 2, :], ff[:, 1, :], ACT.Exp, scale=-1.0))
                go(ff[:, 1, :], ff[:, 2, :], ACT.Ln, bias=1.0).then_inc(S("log1p_ready"), 1)
                for n in range(NIS):
                    j = jobs[l, f"is{n}"]
                    b = filled(act, j)
                    if NIS * l + n >= 2:
                        act.wait_ge(S("isc_steps"), NIS * l + n - 1)
                    w = 2 * (ISCORES[n][0] + 1) * P
                    free(go(relu[:, n % 2, 0:w], b[:, 0:w], ACT.Relu), j)
                for name, dst, tiles in (("fq01", fq, (0, 2)), ("fq2", fq, (2, 3)), ("fk01", fk, (0, 2)), ("fk2", fk, (2, 3))):
                    j = jobs[l, name]
                    free(copy(dst[:, tiles[0]:tiles[1], :], filled(act, j)[:, 0:(tiles[1] - tiles[0]) * T],
                              HD ** -0.5 if dst is fq else 1.0), j)
                j = jobs[l, "nq01"]
                free(copy(raw["nq01"][:, :, :], filled(act, j)[:, :], HD ** -0.5), j)
                j = jobs[l, "nq2"]
                free(copy(raw["nq2"][:, 0, :], filled(act, j)[:, 0:T], HD ** -0.5), j)
                j = jobs[l, "ks"]
                free(copy(raw["ks"][:, 0, :], filled(act, j)[:, 0:T]), j)
                j = jobs[l, "vsw"]
                free(copy(vsw[:, :, :, :], filled(act, j)[:, :]), j)
                j = jobs[l, "kwg"]
                b = filled(act, j)
                copy(raw["kw"][:, 0, :], b[:, 0:T])
                free(go(sgate[:, :, :], b[:, T:T + 36], ACT.Exp, scale=-1.0), j)
                j = jobs[l, "ch"]
                go(ch[:, 0, :, :], filled(act, j)[0:HD, 0:60], ACT.Exp, scale=-1.0).then_inc(S("ch_exp"), 1)
                for c in range(2):
                    for i in range(NT):
                        j = jobs[l, f"gt{c}{i}"]
                        free(go(sg[:, i, 512 * c:512 * c + 512], filled(act, j)[:, :], ACT.Silu), j)
                j = jobs[l, "ckv"]
                b = filled(act, j)
                copy(kcT[0:HD, :, :], b[0:HD, 0:30])
                free(copy(kcT[HD:P, :, :], b[0:HD, 0:30]), j)
                for n, (kind, i, heads, keys) in enumerate(GROUPS):
                    if l + 1 < DEPTH and NEXT_FROM <= n < NEXT_BY:
                        at, of = n - NEXT_FROM, NEXT_BY - NEXT_FROM
                        for step in range(4 * KD * at // of, 4 * KD * (at + 1) // of):
                            k = step % KD
                            w = weights(act, (l + 1, f"ada{step // KD}"))
                            go(w[:, k, :], w[:, k, :], ACT.Copy, scale=vecs[:, k:k + 1]).then_inc(S("ada_scaled"), 1)
                    if n >= 2:
                        act.wait_ge(bank_full[jobs[l, f"T{n - 2}"].bank], jobs[l, f"T{n - 2}"].fill)
                    if kind == "cmp":
                        copied(act, jobs[l, f"S{n}"])
                        go(p_sb[:, n % 2, 0:NHC], cmp_s[:, i, :, :], ACT.Exp).then_inc(S("cmp_p_ready"), 1)
                        continue
                    j = jobs[l, f"S{n}"]
                    act.wait_ge(S("max_ready"), NG * l + n + 1)
                    b = filled(act, j)
                    for m in range(len(heads)):
                        last = go(p_sb[:, n % 2, m * keys:(m + 1) * keys], b[:, m * keys:(m + 1) * keys], ACT.Exp,
                                  bias=stat[:, n % 4, 0, m:m + 1], accum_out=stat[:, n % 4, 1, m:m + 1])
                    free(last, j)
                for i in range(NT):
                    for half in range(2):
                        j = jobs[l, f"yT{i}{half}"]
                        free(copy(uT[:, 4 * half:4 * half + 4, i * P:(i + 1) * P], filled(act, j)[:, :]), j)
                norm_scale(l)

            def copy_xT(key):
                for m in (1, 3):
                    j = jobs[(*key, f"xT{m}")]
                    free(copy(uT[:, 2 * m:2 * m + 2, :], filled(act, j)[:, :]), j)

            def mixer(m):
                q = DEPTH + 2 * m
                J = lambda name: jobs["mix", m, name]
                hs_ = lambda h: slice(h * P, (h + 1) * P)
                tile = lambda i: slice(i * P, (i + 1) * P)
                two = lambda a: a.rearrange("p (f t) -> p f t", f=2)
                copy_xT(("mix", m))
                for half in range(2):
                    j = J(f"c_gate{2 * half}{2 * half + 1}")
                    free(go(sig[:, 2 * half:2 * half + 2, :], two(filled(act, j)[:, :]), ACT.Sigmoid), j)
                copied(act, J("ba"))
                go(sm["ea"][:, 0, 0:DH], decay_in[:, 0, :], ACT.Exp)
                go(sm["eb"][:, :, 0:DH], sm["logit"][:, :, 0:DH], ACT.Exp, scale=-1.0)
                act.wait_ge(S("dt_ready"), m + 1)
                link(go(sm["za"][:, :, 0:DH], sm["z"][:, :, 0:DH], ACT.Abs))
                link(go(sm["ze"][:, :, 0:DH], sm["za"][:, :, 0:DH], ACT.Exp, scale=-1.0))
                go(sm["zl"][:, :, 0:DH], sm["ze"][:, :, 0:DH], ACT.Ln, bias=1.0).then_inc(S("soft_ready"), 1)
                act.wait_ge(S("pads_ready"), m + 1)
                for n, name in enumerate(QKV):
                    for half in range(2):
                        j = J(f"{name}{2 * half}{2 * half + 1}")
                        f = 4 * n + 2 * half
                        free(copy(qkvpad[:, f:f + 2, SHORT - 1:], two(filled(act, j)[:, :])), j)
                for n in range(6):
                    act.wait_ge(S("short_done"), 6 * m + n + 1)
                    part = qkv[:, 2 * n:2 * n + 2, :]
                    go(part, part, ACT.Silu).then_inc(S("qkv_silu"), 1)
                    if n < 4:
                        act.wait_ge(S("qkv_silu"), 6 * m + n + 1)
                        go(sq[:, 2 * n:2 * n + 2, :], part, ACT.Square).then_inc(S("squares"), 1)
                for i in range(NT):
                    j = J(f"z{i}")
                    free(go(sz[:, i, :], filled(act, j)[:, :], ACT.Silu), j)
                copied(act, J("gc"))
                go(sm["coef"][:, 0, 0:DH], sm["rest"][:, 0, 0:DH], ACT.Exp, scale=-1.0)
                go(sm["coef"][:, 1, 0:DH], sm["ncum"][:, 1, 0:DH], ACT.Exp).then_inc(S("coef_ready"), 1)
                for i in range(NT):
                    j = J(f"dm{i}")
                    b = filled(act, j)
                    for h in range(DH):
                        last = go(decay[:, i, hs_(h)], b[:, hs_(h)], ACT.Exp, bias=sm["ncum"][:, i, h:h + 1])
                    free(last, j)
                copied(act, J("ss"))
                go(sm["norm"][:, :, :], sm["ss"][:, :, :], ACT.Sqrt).then_inc(S("norm_ready"), 1)
                for i in range(NT):
                    j = J(f"kn{i}")
                    free(copy(kT[:, :, tile(i)], filled(act, j)[:, :].rearrange("p (h t) -> p h t", h=DH)), j)
                for name, dst in (("LT", LT), ("aT", attnT)):
                    for i in range(NT):
                        j = J(f"{name}{i}")
                        free(copy(dst[:, i, :], filled(act, j)[:, :]), j)
                for s in range(1, LEVELS):
                    if s == 2:
                        for i in range(NT):
                            act.wait_ge(S("cvar_ready"), NT * m + i + 1)
                            go(cmv[:, i, 2:3], cmv[:, i, 1:2], ACT.Sqrt).then_inc(S("cstd_ready"), 1)
                    if s == 4:
                        for i in range(NT):
                            j = J(f"cb{i}")
                            b = filled(act, j)
                            for f in range(4):
                                last = go(uT[:, f, tile(i)], b[:, hs_(f)], ACT.Silu, scale=cvec[:, 1, 52 + f:53 + f],
                                          bias=cvec[:, 1, 56 + f:57 + f])
                            free(last, j)
                    for i in range(NT):
                        j = J(f"Y{i}.{s}")
                        free(copy(Y[:, i, :], filled(act, j)[:, :]), j)
                j = J("vn0")
                act.wait_ge(S("kdec_ready"), m + 1)
                free(copy(vnew[:, 0, :], filled(act, j)[:, :]), j)
                j = J("S1")
                free(copy(S1[:, :], filled(act, j)[:, :]), j)
                j = J("qS")
                b = filled(act, j)
                for h in range(DH):
                    last = copy(oi[:, hs_(h)], b[:, hs_(h)], sm["coef"][:, 1, h:h + 1])
                free(last, j)

                def rms(i):
                    if i == 0:
                        copied(act, J("o0"))
                    else:
                        act.wait_ge(S("o1_ready"), m + 1)
                    for h in range(DH):
                        link(go(osq[:, :], o[:, i, hs_(h)], ACT.Square, accum_out=sm["osum"][:, i, h:h + 1]))
                    go(sm["orms"][:, i, 0:DH], sm["osum"][:, i, 0:DH], ACT.Sqrt, scale=1.0 / DK, bias=eps_col[:, 0:1])\
                        .then_inc(S("orms_ready"), 1)

                j = J("vn1")
                free(copy(vnew[:, 1, :], filled(act, j)[:, :]), j)
                rms(0)
                rms(1)
                for i in range(NT):
                    j = J(f"yd{i}")
                    free(copy(uT[:, 4:8, tile(i)], filled(act, j)[:, :].rearrange("p (f t) -> p f t", f=4)), j)
                norm_scale(q)

            def dense():
                J = lambda name: jobs["ffn", 0, name]

                def split_hi(m):
                    w = weights(act, ("ffn", 0, FF[m]))
                    if m >= 2 and m - 2 < NFF:
                        act.wait_ge(bank_full[J(f"u{m - 2}").bank], J(f"u{m - 2}").fill)
                    elif m >= 2:
                        act.wait_ge(S("down_used"), m - 1 - NFF)
                    hi, _ = ff_parts(m)
                    k = hi.shape[1] // 2
                    for half in range(2):
                        copy(hi[:, half * k:(half + 1) * k, :], w[:, half * k:(half + 1) * k, :]).then_inc(S("ff_hi_ready"), 1)

                j = jobs["mix", 0, "wo11"]
                act.wait_ge(bank_full[j.bank], j.fill)
                split_hi(0)
                split_hi(1)
                for m in (1, 3):
                    j = J(f"xT{m}")
                    copy(u_hi[:, 2 * m:2 * m + 2, :], filled(act, j)[:, :]).then_inc(S("u_hi_ready"), 1)
                for n in range(NFF):
                    j = J(f"g{n}")
                    b = filled(act, j)
                    if n >= 2:
                        act.wait_ge(S("h_ready"), n - 1)
                    free(go(hs[:, n % 2, :], b[:, :], ACT.Silu), j)
                    split_hi(n + 2)
                    copied(act, J(f"u{n}"))
                    copy(h_hi[:, 2 * n:2 * n + 2, :], hs[:, n % 2, :].rearrange("p (f t) -> p f t", f=2)).then_inc(S("h_hi_ready"), 1)
                for m in range(NFF + 2, NFF + NDOWN):
                    split_hi(m)
                norm_scale(DEPTH + 1)

            def experts():
                copy_xT(("moe", 0))
                act.wait_ge(S("gap_ready"), 1)
                go(gates[:, :, 1], gates[:, :, 0], ACT.Exp).then_inc(S("gap_exp"), 1)
                go(long[:, 0, 0:1], gates[:, 0, 0:1], ACT.Silu).then_inc(S("silu_table"), 1)

                act.wait_ge(S("items_ready"), 1)
                nitems = act.value_load(items[0:1, 4 * NE:4 * NE + 1], min_val=NE, max_val=2 * NE - 1)
                act.wait_ge(S("x_ready"), NT * (NORMS - 1))
                with act.Fori(0, nitems) as n:
                    for p in range(NPIECE):
                        act.wait_ge(piece_loaded[p % MOE_RING], n * (16 * NPIECE // MOE_RING) + 16 * (p // MOE_RING + 1))
                        copy(piece_hi(p), piece_raw(p)).then_inc(S("hi_ready"), 1)
                        if p == 2:
                            act.wait_ge(S("picks_full"), n + 1)
                            copy(pickT[:, :, :], bank[6][:, 0:NT * P].rearrange("p (i s) -> p i s", i=NT)).then_inc(S("picks_copied"), 1)
                        q = (p - 4) // 4
                        if p % 4 == 0 and 0 <= q < NQ:
                            act.wait_ge(S("piece_used"), n * NPIECE + (4 * q + 2))
                            go(hse[:, q % 2, :], bank[2 * (q % 2)][:, :], ACT.Silu).then_inc(S("gate_silu"), 1)
                        q = (p - 10) // 4
                        if p % 4 == 2 and 0 <= q < NQ:
                            act.wait_ge(S("hidden_turned"), n * NQ + (q + 1))
                            copy(he_hi[:, 4 * q:4 * q + 4, :], bank[4 + q % 2][:, :].rearrange("p (f s) -> p f s", f=4))\
                                .then_inc(S("he_hi_ready"), 1)
                    act.wait_ge(S("piece_used"), n * NPIECE + NPIECE)
                    copy(ye[:, 0:512], bank[6][:, :])
                    copy(ye[:, 512:D], bank[7][:, :]).then_inc(S("ye_copied"), 1)
                norm_scale(NORMS - 1)

            mixer(0)
            dense()
            mixer(1)
            experts()

        @block.gpsimd
        def _(pool):
            link = chain(pool, S("pool_chain"))
            pool.wait_ge(S("const_loaded"), 16)
            for l in range(DEPTH):
                for n, (name, tiles, r, dim) in enumerate(ROPES):
                    copied(pool, jobs[l, PROJECTED[name]])
                    if NR * l + n >= 2:
                        pool.wait_ge(S("rope_done"), NR * l + n - 1)
                    nc.gpsimd.tensor_tensor(rope_t2[0:r, n % 2, 0:tiles * T].rearrange("p (a t) -> p a t", a=tiles),
                                            raw[name][0:r, :, :], C(f"cos{dim}", r).unsqueeze(1).broadcast_to([r, tiles, T]),
                                            ALU.mult).then_inc(S("cos_half"), 1)
                for step in range(4 * KD if l + 1 < DEPTH else 0):
                    q, k = step // KD, step % KD
                    pool.wait_ge(S("ada_scaled"), step + 1)
                    if k:
                        w = ring[:, load_at[l + 1, f"ada{q}"] % RING, :].rearrange("p (k n) -> p k n", k=KD)
                        ins = nc.gpsimd.tensor_tensor(w[:, 0, :], w[:, 0, :], w[:, k, :], ALU.add)
                        if k < KD - 1:
                            link(ins)
                        else:
                            ins.then_inc(S("ada_next"), 1)

            def mixer(m):
                J = lambda name: jobs["mix", m, name]
                pool.wait_ge(S("x_ready"), NT * (DEPTH + 2 * m))
                nc.gpsimd.memset(eps_col[:, :], RMS_EPS)
                nc.gpsimd.memset(hpad[:, :, 0:CONV_WIN - 1], 0.0)
                nc.gpsimd.memset(qkvpad[:, :, 0:SHORT - 1], 0.0).then_inc(S("pads_ready"), 1)
                f = 3
                copied(pool, J("vw"))
                pool.wait_ge(S("pads_ready"), m + 1)
                copied(pool, J("c_val23"))
                acc = cacc[:, f, :]
                link(nc.gpsimd.tensor_scalar(acc, hpad[:, f, 0:T], cvec[:, 0, f:f + 1], cvec[:, 1, 48 + f:49 + f],
                                             ALU.mult, ALU.add))
                for t in range(1, CONV_WIN):
                    link(nc.gpsimd.tensor_scalar(ptap[:, t % 2, :], hpad[:, f, t:t + T], cvec[:, 0, 4 * t + f:4 * t + f + 1], None,
                                                 ALU.mult))
                    ins = nc.gpsimd.tensor_tensor(acc, acc, ptap[:, t % 2, :], ALU.add)
                    if t < CONV_WIN - 1:
                        link(ins)
                ins.then_inc(S("conv_pool"), 1)
                for s in range(1, LEVELS):
                    a = CONST_AT["levels"][0] + s * P
                    for i in range(NT):
                        copied(pool, J(f"LT{i}"))
                        if s > 1:
                            jy = J(f"Y{i}.{s - 1}")
                            pool.wait_ge(bank_full[jy.bank], jy.fill)
                        nc.gpsimd.tensor_tensor(NsT[:, i, :].rearrange("p (h c) -> p h c", h=DH),
                                                LT[:, i, :].rearrange("p (h c) -> p h c", h=DH),
                                                const2[:, a:a + P].unsqueeze(1).broadcast_to([P, DH, P]),
                                                ALU.mult).then_inc(S("level_ready"), 1)

            pool.wait_ge(S("const2_loaded"), 16)

            def dense():
                for m in range(NFF + NDOWN):
                    w = weights(pool, ("ffn", 0, FF[m]))
                    hi, lo = ff_parts(m)
                    k = hi.shape[1] // 2
                    for half in range(2):
                        part = slice(half * k, (half + 1) * k)
                        pool.wait_ge(S("ff_hi_ready"), 2 * m + half + 1)
                        nc.gpsimd.tensor_tensor(lo[:, part, :], w[:, part, :], hi[:, part, :].bitcast(fp32), ALU.subtract)\
                            .then_inc(S("ff_split"), 1)

            mixer(0)
            dense()
            mixer(1)
            pool.wait_ge(S("items_ready"), 1)
            nitems = pool.value_load(items[0:1, 4 * NE:4 * NE + 1], min_val=NE, max_val=2 * NE - 1)
            with pool.Fori(0, nitems) as n:
                for p in range(0, NPIECE, 2):
                    pool.wait_ge(S("hi_ready"), n * NPIECE + (p + 1))
                    nc.gpsimd.tensor_tensor(piece_lo(p), piece_raw(p), piece_hi(p).bitcast(fp32), ALU.subtract).then_inc(S("lo_even"), 1)

        @block.vector
        def _(dve):
            link = chain(dve, S("dve_chain"))
            tt, ts, stt = nc.vector.tensor_tensor, nc.vector.tensor_scalar, nc.vector.scalar_tensor_tensor

            def free(ins, j):
                ins.then_inc(bank_free[j.bank], 1)

            def rope(l, name):
                n = ROPE_AT[name]
                _, tiles, r, dim = ROPES[n]
                w = tiles * T
                j = jobs[l, f"rot_{name}"]
                b = filled(dve, j)
                free(tt(rope_t1[0:r, n % 2, 0:w].rearrange("p (a t) -> p a t", a=tiles),
                        b[0:r, 0:w].rearrange("p (a t) -> p a t", a=tiles),
                        C(f"sin{dim}", r).unsqueeze(1).broadcast_to([r, tiles, T]), ALU.mult), j)
                copied(dve, j)
                dve.wait_ge(S("cos_half"), NR * l + n + 1)
                t1, t2 = rope_t1[:, n % 2, 0:w], rope_t2[:, n % 2, 0:w]
                outs = [(rot[name][0:r, :, :], 0, r)]
                if name == "ik":
                    outs = [(rot[name][32 * q:32 * q + 32, :, :], 0, r) for q in range(4)]
                elif name == "dk":
                    outs = [(rot[name][HD * q:HD * q + HD, :, :], 0, r) for q in range(2)]
                elif name in ("ks", "kw"):
                    other = ksS if name == "ks" else kwS
                    outs += [(other[HD:P, :], 0, HD), (other[0:HD, :], HD, P)]
                for o, a, z in outs:
                    last = tt(o, t1[a:z], t2[a:z], ALU.add)
                last.then_inc(S("rope_done"), 1)

            def norm(q, i, z):
                link(nc.vector.bn_aggr(lnmv[:, i, 0:2], lnst[:, i, :, :]))
                ts(lnmv[:, i, 1:2], lnmv[:, i, 1:2], LN_EPS, None, ALU.add).then_inc(S("var_ready"), 1)
                dve.wait_ge(S("norm_rows"), 32 * (q + 1))
                link(stt(x[:, i, :], z[:, i, :], lnmv[:, i, 0:1], lng[:, :], ALU.subtract, ALU.mult))
                dve.wait_ge(S("std_ready"), NT * q + i + 1)
                link(nc.vector.reciprocal(lnmv[:, i, 3:4], lnmv[:, i, 2:3]))
                stt(x[:, i, :], x[:, i, :], lnmv[:, i, 3:4], lnb[:, :], ALU.mult, ALU.add).then_inc(S("x_ready"), 1)

            def half_stats(i, c, z):
                link(nc.vector.bn_stats(lnst[:, i, c, :], z[:, i, 512 * c:512 * c + 512]))

            def residual(q, key, name, z):
                for i in range(NT):
                    for c in range(2):
                        j = jobs[(*key, f"{name}{i}{c}")]
                        b = filled(dve, j)
                        cs = slice(512 * c, 512 * c + 512)
                        free(stt(z[:, i, cs], x[:, i, cs], ALPHA, b[:, :], ALU.mult, ALU.add), j)
                        copied(dve, j)
                        half_stats(i, c, z)
                    norm(q, i, z)

            dve.wait_ge(S("const_loaded"), 16)
            dve.wait_ge(S("vecs_T"), 1)
            nc.vector.tensor_copy(vecs[:, 0:40], bank[6][:, 0:40]).then_inc(S("vecs_ready"), 1)
            dve.wait_ge(S("vecs_ready"), 1)
            dve.wait_ge(S("pe_ready"), 2)
            dve.wait_ge(S("small_loaded"), 48)

            def shift_scale(l, q):
                j = jobs[l, f"ada{q}"]
                b = filled(dve, j)
                part = slice(4 * q, 4 * q + 4)
                free(stt(adac[:, part], b[:, 0:4], 0.0 if q < 2 else 1.0, vec_bada(l)[:, part], ALU.add, ALU.add), j)

            def ada_step(l, q, k):
                w = weights(dve, (l, f"ada{q}"))
                if k == 0:
                    link(ts(w[:, 0, :], w[:, 0, :], vec_c(0), None, ALU.mult))
                    return
                ins = stt(w[:, 0, :], w[:, k, :], vec_c(k), w[:, 0, :], ALU.mult, ALU.add)
                if k < KD - 1:
                    link(ins)
                else:
                    ins.then_inc(S("ada_summed"), 1)

            for q in range(4):
                for k in range(KD):
                    ada_step(0, q, k)
            for q in range(4):
                shift_scale(0, q)
            for l in range(DEPTH):
                for q in range(4):
                    copied(dve, jobs[l, f"ada{q}"])
                for m in (0, 2):
                    j = jobs[l, f"xT{m}"]
                    b = filled(dve, j)
                    for k in (2 * m, 2 * m + 1):
                        last = ts(uT[:, k, :], b[:, (k % 2) * T:(k % 2 + 1) * T], adac[:, 8 + k:9 + k], adac[:, k:k + 1],
                                  ALU.mult, ALU.add)
                    free(last, j)
                rope(l, "iq")
                rope(l, "ik")
                j = jobs[l, "ff"]
                b = filled(dve, j)
                free(ts(ff[:, 0, :], b[0:FOX_HEADS, 0:T], b_f[:, l:l + 1], None, ALU.add), j)
                rope(l, "dq")
                rope(l, "dk")
                copied(dve, jobs[l, "ff"])
                dve.wait_ge(S("log1p_ready"), l + 1)
                link(stt(ff[:, 3, :], ff[:, 0, :], 0.0, ff[:, 1, :], ALU.min, ALU.subtract))
                nc.vector.tensor_tensor_scan(ff[:, 4, :], C("ones", FOX_HEADS)[:, 0:1].broadcast_to([FOX_HEADS, T]),
                                             ff[:, 3, :], 0.0, ALU.mult, ALU.subtract).then_inc(S("fox_ready"), 1)
                copied(dve, jobs[l, "ikw"])
                for n, (i, heads) in enumerate(ISCORES):
                    copied(dve, jobs[l, f"is{n}"])
                    keys = (i + 1) * P
                    for m, h in enumerate(heads):
                        r = relu[:, n % 2, m * keys:(m + 1) * keys]
                        acc = isc[:, i, 0:keys]
                        if h == 0:
                            ins = ts(acc, r, iw[:, i, h:h + 1], None, ALU.mult)
                        else:
                            ins = stt(acc, r, iw[:, i, h:h + 1], acc, ALU.mult, ALU.add)
                        if m < len(heads) - 1:
                            link(ins)
                    ins.then_inc(S("isc_steps"), 1)
                    dve.wait_ge(S("isc_steps"), NIS * l + n + 1)
                rope(l, "nq01")
                j = jobs[l, "kcvc"]
                b = filled(dve, j)
                for v in range(2):
                    for g in range(NSA_GROUPS):
                        rows_g = slice(HD * g, HD * g + HD)
                        taps = b[rows_g, v * T:(v + 1) * T].rearrange("p (c r) -> p r c", r=CMP_STRIDE)
                        for par in range(2):
                            for hi in range(2):
                                last = tt(blk[HD * par:HD * par + HD, v, 8 * hi:8 * hi + 8, g, :],
                                          taps[:, par:CMP_STRIDE:2, hi:hi + NCMP],
                                          pe_sb[rows_g, l, v, CMP_STRIDE * hi + par:CMP_STRIDE * (hi + 1):2]
                                          .unsqueeze(2).broadcast_to([HD, 8, NCMP]), ALU.add)
                free(last, j)
                rope(l, "nq2")
                rope(l, "ks")
                j = jobs[l, "ch"]
                b = filled(dve, j)
                dve.wait_ge(S("ch_exp"), l + 1)
                link(ts(ch[:, 1, :, :], ch[:, 0, :, :], 1.0, None, ALU.add))
                link(nc.vector.reciprocal(ch[:, 0, :, :], ch[:, 1, :, :]))
                free(tt(ch[:, 2, :, :], b[0:HD, 0:60].rearrange("p (v c) -> p v c", v=2), ch[:, 0, :, :], ALU.mult), j)
                copied(dve, j)
                nc.vector.tensor_copy(chrep[:, :, :, :], ch[:, 2, 1, :].rearrange("p (g c) -> p g c", g=2)
                                      .unsqueeze(2).broadcast_to([HD, NSA_GROUPS, NSA_HPG, NCMP])).then_inc(S("ch_ready"), 1)
                rope(l, "kw")
                copied(dve, jobs[l, "kwg"])
                link(ts(sgate[:, :, :], sgate[:, :, :], 1.0, None, ALU.add))
                link(nc.vector.reciprocal(sgate[:, :, :], sgate[:, :, :]))
                for i in range(NT):
                    keys = (i + 1) * P
                    link(tt(isc[:, i, keys - P:keys], isc[:, i, keys - P:keys], C("causal"), ALU.add))
                    cur, nxt = isc, isw
                    for k in range(TOPK // 8):
                        link(nc.vector.max(m8[:, i, :], cur[:, i, 0:keys]))
                        link(nc.vector.match_replace(nxt[:, i, 0:keys], m8[:, i, :], cur[:, i, 0:keys], TAKEN))
                        cur, nxt = nxt, cur
                    link(ts(isw[:, i, 0:keys], cur[:, i, 0:keys], TAKEN / 2, NEG, ALU.is_gt, ALU.mult))
                    tt(isw[:, i, keys - P:keys], isw[:, i, keys - P:keys], C("causal"), ALU.add).then_inc(S("sel_ready"), 1)
                j = jobs[l, "ckv"]
                b = filled(dve, j)
                dve.wait_ge(bank_free[j.bank], j.free_before + 1)
                free(tt(vblk[:, :, :], b[0:NHC, HD:2 * HD].unsqueeze(1).broadcast_to([NHC, NSA_HEADS, HD]),
                        C("cmp_block", NHC).rearrange("p (h d) -> p h d", h=NSA_HEADS), ALU.mult), j)
                dve.wait_ge(S("gate_bias"), 16 * (l + 1))

                def gate(c):
                    j = jobs[l, f"gb{c}"]
                    b = filled(dve, j)
                    gc = gate1p[:, 512 * c:512 * c + 512]
                    free(stt(gc, b[:, :], 1.0, gc, ALU.add, ALU.add), j)

                def row_max(n):
                    kind, i, heads, keys = GROUPS[n]
                    j = jobs[l, f"S{n}"]
                    b = filled(dve, j)
                    nh = len(heads)
                    nmax = stat[:, n % 4, 0, 0:nh]
                    view = b[:, 0:nh * keys].rearrange("p (h s) -> p h s", h=nh)
                    ins = nc.vector.tensor_reduce(nmax, view, AX, ALU.max, negate=True)
                    ins.then_inc(S("max_ready"), 1)
                    if kind == "cmp":
                        dve.wait_ge(S("max_ready"), NG * l + n + 1)
                        free(tt(cmp_s[:, i, :, :], view, nmax.unsqueeze(2).broadcast_to([P, nh, keys]), ALU.add), j)

                def copy_pT(n):
                    kind, i, heads, keys = GROUPS[n]
                    j = jobs[l, f"T{n}"]
                    b = filled(dve, j)
                    if kind == "cmp":
                        dve.wait_ge(S("cmp_p_ready"), NT * l + i + 1)
                        link(nc.vector.tensor_reduce(stat[:, n % 4, 1, 0:NSA_HEADS],
                                                     p_sb[:, n % 2, 0:NHC].rearrange("p (h c) -> p h c", h=NSA_HEADS), AX, ALU.add))
                        free(nc.vector.tensor_copy(pT[0:NHC, n % 2, 0:P], b[0:NHC, 0:P]), j)
                    else:
                        w = len(heads) * keys
                        free(nc.vector.tensor_copy(pT[:, n % 2, 0:w], b[:, 0:w]), j)

                def mixed(n):
                    kind, i, heads, keys = GROUPS[n]
                    j = jobs[l, f"O{n}"]
                    nh = len(heads)
                    rinv, cf = stat[:, n % 4, 2, 0:nh], stat[:, n % 4, 3, 0:nh]
                    if kind in ("dsa", "fox"):
                        link(nc.vector.reciprocal(cf, stat[:, n % 4, 1, 0:nh]))
                    else:
                        link(nc.vector.reciprocal(rinv, stat[:, n % 4, 1, 0:nh]))
                        g0 = GATE_OF[kind] * NSA_HEADS + heads[0]
                        g = sgate[:, i, g0:g0 + nh]
                        if kind == "cmp":
                            v0 = CONST_AT["cmp_valid"][0] + i
                            link(stt(cf, rinv, const[:, v0:v0 + 1], g, ALU.mult, ALU.mult))
                        else:
                            link(tt(cf, rinv, g, ALU.mult))
                    b = filled(dve, j)
                    o = b[:, 0:nh * HD].rearrange("p (h d) -> p h d", h=nh)
                    c0 = MIX_COL[kind] + heads[0] * HD
                    dst = mix[:, i, c0:c0 + nh * HD]
                    by = cf.unsqueeze(2).broadcast_to([P, nh, HD])
                    if kind in ("win", "slc"):
                        tmp = otmp[:, 0:nh * HD]
                        free(tt(tmp.rearrange("p (h d) -> p h d", h=nh), o, by, ALU.mult), j)
                        copied(dve, j)
                        link(tt(dst, dst, tmp, ALU.add))
                    else:
                        free(tt(dst.rearrange("p (h d) -> p h d", h=nh), o, by, ALU.mult), j)
                        copied(dve, j)

                for n in range(NG + 2):
                    if n < NG:
                        row_max(n)
                    if 1 <= n <= NG:
                        copy_pT(n - 1)
                    if n >= 2:
                        mixed(n - 2)
                    if n < GATE_BY:
                        for step in range(2 * KD * n // GATE_BY, 2 * KD * (n + 1) // GATE_BY):
                            ada_step(l, 4 + step // KD, step % KD)
                    if n in GATE_AT:
                        gate(GATE_AT[n])
                    if l + 1 < DEPTH and n in NEXT_AT:
                        shift_scale(l + 1, NEXT_AT[n])
                for c in range(2):
                    for i in range(NT):
                        copied(dve, jobs[l, f"gt{c}{i}"])
                for i in range(NT):
                    tt(mix[:, i, :], mix[:, i, :], sg[:, i, :], ALU.mult).then_inc(S("mix_ready"), 1)
                for c in range(2):
                    copied(dve, jobs[l, f"gb{c}"])
                for i in range(NT):
                    for c in range(2):
                        j = jobs[l, f"wo{i}{c}"]
                        b = filled(dve, j)
                        cs = slice(512 * c, 512 * c + 512)
                        free(tt(mix[:, i, cs], b[:, :], gate1p[:, cs], ALU.mult), j)
                        copied(dve, j)
                        link(stt(mix[:, i, cs], x[:, i, cs], ALPHA, mix[:, i, cs], ALU.mult, ALU.add))
                        half_stats(i, c, mix)
                    norm(l, i, mix)

            def copy_xT(key):
                for m in (0, 2):
                    j = jobs[(*key, f"xT{m}")]
                    b = filled(dve, j)
                    free(nc.vector.tensor_copy(uT[:, 2 * m:2 * m + 2, :], b[:, :].rearrange("p (k t) -> p k t", k=2)), j)

            dve.wait_ge(S("const2_loaded"), 16)

            def mixer(m):
                q = DEPTH + 2 * m
                J = lambda name: jobs["mix", m, name]
                hs_ = lambda h: slice(h * P, (h + 1) * P)
                by_head = lambda a: a.rearrange("p (h d) -> p h d", h=DH)
                per_head = lambda a: a.unsqueeze(2).broadcast_to([P, DH, P])
                all_heads = lambda a: a.unsqueeze(1).broadcast_to([P, DH, P])
                copy_xT(("mix", m))
                for half in range(2):
                    copied(dve, J(f"c_gate{2 * half}{2 * half + 1}"))
                    j = J(f"c_val{2 * half}{2 * half + 1}")
                    b = filled(dve, j)
                    free(tt(hpad[:, 2 * half:2 * half + 2, CONV_WIN - 1:], b[:, :].rearrange("p (f t) -> p f t", f=2),
                            sig[:, 2 * half:2 * half + 2, :], ALU.mult), j)
                j = J("vw")
                b = filled(dve, j)
                nc.vector.tensor_copy(cvec[:, 0, 0:CONV_WIN * 4], b[:, 0:CONV_WIN * 4])
                free(nc.vector.tensor_copy(cvec[:, 1, 0:60], b[:, P:P + 60]), j)
                dve.wait_ge(S("mix_small"), 16 * MIX_SMALL * (m + 1))
                j = J("ba")
                b = filled(dve, j)
                free(nc.vector.tensor_copy(sm["logit"][:, :, :], b[:, 0:16].rearrange("p (i n) -> p i n", i=NT)), j)
                copied(dve, j)
                tt(sm["z"][:, :, 0:DH], sm["logit"][:, :, DH:2 * DH], decay_in[:, 1, :].unsqueeze(1).broadcast_to([P, NT, DH]),
                   ALU.add).then_inc(S("dt_ready"), 1)
                copied(dve, J("vw"))
                copied(dve, J("c_val01"))
                copied(dve, J("c_val23"))
                dve.wait_ge(S("pads_ready"), m + 1)
                taken = [0]

                def taps(n):
                    for t in range(taken[0], min(taken[0] + n, CONV_WIN)):
                        for f in range(3):
                            src, w = hpad[:, f, t:t + T], cvec[:, 0, 4 * t + f:4 * t + f + 1]
                            if t == 0:
                                ins = ts(cacc[:, f, :], src, w, cvec[:, 1, 48 + f:49 + f], ALU.mult, ALU.add)
                            else:
                                ins = stt(cacc[:, f, :], src, w, cacc[:, f, :], ALU.mult, ALU.add)
                        if t < CONV_WIN - 1:
                            link(ins)
                        else:
                            ins.then_inc(S("conv_dve"), 1)
                    taken[0] += n

                taps(9)
                for n, name in enumerate(QKV):
                    for half in range(2):
                        copied(dve, J(f"{name}{2 * half}{2 * half + 1}"))
                        for t in range(SHORT):
                            for f in range(4 * n + 2 * half, 4 * n + 2 * half + 2):
                                w = 12 * t + QKV_CHUNK[name] + f - 4 * n
                                src, tap = qkvpad[:, f, t:t + T], cvec[:, 1, w:w + 1]
                                if t == 0:
                                    ins = ts(qkv[:, f, :], src, tap, None, ALU.mult)
                                else:
                                    ins = stt(qkv[:, f, :], src, tap, qkv[:, f, :], ALU.mult, ALU.add)
                            if t < SHORT - 1:
                                link(ins)
                        ins.then_inc(S("short_done"), 1)
                    taps(8)
                dve.wait_ge(S("soft_ready"), m + 1)
                link(ts(sm["eb"][:, :, 0:DH], sm["eb"][:, :, 0:DH], 1.0, None, ALU.add))
                link(nc.vector.reciprocal(sm["beta"][:, :, 0:DH], sm["eb"][:, :, 0:DH]))
                link(stt(sm["soft"][:, :, 0:DH], sm["z"][:, :, 0:DH], 0.0, sm["zl"][:, :, 0:DH], ALU.max, ALU.add))
                tt(sm["g"][:, :, 0:DH], sm["soft"][:, :, 0:DH], sm["ea"][:, 0:1, 0:DH].broadcast_to([P, NT, DH]), ALU.mult)\
                    .then_inc(S("g_ready"), 1)
                j = J("gc")
                b = filled(dve, j)
                link(ts(sm["ncum"][:, :, 0:DH], b[:, 0:8].rearrange("p (i h) -> p i h", i=NT), -1.0, None, ALU.mult))
                free(tt(sm["rest"][:, 0, 0:DH], b[:, 8:12], sm["ncum"][:, 0, 0:DH], ALU.add), j)
                j = J("ss")
                free(ts(sm["ss"][:, :, :], filled(dve, j)[:, 0:16].rearrange("p (i n) -> p i n", i=NT), L2_EPS, None, ALU.add), j)
                dve.wait_ge(S("norm_ready"), m + 1)
                link(nc.vector.reciprocal(sm["rnorm"][:, :, :], sm["norm"][:, :, :]))
                for i in range(NT):
                    j = J(f"kt{i}")
                    b = filled(dve, j)
                    free(tt(by_head(ktok[:, i, :]), by_head(b[:, :]), per_head(sm["rnorm"][:, i, 0:DH]), ALU.mult), j)
                link(ts(sm["rq"][:, :, 0:DH], sm["rnorm"][:, :, DH:], DK ** -0.5, None, ALU.mult))
                for i in range(NT):
                    j = J(f"vt{i}")
                    b = filled(dve, j)
                    free(tt(by_head(vb[:, i, :]), by_head(b[:, :]), per_head(sm["beta"][:, i, 0:DH]), ALU.mult), j)
                dve.wait_ge(S("coef_ready"), m + 1)
                copied(dve, J("kt0"))
                tt(by_head(kdec[:, :]), by_head(ktok[:, 0, :]), per_head(sm["coef"][:, 0, 0:DH]), ALU.mult)\
                    .then_inc(S("kdec_ready"), 1)
                link(stt(sm["nbe"][:, 1, 0:DH], sm["beta"][:, 1, 0:DH], -1.0, sm["coef"][:, 1, 0:DH], ALU.mult, ALU.mult))
                for i in range(NT):
                    copied(dve, J(f"dm{i}"))
                    j = J(f"A{i}")
                    b = filled(dve, j)
                    for h in range(DH):
                        last = stt(Lw[:, i, hs_(h)], b[:, hs_(h)], sm["beta"][:, i, h:h + 1], decay[:, i, hs_(h)], ALU.mult, ALU.mult)
                    free(last, j)
                for i in range(NT):
                    j = J(f"at{i}")
                    b = filled(dve, j)
                    free(tt(attn[:, i, :], b[:, :], decay[:, i, :], ALU.mult), j)
                lv = CONST_AT["levels"][0]
                for i in range(NT):
                    copied(dve, J(f"A{i}"))
                    link(tt(by_head(X[:, i, :]), by_head(Lw[:, i, :]), all_heads(C("level0")), ALU.mult))
                    link(tt(by_head(X[:, i, :]), by_head(X[:, i, :]), all_heads(C("ident")), ALU.add))
                    copied(dve, J(f"LT{i}"))
                    link(tt(by_head(XT[:, i, :]), by_head(LT[:, i, :]), all_heads(const2[:, lv:lv + P]), ALU.mult))
                    tt(by_head(XT[:, i, :]), by_head(XT[:, i, :]), all_heads(C("ident")), ALU.add).then_inc(S("x_first"), 1)
                dve.wait_ge(S("x_first"), NT * (m + 1))
                for s in range(1, LEVELS):
                    if s == 1:
                        for i in range(NT):
                            b = filled(dve, J(f"ct{i}"))
                            link(nc.vector.bn_stats(cstat[:, i, :], b[:, :]))
                            link(nc.vector.bn_aggr(cmv[:, i, 0:2], cstat[:, i, :]))
                            ts(cmv[:, i, 1:2], cmv[:, i, 1:2], LN_EPS, None, ALU.add).then_inc(S("cvar_ready"), 1)
                    if s == 2:
                        for i in range(NT):
                            dve.wait_ge(S("cstd_ready"), NT * m + i + 1)
                            link(nc.vector.reciprocal(cmv[:, i, 3:4], cmv[:, i, 2:3]))
                            j = J(f"ct{i}")
                            b = filled(dve, j)
                            free(ts(cn[:, i, :], b[:, :], cmv[:, i, 0:1], cmv[:, i, 3:4], ALU.subtract, ALU.mult), j)
                    for i in range(NT):
                        for name, dst in (("D", X), ("E", XT)):
                            if s < LEVELS - 1 or name == "E":
                                j = J(f"{name}{i}.{s}")
                                b = filled(dve, j)
                                if s > 1:
                                    copied(dve, J(f"{name}{i}.{s - 1}"))
                                free(tt(dst[:, i, :], dst[:, i, :], b[:, :], ALU.add), j)
                j = J("kS")
                b = filled(dve, j)
                copied(dve, J("vt1"))
                for h in range(DH):
                    last = stt(vb[:, 1, hs_(h)], b[:, hs_(h)], sm["nbe"][:, 1, h:h + 1], vb[:, 1, hs_(h)], ALU.mult, ALU.add)
                free(last, j)
                j = J("o0")
                b = filled(dve, j)
                free(tt(by_head(o[:, 0, :]), by_head(b[:, :]), per_head(sm["rq"][:, 0, 0:DH]), ALU.mult), j)
                j = J("o1")
                b = filled(dve, j)
                copied(dve, J("qS"))
                free(tt(o[:, 1, :], b[:, :], oi[:, :], ALU.add), j)
                copied(dve, j)
                tt(by_head(o[:, 1, :]), by_head(o[:, 1, :]), per_head(sm["rq"][:, 1, 0:DH]), ALU.mult)\
                    .then_inc(S("o1_ready"), 1)
                for i in range(NT):
                    if i == 0:
                        copied(dve, J("o0"))
                    else:
                        dve.wait_ge(S("o1_ready"), m + 1)
                    dve.wait_ge(S("orms_ready"), NT * m + i + 1)
                    link(nc.vector.reciprocal(sm["orstd"][:, i, 0:DH], sm["orms"][:, i, 0:DH]))
                    copied(dve, J(f"z{i}"))
                    link(tt(by_head(o[:, i, :]), by_head(o[:, i, :]), per_head(sm["orstd"][:, i, 0:DH]), ALU.mult))
                    link(tt(by_head(o[:, i, :]), by_head(o[:, i, :]), all_heads(ong[:, :]), ALU.mult))
                    tt(o[:, i, :], o[:, i, :], sz[:, i, :], ALU.mult).then_inc(S("delta_ready"), 1)
                residual(q, ("mix", m), "wo", z2)

            def dense():
                J = lambda name: jobs["ffn", 0, name]
                for m in range(4):
                    j = J(f"xT{m}")
                    b = filled(dve, j)[:, :].rearrange("p (k t) -> p k t", k=2)
                    part = slice(2 * m, 2 * m + 2)
                    if m % 2 == 0:
                        link(nc.vector.tensor_copy(u_hi[:, part, :], b))
                    else:
                        dve.wait_ge(S("u_hi_ready"), m // 2 + 1)
                    free(tt(u_lo[:, part, :], b, u_hi[:, part, :].bitcast(fp32), ALU.subtract), j)
                for n in range(NFF):
                    copied(dve, J(f"g{n}"))
                    j = J(f"u{n}")
                    h = hs[:, n % 2, :]
                    free(tt(h, filled(dve, j)[:, :], h, ALU.mult), j)
                    dve.wait_ge(S("h_hi_ready"), n + 1)
                    part = slice(2 * n, 2 * n + 2)
                    tt(h_lo[:, part, :], h.rearrange("p (f t) -> p f t", f=2), h_hi[:, part, :].bitcast(fp32), ALU.subtract)\
                        .then_inc(S("h_ready"), 1)
                residual(DEPTH + 1, ("ffn", 0), "d", z3)

            def experts():
                copy_xT(("moe", 0))
                j = jobs["moe", 0, "logits"]
                b = filled(dve, j)
                free(nc.vector.tensor_copy(logits[:, :, :], b[:, 0:NT * NE].rearrange("p (i e) -> p i e", i=NT)), j)
                copied(dve, j)
                for i in range(NT):
                    link(nc.vector.max(out=best[:, i, :], in_=logits[:, i, :]))
                    link(nc.vector.max_index(out=best_at[:, i, :], in_max=best[:, i, :], in_values=logits[:, i, :]))
                link(nc.vector.tensor_copy(best_f[:, :, :], best_at[:, :, :]))
                for i in range(NT):
                    for n in range(2):
                        last = ts(hot[:, n, i, :], C("iota")[:, 0:NE], best_f[:, i, n:n + 1], None, ALU.is_equal)
                link(last)
                tt(chosen[:, :, :], hot[:, 0, :, :], hot[:, 1, :, :], ALU.add).then_inc(S("chosen_ready"), 1)
                tt(gates[:, :, 0], best[:, :, 1], best[:, :, 0], ALU.subtract).then_inc(S("gap_ready"), 1)
                dve.wait_ge(S("gap_exp"), 1)
                link(ts(gates[:, :, 3], gates[:, :, 1], 1.0, None, ALU.add))
                link(nc.vector.reciprocal(gates[:, :, 2], gates[:, :, 3]))
                link(tt(gates[:, :, 3], gates[:, :, 1], gates[:, :, 2], ALU.mult))
                for i in range(NT):
                    link(ts(comb[:, i, 0:NE], hot[:, 0, i, :], gates[:, i, 2:3], None, ALU.mult))
                    link(stt(comb[:, i, 0:NE], hot[:, 1, i, :], gates[:, i, 3:4], comb[:, i, 0:NE], ALU.mult, ALU.add))
                link(nc.vector.tensor_copy(comb[:, :, NE:], comb[:, :, 0:NE]))
                dve.wait_ge(S("chosen_ready"), 1)
                link(ts(places[:, :, 0:NE], chosen[:, :, :], FAR, -FAR, ALU.mult, ALU.add))
                j = jobs["moe", 0, "places"]
                b = filled(dve, j)
                link(tt(places[:, :, 0:NE], places[:, :, 0:NE], b[:, 0:NT * NE].rearrange("p (i e) -> p i e", i=NT), ALU.add))
                link(ts(places[:, :, NE:], places[:, :, 0:NE], -float(P), None, ALU.add))
                dve.wait_ge(S("silu_table"), 1)
                free(nc.vector.tensor_copy(long[:, 0, :], b[:, NT * NE:NT * NE + NE]), j)
                copied(dve, j)
                link(ts(long[:, 1, :], long[:, 0, :], float(P), None, ALU.is_gt))
                link(tt(long[:, 2, :], long[:, 1, :], C("iota")[:, NE:2 * NE], ALU.mult))
                link(nc.vector.max(out=long[:, 3, :], in_=long[:, 2, :]))
                link(nc.vector.tensor_reduce(out=item_f[:, 4 * NE:4 * NE + 1], in_=long[:, 1, :], axis=AX, op=ALU.add))
                link(ts(item_f[:, 4 * NE:4 * NE + 1], item_f[:, 4 * NE:4 * NE + 1], float(NE), None, ALU.add))
                nc.vector.tensor_copy(item_f[:, 0:NE], C("iota")[:, 0:NE])
                nc.vector.tensor_copy(item_f[:, NE:2 * NE], long[:, 3, :])
                nc.vector.tensor_copy(item_f[:, 2 * NE:3 * NE], C("iota")[:, 0:NE])
                link(ts(item_f[:, 3 * NE:4 * NE], long[:, 3, :], float(NE), 0.0, ALU.subtract, ALU.max))
                nc.vector.tensor_copy(items[:, :], item_f[:, :]).then_inc(S("items_ready"), 1)
                dve.wait_ge(S("items_ready"), 1)

                def pick_tokens(n):
                    c = dve.value_load(items[0:1, bass.ds(n, 1)], min_val=0, max_val=2 * NE - 1)
                    for i in range(NT):
                        ts(pick[:, i, :], C("iota"), places[:, i, bass.ds(c, 1)], None, ALU.is_equal)
                        last = ts(pickc[:, i, :], C("iota"), places[:, i, bass.ds(c, 1)], comb[:, i, bass.ds(c, 1)],
                                  ALU.is_equal, ALU.mult)
                    last.then_inc(S("picked"), 1)

                def evacuate(count):
                    for half in range(2):
                        dve.wait_ge(S("gathered"), count * 2 + (half + 1))
                        b = bank[4 + half][:, :].rearrange("p (f s) -> p f s", f=4)
                        hi, lo = xe_hi[:, 4 * half:4 * half + 4, :], xe_lo[:, 4 * half:4 * half + 4, :]
                        nc.vector.tensor_copy(hi, b).then_inc(S("xe_hi_ready"), 1)
                        dve.wait_ge(S("xe_hi_ready"), count * 2 + (half + 1))
                        tt(lo, b, hi.bitcast(fp32), ALU.subtract).then_inc(S("xe_ready"), 1)

                pick_tokens(0)
                for i in range(NT):
                    for c in range(2):
                        cs = slice(512 * c, 512 * c + 512)
                        ts(total[:, i, cs], x[:, i, cs], ALPHA, None, ALU.mult).then_inc(S("acc_added"), 1)
                evacuate(0)
                nitems = dve.value_load(items[0:1, 4 * NE:4 * NE + 1], min_val=NE, max_val=2 * NE - 1)
                with dve.Fori(0, nitems) as n:
                    for p in range(1, NPIECE, 2):
                        dve.wait_ge(S("hi_ready"), n * NPIECE + (p + 1))
                        tt(piece_lo(p), piece_raw(p), piece_hi(p).bitcast(fp32), ALU.subtract).then_inc(S("lo_odd"), 1)
                        if p == 3:
                            dve.wait_ge(S("picks_full"), n + 1)
                            pick_tokens(n + 1)
                        q = (p - 5) // 4
                        if p % 4 == 1 and 0 <= q < NQ:
                            dve.wait_ge(S("gate_silu"), n * NQ + (q + 1))
                            dve.wait_ge(S("piece_used"), n * NPIECE + (4 * q + 4))
                            tt(ht[:, q % 2, :], bank[2 * (q % 2) + 1][:, :], hse[:, q % 2, :], ALU.mult).then_inc(S("hidden"), 1)
                        q = (p - 11) // 4
                        if p % 4 == 3 and 0 <= q < NQ:
                            dve.wait_ge(S("he_hi_ready"), n * NQ + (q + 1))
                            part = slice(4 * q, 4 * q + 4)
                            tt(he_lo[:, part, :], bank[4 + q % 2][:, :].rearrange("p (f s) -> p f s", f=4),
                               he_hi[:, part, :].bitcast(fp32), ALU.subtract).then_inc(S("he_ready"), 1)
                    evacuate(n + 1)
                    for i in range(NT):
                        for c in range(2):
                            b, cs = 2 * i + c, slice(512 * c, 512 * c + 512)
                            dve.wait_ge(S("scattered"), n * 4 + (b + 1))
                            dve.wait_ge(S("acc_added"), n * 4 + (b + 1))
                            tt(total[:, i, cs], total[:, i, cs], bank[b][:, :], ALU.add).then_inc(S("acc_added"), 1)
                dve.wait_ge(S("acc_added"), nitems * 4 + 4)
                for i in range(NT):
                    for c in range(2):
                        half_stats(i, c, total)
                    norm(NORMS - 1, i, total)

            mixer(0)
            dense()
            mixer(1)
            experts()


def kernel(**inputs):
    import numpy as _np
    import concourse.bacc as _bacc
    from concourse import mybir as _mybir
    from concourse.bass_utils import run_bass_kernel_spmd as _run

    nc = _bacc.Bacc("TRN2", target_bir_lowering=False, num_devices=1)
    arrays, A = {}, {}
    for name in _INS:
        a = _np.ascontiguousarray(inputs[name])
        arrays[f"in_{name}_dram"] = a
        A[name] = nc.dram_tensor(f"in_{name}_dram", a.shape, _mybir.dt.from_np(a.dtype), kind="ExternalInput").ap()
    for name, a in (("const", _CONST), ("const2", _CONST2)):
        arrays[f"in_{name}_dram"] = a
        A[name] = nc.dram_tensor(f"in_{name}_dram", a.shape, _mybir.dt.float32, kind="ExternalInput").ap()
    out = nc.dram_tensor("out_0_dram", (1, T, D), _mybir.dt.float32, kind="ExternalOutput").ap()
    build(nc, A, out)
    r = _run(nc, [arrays], core_ids=[0])
    return r.results[0]["out_0_dram"]

_INS = ["x", "c", "w_ada", "b_ada", "w_in", "b_f", "cmp_pe", "cmp_w1", "cmp_w2", "w_out", "ln_g", "ln_b",
        "w_in_2", "conv_dw_w_2", "conv_dw_b_2", "conv_ln_g_2", "conv_ln_b_2", "short_conv_w_2", "a_log_2", "dt_bias_2",
        "out_norm_g_2", "w_out_2", "ln_mix_g_2", "ln_mix_b_2", "ffn_w_gate_2", "ffn_w_up_2", "ffn_w_down_2",
        "router_w_2", "moe_w_gate_2", "moe_w_up_2", "moe_w_down_2", "ln_ffn_g_2", "ln_ffn_b_2"]
```
